# Optimizing a Trainium2 kernel written in Bass

```python
import math
import jax
import jax.numpy as jnp
from jax import lax
import numpy as np

D_MODEL = 1024
BATCH = 1
SEQ = 1024
DEPTH = 2

GRID_W = 64
CTX_LEN = 256
D_MIX = D_MODEL
GROUP_W = D_MIX // 4
A_HEADS = 4
A_DV = GROUP_W // A_HEADS
A_DK = A_DV // 2
B_HEADS = 4
B_DH = GROUP_W // B_HEADS
CONV_W = 3
C_HEADS = 4
C_DV = GROUP_W // C_HEADS
C_DK = C_DV // 2
GLA_RANK = 16
GLA_TAU = 16.0
D_HEADS = 4
D_KV = 2
D_GROUP = D_HEADS // D_KV
D_HD = GROUP_W // D_HEADS
WINDOW = 128
BLOCK = 128
CHUNK = 64
ROPE_THETA = 10000.0
EPS = 1e-6
F32 = jnp.float32

SPLIT_SIZES = (
    A_HEADS * 2 * A_DK, A_HEADS * 2 * A_DK, A_HEADS * A_DV,
    B_HEADS * B_DH, B_HEADS * B_DH, B_HEADS * B_DH, 4 * B_HEADS, B_HEADS * B_DH,
    C_HEADS * C_DK, C_HEADS * C_DK, C_HEADS * C_DV, 2 * GLA_RANK,
    D_HEADS * D_HD, D_KV * D_HD, D_KV * D_HD,
    D_MIX,
)
N_IN = sum(SPLIT_SIZES)

kernel_name = 'hybrid_parallel_heads_diffusion_block'

def rmsnorm(x, g):
    xf = x.astype(F32)
    y = xf * lax.rsqrt(jnp.mean(xf * xf, axis=-1, keepdims=True) + EPS)
    return (y * g.astype(F32)).astype(x.dtype)

def split_cols(p):
    outs, start = [], 0
    for size in SPLIT_SIZES:
        outs.append(p[..., start:start + size])
        start += size
    return outs

def _rotate(xh, ang):
    x1, x2 = jnp.split(xh, 2, axis=-1)
    cos, sin = jnp.cos(ang), jnp.sin(ang)
    return jnp.concatenate([x1 * cos - x2 * sin, x1 * sin + x2 * cos], axis=-1)

def axial_rope(x, rows, cols):
    hd = x.shape[-1]
    nq = hd // 4
    inv = ROPE_THETA ** (-jnp.arange(nq, dtype=F32) / nq)
    shp = (x.shape[1],) + (1,) * (x.ndim - 3) + (nq,)
    ang_r = (rows.astype(F32)[:, None] * inv).reshape(shp)
    ang_c = (cols.astype(F32)[:, None] * inv).reshape(shp)
    xf = x.astype(F32)
    out = jnp.concatenate([_rotate(xf[..., :hd // 2], ang_r), _rotate(xf[..., hd // 2:], ang_c)], axis=-1)
    return out.astype(x.dtype)

def short_conv(x, w, b):
    ch = x.shape[-1]
    y = lax.conv_general_dilated(x, w.reshape(CONV_W, 1, ch).astype(x.dtype), (1,),
                                 [((CONV_W - 1) // 2, CONV_W // 2)],
                                 dimension_numbers=('NWC', 'WIO', 'NWC'), feature_group_count=ch)
    return y + b.astype(x.dtype)

def _to_chunks(a):
    bsz, nh, t = a.shape[:3]
    a = a.reshape((bsz, nh, t // CHUNK, CHUNK) + a.shape[3:])
    return jnp.moveaxis(a, 2, 0)

def chunked_scan(step, state, seqs):
    t = seqs[0].shape[2]
    state, hs = lax.scan(step, state, tuple(_to_chunks(a) for a in seqs))
    hs = jnp.moveaxis(hs, 0, 2)
    return hs.reshape(hs.shape[:2] + (t,) + hs.shape[4:]), state

def bidir(step, init, ctx_f, lat_f, ctx_b, lat_b):
    flip = lambda seqs: tuple(jnp.flip(a, 2) for a in seqs)
    hc_f, st_f = chunked_scan(step, init, ctx_f)
    hl_f, _ = chunked_scan(step, st_f, lat_f)
    hc_b, st_b = chunked_scan(step, init, flip(ctx_b))
    hl_b, _ = chunked_scan(step, st_b, flip(lat_b))
    return hl_f + jnp.flip(hl_b, 2), hc_f + jnp.flip(hc_b, 2)

def _mlstm_step(state, xs):
    cmat, nvec, m = state
    q, k, v, li, lf = xs
    ln = q.shape[2]
    tril = jnp.tril(jnp.ones((ln, ln), dtype=bool))
    b = jnp.cumsum(lf, axis=-1)
    d = jnp.where(tril, b[..., :, None] - b[..., None, :] + li[..., None, :], -jnp.inf)
    m_inter = b + m[..., None]
    m_t = jnp.maximum(m_inter, jnp.max(d, axis=-1))
    w = jnp.exp(d - m_t[..., None])
    g_inter = jnp.exp(m_inter - m_t)
    s = jnp.einsum('bhtd,bhsd->bhts', q, k) * w
    num = jnp.einsum('bhts,bhsv->bhtv', s, v) + g_inter[..., None] * jnp.einsum('bhvd,bhtd->bhtv', cmat, q)
    nq = jnp.sum(s, axis=-1) + g_inter * jnp.einsum('bhd,bhtd->bht', nvec, q)
    h = num / jnp.maximum(jnp.abs(nq), jnp.exp(-m_t))[..., None]
    b_end = b[..., -1]
    g = b_end[..., None] - b + li
    m_new = jnp.maximum(b_end + m, jnp.max(g, axis=-1))
    w_end = jnp.exp(g - m_new[..., None])
    decay = jnp.exp(b_end + m - m_new)
    cmat = decay[..., None, None] * cmat + jnp.einsum('bhs,bhsv,bhsd->bhvd', w_end, v, k)
    nvec = decay[..., None] * nvec + jnp.einsum('bhs,bhsd->bhd', w_end, k)
    return (cmat, nvec, m_new), h

def _gla_step(smat, xs):
    q, k, v, la = xs
    ln = q.shape[2]
    tril = jnp.tril(jnp.ones((ln, ln), dtype=bool))
    bc = jnp.cumsum(la, axis=2)
    inter = jnp.einsum('bhtd,bhdv->bhtv', q * jnp.exp(bc), smat)
    rel = jnp.where(tril[:, :, None], bc[:, :, :, None, :] - bc[:, :, None, :, :], -jnp.inf)
    a = jnp.einsum('bhtd,bhtsd,bhsd->bhts', q, jnp.exp(rel), k)
    o = inter + jnp.einsum('bhts,bhsv->bhtv', a, v)
    b_end = bc[:, :, -1]
    smat = jnp.exp(b_end)[..., None] * smat + jnp.einsum('bhsd,bhsv->bhdv', k * jnp.exp(b_end[:, :, None] - bc), v)
    return smat, o

def diff_attention(pl, pc, qn_g, kn_g, lam_p, subln_g, lam_init, rows, cols, with_ctx):
    (ql, kl, vl), (qc, kc, vc) = pl, pc
    bsz, t = ql.shape[:2]
    lc = qc.shape[1]

    def heads(q, k, v, n):
        q = rmsnorm(q.reshape(bsz, n, A_HEADS, 2, A_DK), qn_g)
        k = rmsnorm(k.reshape(bsz, n, A_HEADS, 2, A_DK), kn_g)
        return q, k, v.reshape(bsz, n, A_HEADS, A_DV)

    ql, kl, vl = heads(ql, kl, vl, t)
    ql = axial_rope(ql, rows, cols)
    kl = axial_rope(kl, rows, cols)
    qc, kc, vc = heads(qc, kc, vc, lc)
    lp = lam_p.astype(F32)
    lam = jnp.exp(jnp.sum(lp[0] * lp[1])) - jnp.exp(jnp.sum(lp[2] * lp[3])) + lam_init
    scale = A_DK ** -0.5

    def attend(q, k, v):
        s = jnp.einsum('bqhcd,bkhcd->bhcqk', q, k).astype(F32) * scale
        p = jax.nn.softmax(s, axis=-1)
        a = p[:, :, 0] - lam * p[:, :, 1]
        return jnp.einsum('bhqk,bkhd->bqhd', a, v.astype(F32))

    k_all = jnp.concatenate([kc, kl], axis=1)
    v_all = jnp.concatenate([vc, vl], axis=1)
    nb = t // BLOCK
    qb = jnp.moveaxis(ql.reshape(bsz, nb, BLOCK, A_HEADS, 2, A_DK), 1, 0)
    ol = lax.map(lambda qblk: attend(qblk, k_all, v_all), qb)
    ol = jnp.moveaxis(ol, 0, 1).reshape(bsz, t, A_HEADS, A_DV)

    def finish(o):
        return (rmsnorm(o, subln_g) * (1.0 - lam_init)).reshape(o.shape[0], o.shape[1], A_HEADS * A_DV)

    out_c = finish(attend(qc, kc, vc)) if with_ctx else None
    return finish(ol), out_c

def mlstm_mixer(pl, pc, conv_w, conv_b, gate_b, outn_g, with_ctx):
    def prep(q, k, v, gt, o):
        bsz, t = q.shape[:2]
        qk = jax.nn.silu(short_conv(jnp.concatenate([q, k], axis=-1), conv_w, conv_b))
        q, k = jnp.split(qk, 2, axis=-1)
        th = lambda a: a.reshape(bsz, t, B_HEADS, B_DH).transpose(0, 2, 1, 3).astype(F32)
        pre = gt.reshape(bsz, t, 4, B_HEADS).astype(F32) + gate_b.astype(F32)
        pre = pre.transpose(2, 0, 3, 1)
        base = (th(q), th(k) * B_DH ** -0.5, th(v))
        fwd = base + (pre[0], jax.nn.log_sigmoid(pre[1]))
        bwd = base + (pre[2], jax.nn.log_sigmoid(pre[3]))
        return fwd, bwd, o

    lat_f, lat_b, o_l = prep(*pl)
    ctx_f, ctx_b, o_c = prep(*pc)
    bsz = o_l.shape[0]
    init = (jnp.zeros((bsz, B_HEADS, B_DH, B_DH), F32), jnp.zeros((bsz, B_HEADS, B_DH), F32),
            jnp.zeros((bsz, B_HEADS), F32))
    hl, hc = bidir(_mlstm_step, init, ctx_f, lat_f, ctx_b, lat_b)

    def finish(h, o):
        h = rmsnorm(jnp.swapaxes(h, 1, 2), outn_g)
        return h.reshape(h.shape[0], h.shape[1], B_HEADS * B_DH) * jax.nn.sigmoid(o.astype(F32))

    out_c = finish(hc, o_c) if with_ctx else None
    return finish(hl, o_l), out_c

def gla_mixer(pl, pc, wg, bg, outn_g, with_ctx):
    def prep(q, k, v, lr):
        bsz, t = q.shape[:2]
        th = lambda a, dd: a.reshape(bsz, t, C_HEADS, dd).transpose(0, 2, 1, 3).astype(F32)
        lr = lr.reshape(bsz, t, 2, GLA_RANK).astype(F32)
        la = jax.nn.log_sigmoid(jnp.einsum('btzr,zrk->btzk', lr, wg.astype(F32)) + bg.astype(F32)) / GLA_TAU
        base = (th(q, C_DK) * C_DK ** -0.5, th(k, C_DK), th(v, C_DV))
        return base + (th(la[:, :, 0], C_DK),), base + (th(la[:, :, 1], C_DK),)

    lat_f, lat_b = prep(*pl)
    ctx_f, ctx_b = prep(*pc)
    bsz = pl[0].shape[0]
    init = jnp.zeros((bsz, C_HEADS, C_DK, C_DV), F32)
    hl, hc = bidir(_gla_step, init, ctx_f, lat_f, ctx_b, lat_b)

    def finish(h):
        h = rmsnorm(jnp.swapaxes(h, 1, 2), outn_g)
        return h.reshape(h.shape[0], h.shape[1], C_HEADS * C_DV)

    out_c = finish(hc) if with_ctx else None
    return finish(hl), out_c

def window_gqa(pl, pc, qn_g, kn_g, sink, rows, cols, with_ctx):
    (ql, kl, vl), (qc, kc, vc) = pl, pc
    bsz, t = ql.shape[:2]
    lc = qc.shape[1]
    ql = axial_rope(rmsnorm(ql.reshape(bsz, t, D_KV, D_GROUP, D_HD), qn_g), rows, cols)
    kl = axial_rope(rmsnorm(kl.reshape(bsz, t, D_KV, D_HD), kn_g), rows, cols)
    vl = vl.reshape(bsz, t, D_KV, D_HD)
    qc = rmsnorm(qc.reshape(bsz, lc, D_KV, D_GROUP, D_HD), qn_g)
    kc = rmsnorm(kc.reshape(bsz, lc, D_KV, D_HD), kn_g)
    vc = vc.reshape(bsz, lc, D_KV, D_HD)
    scale = D_HD ** -0.5
    sk = sink.astype(F32).reshape(D_KV, D_GROUP, 1, 1)
    nb = t // BLOCK
    pad = ((0, 0), (WINDOW, WINDOW), (0, 0), (0, 0))
    kb = jnp.pad(kl, pad).reshape(bsz, nb + 2, BLOCK, D_KV, D_HD)
    vb = jnp.pad(vl, pad).reshape(bsz, nb + 2, BLOCK, D_KV, D_HD)
    kw = jnp.concatenate([kb[:, :-2], kb[:, 1:-1], kb[:, 2:]], axis=2)
    vw = jnp.concatenate([vb[:, :-2], vb[:, 1:-1], vb[:, 2:]], axis=2)
    qb = ql.reshape(bsz, nb, BLOCK, D_KV, D_GROUP, D_HD)
    s_loc = jnp.einsum('bnqhgd,bnkhd->bnhgqk', qb, kw).astype(F32) * scale
    a_idx = jnp.arange(BLOCK)[:, None]
    j_idx = jnp.arange(3 * BLOCK)[None, :]
    kpos = jnp.arange(nb)[:, None, None] * BLOCK - WINDOW + j_idx[None]
    band = (j_idx - a_idx >= 0) & (j_idx - a_idx <= 2 * WINDOW)
    valid = band[None] & (kpos >= 0) & (kpos < t)
    s_loc = jnp.where(valid[None, :, None, None], s_loc, -jnp.inf)
    s_ctx = jnp.einsum('bnqhgd,bchd->bnhgqc', qb, kc).astype(F32) * scale
    logits = jnp.concatenate([s_loc, s_ctx, jnp.broadcast_to(sk, s_loc.shape[:-1] + (1,))], axis=-1)
    p = jax.nn.softmax(logits, axis=-1)
    o = (jnp.einsum('bnhgqk,bnkhd->bnqhgd', p[..., :3 * BLOCK], vw.astype(F32))
         + jnp.einsum('bnhgqc,bchd->bnqhgd', p[..., 3 * BLOCK:3 * BLOCK + lc], vc.astype(F32)))
    out_l = o.reshape(bsz, t, D_HEADS * D_HD)
    out_c = None
    if with_ctx:
        s = jnp.einsum('bqhgd,bkhd->bhgqk', qc, kc).astype(F32) * scale
        lg = jnp.concatenate([s, jnp.broadcast_to(sk, s.shape[:-1] + (1,))], axis=-1)
        pc_ = jax.nn.softmax(lg, axis=-1)
        out_c = jnp.einsum('bhgqk,bkhd->bqhgd', pc_[..., :lc], vc.astype(F32)).reshape(bsz, lc, D_HEADS * D_HD)
    return out_l, out_c

def setup_inputs(seed: int = 0) -> dict:
    key = jax.random.key(seed)
    ks = jax.random.split(key, 24)
    nrm = lambda k, shape, s: s * jax.random.normal(k, shape, F32)
    gain = lambda k, shape: 1.0 + 0.1 * jax.random.normal(k, shape, F32)
    f_bias = jnp.linspace(3.0, 6.0, B_HEADS, dtype=F32)
    zb = jnp.zeros((B_HEADS,), F32)
    gate_base = jnp.stack([zb, f_bias, zb, f_bias])
    return {
        'x': nrm(ks[0], (BATCH, SEQ, D_MODEL), 1.0),
        'c': nrm(ks[1], (BATCH, D_MODEL), 1.0),
        'ctx': nrm(ks[2], (BATCH, CTX_LEN, D_MODEL), 1.0),
        'c_ctx': nrm(ks[3], (D_MODEL,), 1.0),
        'w_mod': nrm(ks[4], (DEPTH, D_MODEL, 3 * D_MODEL), 0.5 * D_MODEL ** -0.5),
        'b_mod': nrm(ks[5], (DEPTH, 3 * D_MODEL), 0.02),
        'norm_g': gain(ks[6], (DEPTH, D_MODEL)),
        'w_in': nrm(ks[7], (DEPTH, D_MODEL, N_IN), D_MODEL ** -0.5),
        'w_out': nrm(ks[8], (DEPTH, D_MIX, D_MODEL), D_MIX ** -0.5),
        'a_qn': gain(ks[9], (DEPTH, A_DK)),
        'a_kn': gain(ks[10], (DEPTH, A_DK)),
        'a_lam': nrm(ks[11], (DEPTH, 4, A_DK), 0.1),
        'a_subln': gain(ks[12], (DEPTH, A_DV)),
        'b_conv_w': nrm(ks[13], (DEPTH, CONV_W, 2 * B_HEADS * B_DH), CONV_W ** -0.5),
        'b_conv_b': nrm(ks[14], (DEPTH, 2 * B_HEADS * B_DH), 0.02),
        'b_gate_b': gate_base + nrm(ks[15], (DEPTH, 4, B_HEADS), 0.1),
        'b_outn': gain(ks[16], (DEPTH, B_DH)),
        'c_wg': nrm(ks[17], (DEPTH, 2, GLA_RANK, C_HEADS * C_DK), GLA_RANK ** -0.5),
        'c_bg': nrm(ks[18], (DEPTH, 2, C_HEADS * C_DK), 0.1),
        'c_outn': gain(ks[19], (DEPTH, C_DV)),
        'd_qn': gain(ks[20], (DEPTH, D_HD)),
        'd_kn': gain(ks[21], (DEPTH, D_HD)),
        'd_sink': nrm(ks[22], (DEPTH, D_HEADS), 0.5),
    }

def reference(x, c, ctx, c_ctx, w_mod, b_mod, norm_g, w_in, w_out, a_qn, a_kn, a_lam, a_subln,
              b_conv_w, b_conv_b, b_gate_b, b_outn, c_wg, c_bg, c_outn, d_qn, d_kn, d_sink):
    t = x.shape[1]
    rows_n = t // GRID_W
    rows = jnp.repeat(jnp.arange(rows_n, dtype=jnp.int32), GRID_W)
    cols = jnp.tile(jnp.arange(GRID_W, dtype=jnp.int32), rows_n)
    s_lat = jax.nn.silu(c)
    s_ctx = jax.nn.silu(c_ctx)
    for l in range(DEPTH):
        with_ctx = l < DEPTH - 1
        sh, sc, gt = jnp.split(s_lat @ w_mod[l] + b_mod[l], 3, axis=-1)
        sh_c, sc_c, gt_c = jnp.split(s_ctx @ w_mod[l] + b_mod[l], 3, axis=-1)
        hx = rmsnorm(x, norm_g[l]) * (1.0 + sc[:, None]) + sh[:, None]
        hc = rmsnorm(ctx, norm_g[l]) * (1.0 + sc_c) + sh_c
        px = split_cols(hx @ w_in[l])
        pcx = split_cols(hc @ w_in[l])
        lam_init = 0.8 - 0.6 * math.exp(-0.3 * l)
        a_l, a_c = diff_attention(px[0:3], pcx[0:3], a_qn[l], a_kn[l], a_lam[l], a_subln[l], lam_init,
                                  rows, cols, with_ctx)
        b_l, b_c = mlstm_mixer(px[3:8], pcx[3:8], b_conv_w[l], b_conv_b[l], b_gate_b[l], b_outn[l], with_ctx)
        c_l, c_c = gla_mixer(px[8:12], pcx[8:12], c_wg[l], c_bg[l], c_outn[l], with_ctx)
        d_l, d_c = window_gqa(px[12:15], pcx[12:15], d_qn[l], d_kn[l], d_sink[l], rows, cols, with_ctx)
        y = jnp.concatenate([a_l, b_l, c_l, d_l], axis=-1).astype(x.dtype) * jax.nn.silu(px[15])
        x = x + gt[:, None] * (y @ w_out[l])
        if with_ctx:
            yc = jnp.concatenate([a_c, b_c, c_c, d_c], axis=-1).astype(ctx.dtype) * jax.nn.silu(pcx[15])
            ctx = ctx + gt_c * (yc @ w_out[l])
    return x


_drawn_inputs = setup_inputs


def setup_inputs(seed=0):
    import zlib

    import numpy as np

    out = dict(_drawn_inputs(seed))
    spreads = {}
    factors = {'ctx': 2.869,
     'b_mod': 2.915,
     'a_qn': 8.0,
     'a_kn': 8.0,
     'a_lam': 7.266,
     'a_subln': 6.166,
     'b_conv_b': 8.0,
     'b_outn': 6.611,
     'c_bg': 8.0,
     'c_outn': 4.083,
     'd_qn': 8.0,
     'd_kn': 8.0,
     'd_sink': 8.0}
    for name, (base, spread) in spreads.items():
        noise = np.random.default_rng([zlib.crc32(name.encode()), seed]).standard_normal(out[name].shape)
        drawn = base * np.exp(spread * noise) if base else spread * noise
        out[name] = jnp.asarray(drawn.astype(out[name].dtype))
    for name, factor in factors.items():
        out[name] = (out[name] * factor).astype(out[name].dtype)
    return out
```

```python
from contextlib import ExitStack

import numpy as np

import concourse.bass as bass
from concourse import mybir

F32 = mybir.dt.float32
ALU = mybir.AluOpType
ACT = mybir.ActivationFunctionType
AX = mybir.AxisListType

P = 128
DEPTH = 2
D = 1024
KT = D // P
CTX = 256
SEQ = 1024
T = CTX + SEQ
NT = T // P
NC = CTX // P
GRID_W = 64
HEADS = 4
DH = 64
GW = HEADS * DH
RANK = 16
TAU = 16.0
EPS = 1e-6
NEG = -1e30
LA_MIN = -19.0
BANK = 512
ROWS = 36
BLOCKS = [(0, 512), (512, 512), (1024, 256)]

A0, B0, C0, D0, G0 = 0, 768, 1808, 2352, 2864
A_QK, A_V = (A0, 512), (A0 + 512, 256)
B_QK, B_V, B_G, B_O = (B0, 512), (B0 + 512, 256), B0 + 768, (B0 + 784, 256)
C_QK, C_V, C_LR = (C0, 256), (C0 + 256, 256), (C0 + 512, 32)

SLAB_W = [512] * 6 + [512, 328, 288, 256, 512, 256, 512, 256, 512, 512] + [512] * 2
SLAB_AT = [sum(SLAB_W[:i]) * KT for i in range(len(SLAB_W) + 1)]
(S_BQK, S_BV, S_CQK, S_CV, S_AQK, S_AV, S_D, S_BO, S_G0, S_G1) = range(6, 16)
S_OUT = 16
NSLAB = len(SLAB_W)
RING = 2

PAR = {}
_at = 0
for _n, _w in [("norm_g", KT), ("b_sh", KT), ("b_sc", KT), ("b_gt", D), ("a_gain", 512), ("d_gain", 384),
               ("conv_w", 12), ("conv_b", 4), ("gate_li", 1), ("gate_lf", 1), ("c_bg", 2), ("c_wg", 256),
               ("out_gain", KT), ("a_lam", 128), ("d_sink", 4), ("lam_init", 2)]:
    PAR[_n] = (_at, _at + _w)
    _at += _w
NPAR = _at

CST = {}
_at = 0
for _n, _w in [("ident", P), ("neg", 2 * P), ("band", 2 * P), ("cos_a", NT * 32), ("sin_a", NT * 32),
               ("cos_d", NT * 64), ("sin_d", NT * 64), ("sel_row", 8 * P), ("sel_pair", 4 * P),
               ("sel_mod", 2 * P), ("ones", P), ("diag", GW), ("pick", 6 * P)]:
    CST[_n] = (_at, _at + _w)
    _at += _w
NCST = _at


class Signal:

    def __init__(self, sem):
        self.sem, self.n = sem, 0

    def mark(self, ins, by=1):
        ins.then_inc(self.sem, by)
        self.n += by
        return self.n

    def link(self, eng, ins):
        self.mark(ins)
        eng.wait_ge(self.sem, self.n)


def layer_program(nc, dram):
    ctx = ExitStack()
    with ctx:
        def keep(name, shape, dt=F32):
            return ctx.enter_context(nc.sbuf_tensor(name, shape, dt))

        def signal(name):
            s = stage_ctx[-1].enter_context(nc.semaphore(name, num=first_free + len(stage_sems)))
            stage_sems.append(s)
            return Signal(s)

        stage_ctx, stage_sems = [], []
        ps = ctx.enter_context(nc.psum_tensor("ps", [P, 8, BANK], F32))
        hT = keep("hT", [P, KT, T])
        yT = keep("yT", [P, KT, T])
        ring = keep("ring", [P, RING, KT * 512])
        gate_rows = keep("gate_rows", [P, 2, D])
        par = keep("par", [P, NPAR])
        cst = keep("cst", [P, NCST])
        csil = keep("csil", [P, KT, 2])
        setup_sem = [Signal(ctx.enter_context(nc.semaphore(n))) for n in ("const_loaded", "setup_act", "setup_dve")]

        loaded = [Signal(ctx.enter_context(nc.semaphore(f"slab{i}_loaded"))) for i in range(NSLAB)]
        slab_used = Signal(ctx.enter_context(nc.semaphore("slab_used")))
        first_free = slab_used.sem.num + 1
        env = dict(nc=nc, ps=ps, hT=hT, yT=yT, ring=ring, gate_rows=gate_rows, par=par, cst=cst,
                   csil=csil, mod_cols=keep("mod_cols", [P, 2, KT, 2]), loaded=loaded, slab_used=slab_used,
                   signal=signal, dram=dram)
        setup(nc, env, setup_sem)
        with nc.Fori(0, DEPTH) as layer:
            env["layer"] = layer
            for stage in (stage_modulation, stage_norm, stage_mlstm, stage_gla, stage_diff_attention,
                          stage_window_attention, stage_gates, stage_output):
                with ExitStack() as own:
                    stage_ctx.append(own)
                    stage(nc, env)
                    first = loaded[0].sem.num if stage is stage_output else first_free
                    nc.all_engine_barrier(sems_to_clear=range(first, first_free + len(stage_sems)))
                stage_sems.clear()


def C(env, name, rows=P):
    a, b = CST[name]
    return env["cst"][0:rows, a:b]


def W(env, name, rows=P):
    a, b = PAR[name]
    return env["par"][0:rows, a:b]


def slab(env, i):
    w = SLAB_W[i]
    return env["ring"][:, i % RING, 0:KT * w].rearrange("p (k n) -> p k n", k=KT)


def load_slabs(sp, env, first, last):
    for i in range(first, last):
        if i >= RING:
            sp.wait_ge(env["slab_used"].sem, i - RING + 1)
        src = env["dram"]["w"][bass.ds(env["layer"] * P, P), SLAB_AT[i]:SLAB_AT[i + 1]]
        sp.dma_start(env["ring"][:, i % RING, 0:KT * SLAB_W[i]], src).then_inc(env["loaded"][i].sem, 16)


def rsqrt_newton(dve, sig, y, x, t):
    sig.link(dve, dve.tensor_tensor(t, y, y, ALU.mult))
    sig.link(dve, dve.tensor_tensor(t, t, x, ALU.mult))
    sig.link(dve, dve.tensor_scalar(t, t, -0.5, 1.5, ALU.mult, ALU.add))
    sig.link(dve, dve.tensor_tensor(y, y, t, ALU.mult))


def setup(nc, env, sems):
    dram = env["dram"]
    const_loaded, act_done, dve_done = sems
    with ExitStack() as own, nc.Block() as block:
        craw = own.enter_context(nc.sbuf_tensor("craw", [P, KT, 2], F32))
        csig = own.enter_context(nc.sbuf_tensor("csig", [P, KT, 2], F32))

        @block.sync
        def _(sp):
            sp.dma_start(env["cst"][:, :], dram["cst"][:, :]).then_inc(const_loaded.sem, 16)
            sp.dma_start(craw[:, :, :], dram["c"].rearrange("p (k c) -> p k c", k=KT)).then_inc(const_loaded.sem, 16)
            sp.dma_start(dram["ctx_now"][:, :], dram["tok"][0:CTX, :]).then_inc(const_loaded.sem, 16)
            sp.dma_start(dram["out"][:, :], dram["tok"][CTX:T, :]).then_inc(const_loaded.sem, 16)
            sp.wait_ge(const_loaded.sem, 64)

        @block.scalar
        def _(act):
            act.wait_ge(const_loaded.sem, 64)
            act.activation(csig[:, :, :], craw[:, :, :], ACT.Sigmoid).then_inc(act_done.sem, 1)

        @block.vector
        def _(dve):
            dve.wait_ge(act_done.sem, 1)
            dve.tensor_tensor(env["csil"][:, :, :], craw[:, :, :], csig[:, :, :], ALU.mult)\
               .then_inc(dve_done.sem, 1)
            dve.wait_ge(dve_done.sem, 1)


def stage_modulation(nc, env):
    ps, signal = env["ps"], env["signal"]
    par_loaded, mm, ev, tr, dv, gate_mm, gate_ev = (
        signal(n) for n in ("par_loaded", "mod_product", "mod_rows", "mod_turned", "mod_dve", "gate_spread", "gate_kept"))
    own = ExitStack()
    mod_cols = env["mod_cols"]
    with own, nc.Block() as block:
        rows = own.enter_context(nc.sbuf_tensor("mod_row", [2, 3 * D], F32))

        @block.sync
        def _(sp):
            sp.dma_start(env["par"][:, :], env["dram"]["par"][bass.ds(env["layer"] * P, P), :])\
              .then_inc(par_loaded.sem, 16)
            load_slabs(sp, env, 0, 8)
            sp.wait_ge(par_loaded.sem, 16)

        @block.tensor
        def _(pe):
            for s in range(6):
                pe.wait_ge(env["loaded"][s].sem, 16)
                if s >= 2:
                    pe.wait_ge(ev.sem, s - 1)
                for k in range(KT):
                    last = pe.matmul(ps[0:2, s % 2, :], env["csil"][:, k, :], slab(env, s)[:, k, :],
                                     start=k == 0, stop=k == KT - 1)
                last.then_inc(mm.sem, 1)
                pe.wait_ge(mm.sem, s + 1)
                pe.sem_inc(env["slab_used"].sem, 1)
            pe.wait_ge(ev.sem, 4)
            for i in range(2 * KT):
                last = pe.transpose(ps[:, 2, 2 * i:2 * i + 2], rows[:, i * P:(i + 1) * P], C(env, "ident")[0:2, 0:2])
            last.then_inc(tr.sem, 1)
            pe.wait_ge(dv.sem, 1)
            sel = C(env, "sel_mod", 2).rearrange("p (a b) -> p a b", a=2)
            for v in range(2):
                for n in range(2):
                    last = pe.matmul(ps[:, 3 + 2 * v + n, :], sel[:, v, :], rows[:, 2 * D + n * 512:2 * D + (n + 1) * 512],
                                     start=True, stop=True)
                    last.then_inc(gate_mm.sem, 1)

        @block.scalar
        def _(act):
            for s in range(6):
                act.wait_ge(mm.sem, s + 1)
                act.activation(rows[:, s * 512:(s + 1) * 512], ps[0:2, s % 2, :], ACT.Copy).then_inc(ev.sem, 1)
            for i in range(4):
                act.wait_ge(gate_mm.sem, i + 1)
                act.activation(env["gate_rows"][:, i // 2, (i % 2) * 512:(i % 2 + 1) * 512], ps[:, 3 + i, :], ACT.Copy)\
                   .then_inc(gate_ev.sem, 1)
            act.wait_ge(gate_ev.sem, 4)

        @block.vector
        def _(dve):
            dve.wait_ge(par_loaded.sem, 16)
            dve.wait_ge(ev.sem, 6)
            dv.mark(dve.tensor_tensor(rows[:, 2 * D:], rows[:, 2 * D:], W(env, "b_gt", 2), ALU.add))
            dve.wait_ge(tr.sem, 1)
            turned = ps[:, 2, 0:4 * KT].rearrange("p (s k v) -> p s k v", s=2, k=KT)
            for s, b in ((0, "b_sh"), (1, "b_sc")):
                dv.link(dve, dve.tensor_tensor(mod_cols[:, s, :, :], turned[:, s, :, :],
                                               W(env, b).unsqueeze(2).broadcast_to([P, KT, 2]), ALU.add))
            dv.link(dve, dve.tensor_scalar(mod_cols[:, 1, :, :], mod_cols[:, 1, :, :], 1.0, None, ALU.add))
            dv.link(dve, dve.tensor_tensor(mod_cols[:, 1, :, :], mod_cols[:, 1, :, :],
                                           W(env, "norm_g").unsqueeze(2).broadcast_to([P, KT, 2]), ALU.mult))
            dv.link(dve, dve.tensor_scalar(W(env, "out_gain")[:, 0:2], W(env, "out_gain")[:, 0:2],
                                           W(env, "lam_init")[:, 1:2], None, ALU.mult))


def stage_norm(nc, env):
    ps, signal, hT = env["ps"], env["signal"], env["hT"]
    rowsx = env["yT"][:, :, :].rearrange("p k t -> p (k t)").rearrange("p (t d) -> p t d", t=NT)
    x_loaded = [signal(f"x{t}_loaded") for t in range(NT)]
    squares, ms_ready, root, rstd_ready, scaled_a, scaled_d, turned, kept_a, kept_d, dv = (
        signal(n) for n in ("x_squares", "x_mean", "x_root", "x_rstd", "x_scaled_act", "x_scaled_dve",
                            "x_turned", "h_kept_act", "h_kept_dve", "norm_dve"))
    mod_cols = env["mod_cols"]
    groups = [(0, 0, 2), (1, 2, 4), (1, 6, 4)]
    jobs = [(k, g) for g in groups for k in range(KT)]
    own = ExitStack()
    with own, nc.Block() as block:
        junk = hT[:, :, :].rearrange("p k t -> p (k t)").rearrange("p (t d) -> p t d", t=NT)
        small = own.enter_context(nc.sbuf_tensor("x_stats", [P, 4, NT], F32))
        ss, ms, rstd, tmp = (small[:, i, :] for i in range(4))

        @block.sync
        def _(sp):
            for t in range(NT):
                src = env["dram"]["ctx_now"][t * P:(t + 1) * P, :] if t < NC else \
                    env["dram"]["out"][(t - NC) * P:(t - NC + 1) * P, :]
                sp.dma_start(rowsx[:, t, :], src).then_inc(x_loaded[t].sem, 16)

        @block.scalar
        def _(act):
            for t in range(NT):
                act.wait_ge(x_loaded[t].sem, 16)
                act.activation(junk[:, t, :], rowsx[:, t, :], ACT.Square, accum_out=ss[:, t:t + 1]).then_inc(squares.sem, 1)
            act.wait_ge(ms_ready.sem, 1)
            root.link(act, act.activation(rstd, ms, ACT.Ln))
            root.mark(act.activation(rstd, rstd, ACT.Exp, scale=-0.5))
            act.wait_ge(rstd_ready.sem, 1)
            for t in range(0, NT, 2):
                act.activation(rowsx[:, t, :], rowsx[:, t, :], ACT.Copy, scale=rstd[:, t:t + 1]).then_inc(scaled_a.sem, 1)
            for n, (k, (v, t0, m)) in enumerate(jobs):
                if n % 2 == 0:
                    act.wait_ge(turned.sem, n + 1)
                    act.activation(hT[:, k, t0 * P:(t0 + m) * P], ps[:, n % 4, 0:m * P], ACT.Identity,
                                   bias=mod_cols[:, 0, k, v:v + 1], scale=mod_cols[:, 1, k, v:v + 1]).then_inc(kept_a.sem, 1)

        @block.vector
        def _(dve):
            dve.wait_ge(squares.sem, NT)
            dve.tensor_scalar(ms, ss, 1.0 / D, EPS, ALU.mult, ALU.add).then_inc(ms_ready.sem, 1)
            dve.wait_ge(root.sem, 2)
            rsqrt_newton(dve, dv, rstd, ms, tmp)
            dve.sem_inc(rstd_ready.sem, 1)
            for t in range(1, NT, 2):
                dve.tensor_scalar(rowsx[:, t, :], rowsx[:, t, :], rstd[:, t:t + 1], None, ALU.mult)\
                   .then_inc(scaled_d.sem, 1)
            for n, (k, (v, t0, m)) in enumerate(jobs):
                if n % 2 == 1:
                    dve.wait_ge(turned.sem, n + 1)
                    dve.tensor_scalar(hT[:, k, t0 * P:(t0 + m) * P], ps[:, n % 4, 0:m * P],
                                      mod_cols[:, 1, k, v:v + 1], mod_cols[:, 0, k, v:v + 1], ALU.mult, ALU.add)\
                       .then_inc(kept_d.sem, 1)

        @block.tensor
        def _(pe):
            for n, (k, (v, t0, m)) in enumerate(jobs):
                pe.wait_ge(scaled_a.sem, (t0 + m) // 2)
                pe.wait_ge(scaled_d.sem, (t0 + m) // 2)
                if n >= 4:
                    pe.wait_ge((kept_a if n % 2 == 0 else kept_d).sem, (n - 4) // 2 + 1)
                for t in range(t0, t0 + m):
                    last = pe.transpose(ps[:, n % 4, (t - t0) * P:(t - t0 + 1) * P],
                                        rowsx[:, t, k * P:(k + 1) * P], C(env, "ident"))
                last.then_inc(turned.sem, 1)


def proj_channels(pe, env, out, s, c0, c1, t0, n):
    for k in range(KT):
        last = pe.matmul(out, slab(env, s)[:, k, c0:c1], env["hT"][:, k, t0:t0 + n], start=k == 0, stop=k == KT - 1)
    return last


def proj_tokens(pe, env, out, s, c0, c1, t):
    for k in range(KT):
        last = pe.matmul(out, env["hT"][:, k, t * P:(t + 1) * P], slab(env, s)[:, k, c0:c1],
                         start=k == 0, stop=k == KT - 1)
    return last


def scan_order(way):
    return list(range(NT)) if way == 0 else list(range(NC - 1, -1, -1)) + list(range(NT - 1, NC - 1, -1))


UNITS = [(way, i, scan_order(way)[i]) for i in range(NT) for way in range(2)]


def second_visit(u):
    return any(UNITS[n][2] == UNITS[u][2] for n in range(u))


def stage_mlstm(nc, env):
    ps, signal, hT, yT, ring = (env[n] for n in ("ps", "signal", "hT", "yT", "ring"))
    loaded, slab_used = env["loaded"], env["slab_used"]
    outer = ExitStack()
    with outer:
        v1 = outer.enter_context(nc.sbuf_tensor("b_v", [P, NT, HEADS, DH + 1], F32))
        qkT = outer.enter_context(nc.sbuf_tensor("b_qkT", [P, 4, T], F32))
        row_b = outer.enter_context(nc.sbuf_tensor("b_row_b", [ROWS, T], F32))[:, :]
        cols = outer.enter_context(nc.sbuf_tensor("b_cols", [P, NT, 4, ROWS], F32))
        ends = outer.enter_context(nc.sbuf_tensor("b_ends", [ROWS, 4, NT], F32))
        decay = outer.enter_context(nc.sbuf_tensor("b_decay", [P, 4, NT], F32))
        conv_in = yT[:, 4:8, :]
        ktm = yT[:, 4:6, :].rearrange("p a t -> p (a t)").rearrange("p (t c) -> p t c", t=NT)
        hB = yT[:, 0:2, :].rearrange("p a t -> p (a t)").rearrange("p (t h d) -> p t h d", t=NT, h=HEADS)
        row_e = yT[0:ROWS, 2, :]

        mm, ev, act_s, act_l, dv, conv_ready, silu_ready, logsig, rows_ready, turned, turned_kept, dec_ready, v_ones = (
            signal(n) for n in ("b_product", "b_kept", "b_sigmoid", "b_logs", "b_dve", "b_conv", "b_silu", "b_logsig_in",
                                "b_rows", "b_turned", "b_turned_kept", "b_dec", "b_ones"))
        jobs = [("qk", c, b) for c in range(4) for b in BLOCKS] + [(g, 0, b) for g in ("li", "lf") for b in BLOCKS] + \
            [("v", t, None) for t in range(NT)]
        n_qk, n_gate = 12, 6

        with ExitStack() as own, nc.Block() as block:
            row_a, row_c, row_d = (own.enter_context(nc.sbuf_tensor(f"b_row_{i}", [ROWS, T], F32))[:, :] for i in "acd")
            chunked = [r.rearrange("p (c t) -> p c t", c=NT) for r in (row_a, row_b, row_c, row_d, row_e)]

            @block.sync
            def _(sp):
                load_slabs(sp, env, 8, 10)

            @block.gpsimd
            def _(pool):
                pool.memset(v1[:, :, :, DH:DH + 1], 1.0).then_inc(v_ones.sem, 1)
                pool.wait_ge(v_ones.sem, 1)

            @block.tensor
            def _(pe):
                for n, (kind, c, b) in enumerate(jobs):
                    if n == 0:
                        pe.wait_ge(loaded[S_BQK].sem, 16)
                    if n == n_qk:
                        pe.wait_ge(loaded[S_BV].sem, 16)
                    if n >= 4:
                        pe.wait_ge(ev.sem, n - 3)
                    if kind == "qk":
                        last = proj_channels(pe, env, ps[:, n % 4, 0:b[1]], S_BQK, c * P, (c + 1) * P, *b)
                    elif kind == "v":
                        last = proj_tokens(pe, env, ps[:, n % 4, 0:GW], S_BV, 0, GW, c)
                    else:
                        c0 = GW + (0 if kind == "li" else ROWS)
                        last = proj_channels(pe, env, ps[0:ROWS, n % 4, 0:b[1]], S_BV, c0, c0 + ROWS, *b)
                    last.then_inc(mm.sem, 1)
                    if n in (n_qk - 1, len(jobs) - 1):
                        pe.wait_ge(mm.sem, n + 1)
                        pe.sem_inc(slab_used.sem, 1)
                pe.wait_ge(silu_ready.sem, 4)
                for t in range(NT):
                    if t >= 4:
                        pe.wait_ge(turned_kept.sem, t - 3)
                    for c in range(2):
                        last = pe.transpose(ps[:, t % 4, c * P:(c + 1) * P], qkT[:, 2 + c, t * P:(t + 1) * P], C(env, "ident"))
                    last.then_inc(turned.sem, 1)
                pe.wait_ge(rows_ready.sem, 1)
                for t in range(NT):
                    for q, r in enumerate((row_a, row_c, row_d, row_e)):
                        at = (t % 3) * 4 * ROWS + q * ROWS
                        last = pe.transpose(ps[:, 4 + t // 3, at:at + ROWS], r[:, t * P:(t + 1) * P],
                                            C(env, "ident")[0:ROWS, 0:ROWS])
                last.then_inc(turned.sem, 1)
                pe.wait_ge(dec_ready.sem, 1)
                pe.wait_ge(turned_kept.sem, NT)
                sel = C(env, "sel_pair", ROWS).rearrange("p (a b) -> p a b", a=4)
                for i in range(4):
                    last = pe.matmul(ps[:, 0, i * NT:(i + 1) * NT], sel[:, i, :], ends[:, 3, :], start=True, stop=True)
                last.then_inc(turned.sem, 1)

            @block.scalar
            def _(act):
                for n, (kind, c, b) in enumerate(jobs):
                    act.wait_ge(mm.sem, n + 1)
                    if kind == "qk":
                        ins = act.activation(conv_in[:, c, b[0]:b[0] + b[1]], ps[:, n % 4, 0:b[1]], ACT.Copy)
                    elif kind == "v":
                        ins = act.activation(v1[:, c, :, 0:DH], ps[:, n % 4, 0:GW].rearrange("p (h d) -> p h d", h=HEADS),
                                             ACT.Copy)
                    else:
                        ins = act.activation((row_a if kind == "li" else row_b)[:, b[0]:b[0] + b[1]],
                                             ps[0:ROWS, n % 4, 0:b[1]], ACT.Identity, bias=W(env, "gate_" + kind, ROWS))
                    ins.then_inc(ev.sem, 1)
                act.wait_ge(ev.sem, n_qk + n_gate)
                act_l.link(act, act.activation(row_c, row_b, ACT.Abs))
                act_l.link(act, act.activation(row_c, row_c, ACT.Exp, scale=-1.0))
                act_l.mark(act.activation(row_c, row_c, ACT.Ln, bias=1.0))
                for c in range(4):
                    act.wait_ge(conv_ready.sem, c + 1)
                    act.activation(conv_in[:, c, :], qkT[:, c, :], ACT.Sigmoid).then_inc(act_s.sem, 1)
                for t in range(NT):
                    act.wait_ge(turned.sem, t + 1)
                    act.activation(ktm[:, t, :], ps[:, t % 4, 0:GW], ACT.Copy).then_inc(turned_kept.sem, 1)
                act.wait_ge(rows_ready.sem, 1)
                act.activation(ends[:, 3, :], ends[:, 3, :], ACT.Exp).then_inc(dec_ready.sem, 1)
                act.wait_ge(turned.sem, NT + 1)
                for b in range(4):
                    m = min(3, NT - 3 * b)
                    src = ps[:, 4 + b, 0:m * 4 * ROWS].rearrange("p (t q r) -> p t q r", t=m, q=4)
                    for q, (f, scale) in enumerate(((ACT.Copy, 1.0), (ACT.Exp, 1.0), (ACT.Exp, -1.0), (ACT.Exp, 1.0))):
                        act.activation(cols[:, 3 * b:3 * b + m, q, :], src[:, :, q, :], f, scale=scale)\
                           .then_inc(turned_kept.sem, 1)
                act.wait_ge(turned.sem, NT + 2)
                act.activation(decay[:, :, :], ps[:, 0, 0:4 * NT].rearrange("p (a b) -> p a b", a=4), ACT.Copy)\
                   .then_inc(turned_kept.sem, 1)
                act.wait_ge(turned_kept.sem, NT + 17)

            @block.vector
            def _(dve):
                cw = W(env, "conv_w").rearrange("p (c j) -> p c j", c=4)
                for c in range(4):
                    dve.wait_ge(ev.sem, 3 * (c + 1))
                    y, x = qkT[:, c, :], conv_in[:, c, :]
                    dv.link(dve, dve.tensor_scalar(y, x, cw[:, c, 1:2], W(env, "conv_b")[:, c:c + 1], ALU.mult, ALU.add))
                    for a, b in ((0, CTX), (CTX, T)):
                        dv.link(dve, dve.scalar_tensor_tensor(out=y[:, a + 1:b], in0=x[:, a:b - 1], scalar=cw[:, c, 0:1],
                                                              in1=y[:, a + 1:b], op0=ALU.mult, op1=ALU.add))
                        ins = dve.scalar_tensor_tensor(out=y[:, a:b - 1], in0=x[:, a + 1:b], scalar=cw[:, c, 2:3],
                                                       in1=y[:, a:b - 1], op0=ALU.mult, op1=ALU.add)
                        dv.link(dve, ins)
                    dve.sem_inc(conv_ready.sem, 1)
                dve.wait_ge(act_l.sem, 3)
                dv.link(dve, dve.scalar_tensor_tensor(out=row_b, in0=row_b, scalar=0.0, in1=row_c,
                                                      op0=ALU.min, op1=ALU.subtract))
                ones = C(env, "ones")
                dv.mark(dve.memset(row_d, 0.0))
                dv.link(dve, dve.memset(ends[:, :, :], 0.0))
                for t in range(NT):
                    a, b = t * P, (t + 1) * P
                    dv.mark(dve.tensor_tensor_scan(row_c[0:HEADS, a:b], ones[0:HEADS, :], row_b[0:HEADS, a:b],
                                                   0.0, ALU.mult, ALU.add))
                    dv.mark(dve.tensor_tensor_scan(row_c[32:ROWS, a:b][:, ::-1], ones[32:ROWS, :],
                                                   row_b[32:ROWS, a:b][:, ::-1], 0.0, ALU.mult, ALU.add))
                dv.mark(dve.tensor_tensor_scan(row_d[0:HEADS, :], row_b[0:HEADS, :], row_a[0:HEADS, :], 0.0,
                                               ALU.add, ALU.max))
                dv.link(dve, dve.tensor_tensor_scan(row_d[32:ROWS, 0:CTX][:, ::-1], row_b[32:ROWS, 0:CTX][:, ::-1],
                                                    row_a[32:ROWS, 0:CTX][:, ::-1], 0.0, ALU.add, ALU.max))
                dv.link(dve, dve.tensor_tensor_scan(row_d[32:ROWS, CTX:T][:, ::-1], row_b[32:ROWS, CTX:T][:, ::-1],
                                                    row_a[32:ROWS, CTX:T][:, ::-1], row_d[32:ROWS, 0:1], ALU.add, ALU.max))
                cc, cd = chunked[2], chunked[3]
                for r, at in ((slice(0, HEADS), P - 1), (slice(32, ROWS), 0)):
                    dv.mark(dve.tensor_copy(ends[r, 0, :].unsqueeze(2), cc[r, :, at:at + 1]))
                    dv.link(dve, dve.tensor_copy(ends[r, 1, :].unsqueeze(2), cd[r, :, at:at + 1]))
                dv.mark(dve.tensor_copy(ends[0:HEADS, 2, 1:NT], ends[0:HEADS, 1, 0:NT - 1]))
                dv.mark(dve.tensor_copy(ends[32:ROWS, 2, 0:1], ends[32:ROWS, 1, 1:2]))
                dv.mark(dve.tensor_copy(ends[32:ROWS, 2, NT - 1:NT], ends[32:ROWS, 1, 0:1]))
                dv.link(dve, dve.tensor_copy(ends[32:ROWS, 2, NC:NT - 1], ends[32:ROWS, 1, NC + 1:NT]))
                dv.link(dve, dve.tensor_tensor(ends[:, 0, :], ends[:, 0, :], ends[:, 1, :], ALU.subtract))
                dv.link(dve, dve.tensor_tensor(ends[:, 3, :], ends[:, 0, :], ends[:, 2, :], ALU.add))
                wide = lambda i: ends[:, i, :].unsqueeze(2).broadcast_to([ROWS, NT, P])
                dv.link(dve, dve.tensor_tensor(row_a, row_a, row_c, ALU.subtract))
                dv.link(dve, dve.tensor_tensor(row_b, row_c, row_d, ALU.subtract))
                dv.mark(dve.tensor_tensor(chunked[2], chunked[1], wide(2), ALU.add))
                dv.link(dve, dve.tensor_tensor(chunked[4], chunked[0], wide(0), ALU.add))
                dve.sem_inc(rows_ready.sem, 1)
                for c in range(4):
                    dve.wait_ge(act_s.sem, c + 1)
                    dve.scalar_tensor_tensor(out=qkT[:, c, :], in0=qkT[:, c, :], scalar=1.0 if c < 2 else DH ** -0.5,
                                             in1=conv_in[:, c, :], op0=ALU.mult, op1=ALU.mult).then_inc(silu_ready.sem, 1)
                dve.wait_ge(silu_ready.sem, 4)

        (d_mm, s_mm, dm_ready, w_ready, sw_ready, inter_mm, u_mm, intra_mm, vw_ready, fin, dv2, finished, zeroed) = (
            signal(n) for n in ("b_logs_mm", "b_scores_mm", "b_logw", "b_weight", "b_weighted", "b_inter_mm", "b_new_mm",
                                "b_intra_mm", "b_vw", "b_psum_read", "b_dve2", "b_state", "b_zeroed"))
        with ExitStack() as own, nc.Block() as block:
            def tile(name, shape):
                return own.enter_context(nc.sbuf_tensor(name, shape, F32))

            logw = tile("b_logw", [P, HEADS, P])
            wgt = tile("b_wgt", [P, HEADS, P])
            sw = tile("b_sw", [P, HEADS, P])
            vw = tile("b_vw", [P, 2, HEADS, DH + 1])
            state = tile("b_state", [P, 2, 2, DH + 1])
            tmp = tile("b_tmp", [P, HEADS, DH + 1])
            num = tile("b_num", [P, HEADS, DH + 1])
            den = tile("b_den", [P, HEADS])
            neg = C(env, "neg").rearrange("p (a b) -> p a b", a=2)
            sel = C(env, "sel_row", ROWS).rearrange("p (a b) -> p a b", a=8)
            NU = len(UNITS)

            def col(j, q, way):
                return cols[:, j, q, 32 * way:32 * way + HEADS]

            @block.gpsimd
            def _(pool):
                for u, (way, i, j) in enumerate(UNITS):
                    if u >= 2:
                        pool.wait_ge(u_mm.sem, u - 1)
                    pool.tensor_tensor(vw[:, u % 2, :, :], v1[:, j, :, :],
                                       col(j, 3, way).unsqueeze(2).broadcast_to([P, HEADS, DH + 1]), ALU.mult)\
                        .then_inc(vw_ready.sem, 1)

            @block.tensor
            def _(pe):
                def logs(u):
                    way, i, j = UNITS[u]
                    if u >= 2:
                        pe.wait_ge(dm_ready.sem, HEADS * (u - 1))
                    for h in range(HEADS):
                        last = pe.matmul(ps[:, u % 2, h * P:(h + 1) * P], sel[:, way * HEADS + h, :],
                                         row_b[:, j * P:(j + 1) * P], start=True, stop=True)
                    last.then_inc(d_mm.sem, 1)

                def scores(u):
                    j = UNITS[u][2]
                    t0, t1 = j * P, (j + 1) * P
                    if u >= 1:
                        pe.wait_ge(sw_ready.sem, 2 * u)
                    for h in range(HEADS):
                        r = slice(64 * (h % 2), 64 * (h % 2) + 64)
                        last = pe.matmul(ps[:, 2 + h % 2, (h // 2) * P:(h // 2 + 1) * P], qkT[r, 2 + h // 2, t0:t1],
                                         qkT[r, h // 2, t0:t1], start=True, stop=True)
                    last.then_inc(s_mm.sem, 1)

                logs(0)
                scores(0)
                for u, (way, i, j) in enumerate(UNITS):
                    t0, t1 = j * P, (j + 1) * P
                    if u + 1 < NU:
                        logs(u + 1)
                    if u == 0:
                        pe.wait_ge(zeroed.sem, 1)
                    else:
                        pe.wait_ge(finished.sem, u)
                    for h in range(HEADS):
                        r = slice(64 * (h % 2), 64 * (h % 2) + 64)
                        last = pe.matmul(ps[:, 5 + 2 * (h % 2), (h // 2) * (DH + 1):(h // 2 + 1) * (DH + 1)], qkT[r, h // 2, t0:t1],
                                         state[r, way, h // 2, :], start=True, stop=True)
                    last.then_inc(inter_mm.sem, 1)
                    pe.wait_ge(vw_ready.sem, u + 1)
                    for h in range(HEADS):
                        r = slice(64 * (h % 2), 64 * (h % 2) + 64)
                        last = pe.matmul(ps[r, 6, (h // 2) * (DH + 1):(h // 2 + 1) * (DH + 1)], ktm[:, j, h * DH:(h + 1) * DH],
                                         vw[:, u % 2, h, :], start=True, stop=True)
                    last.then_inc(u_mm.sem, 1)
                    pe.wait_ge(sw_ready.sem, 2 * (u + 1))
                    for h in range(HEADS):
                        last = pe.matmul(ps[:, 4, h * (DH + 1):(h + 1) * (DH + 1)], sw[:, h, :], v1[:, j, h, :],
                                         start=True, stop=True)
                    last.then_inc(intra_mm.sem, 1)
                    if u + 1 < NU:
                        scores(u + 1)

            @block.scalar
            def _(act):
                for u in range(NU):
                    act.wait_ge(dm_ready.sem, HEADS * (u + 1))
                    if u >= 1:
                        act.wait_ge(sw_ready.sem, 2 * u)
                    act.activation(wgt[:, :, :], logw[:, :, :], ACT.Exp).then_inc(w_ready.sem, 1)

            @block.vector
            def _(dve):
                dve.memset(state[:, :, :, :], 0.0).then_inc(zeroed.sem, 1)
                dve.wait_ge(zeroed.sem, 1)

                def finish(u):
                    way, i, j = UNITS[u]
                    dve.wait_ge(inter_mm.sem, u + 1)
                    intra = ps[:, 4, 0:HEADS * (DH + 1)].rearrange("p (h d) -> p h d", h=HEADS)
                    for odd in range(2):
                        inter = ps[:, 5 + 2 * odd, 0:2 * (DH + 1)].rearrange("p (h d) -> p h d", h=2)
                        dv2.mark(dve.tensor_tensor(tmp[:, odd::2, :], inter,
                                                   col(j, 1, way)[:, odd::2].unsqueeze(2).broadcast_to([P, 2, DH + 1]), ALU.mult))
                    dve.wait_ge(dv2.sem, dv2.n)
                    dve.wait_ge(intra_mm.sem, u + 1)
                    dv2.link(dve, dve.tensor_tensor(num[:, :, :], intra, tmp[:, :, :], ALU.add))
                    nq = num[:, :, DH:DH + 1]
                    d3 = den[:, :].unsqueeze(2)
                    dv2.link(dve, dve.scalar_tensor_tensor(out=d3, in0=nq, scalar=-1.0, in1=nq, op0=ALU.mult, op1=ALU.max))
                    dv2.link(dve, dve.tensor_tensor(den[:, :], den[:, :], col(j, 2, way), ALU.max))
                    dv2.link(dve, dve.reciprocal(den[:, :], den[:, :]))
                    rec = den[:, :].unsqueeze(2).broadcast_to([P, HEADS, DH])
                    if second_visit(u):
                        dv2.link(dve, dve.tensor_tensor(num[:, :, 0:DH], num[:, :, 0:DH], rec, ALU.mult))
                        dv2.link(dve, dve.tensor_tensor(hB[:, j, :, :], hB[:, j, :, :], num[:, :, 0:DH], ALU.add))
                    else:
                        dv2.link(dve, dve.tensor_tensor(hB[:, j, :, :], num[:, :, 0:DH], rec, ALU.mult))
                    dve.wait_ge(u_mm.sem, u + 1)
                    for hp in range(2):
                        ins = dve.scalar_tensor_tensor(out=state[:, way, hp, :], in0=state[:, way, hp, :],
                                                       scalar=decay[:, way * 2 + hp, j:j + 1],
                                                       in1=ps[:, 6, hp * (DH + 1):(hp + 1) * (DH + 1)],
                                                       op0=ALU.mult, op1=ALU.add)
                        dv2.mark(ins)
                    dve.wait_ge(dv2.sem, dv2.n)
                    dve.sem_inc(finished.sem, 1)

                for u, (way, i, j) in enumerate(UNITS):
                    dve.wait_ge(d_mm.sem, u + 1)
                    if u >= 1:
                        dve.wait_ge(w_ready.sem, u)
                    for h in range(HEADS):
                        dve.scalar_tensor_tensor(out=logw[:, h, :], in0=ps[:, u % 2, h * P:(h + 1) * P],
                                                 scalar=col(j, 0, way)[:, h:h + 1], in1=neg[:, way, :],
                                                 op0=ALU.add, op1=ALU.min).then_inc(dm_ready.sem, 1)
                    if u >= 1:
                        finish(u - 1)
                    dve.wait_ge(w_ready.sem, u + 1)
                    dve.wait_ge(s_mm.sem, u + 1)
                    if u >= 1:
                        dve.wait_ge(intra_mm.sem, u)
                    for odd in range(2):
                        dve.tensor_tensor(sw[:, odd::2, :], ps[:, 2 + odd, 0:2 * P].rearrange("p (h t) -> p h t", h=2),
                                          wgt[:, odd::2, :], ALU.mult).then_inc(sw_ready.sem, 1)
                finish(NU - 1)

        turn_out(nc, env, hB, 2, "b", norm=True)


def turn_out(nc, env, src, tile0, name, norm):
    ps, signal, yT = env["ps"], env["signal"], env["yT"]
    sq_ready, ms_ready, root, dv, normed, turned, kept = (
        signal(f"{name}_{n}") for n in ("out_square", "out_mean", "out_root", "out_dve", "out_normed", "out_turned", "out_kept"))
    gain = W(env, "out_gain")
    with ExitStack() as own, nc.Block() as block:
        sq = own.enter_context(nc.sbuf_tensor(f"{name}_outsq", [P, 2, HEADS, DH], F32))
        stat = own.enter_context(nc.sbuf_tensor(f"{name}_outstat", [P, 2, NT, HEADS], F32))

        if norm:
            @block.vector
            def _(dve):
                for t in range(NT):
                    dve.wait_ge(sq_ready.sem, t + 1)
                    dv.mark(dve.tensor_reduce(stat[:, 0, t, :], sq[:, t % 2, :, :], AX.X, ALU.add))
                dve.wait_ge(dv.sem, NT)
                dv.link(dve, dve.tensor_scalar(stat[:, 0, :, :], stat[:, 0, :, :], 1.0 / DH, EPS, ALU.mult, ALU.add))
                dve.sem_inc(ms_ready.sem, 1)
                dve.wait_ge(root.sem, 2)
                for t in range(NT):
                    dve.tensor_tensor(src[:, t, :, :], src[:, t, :, :],
                                      stat[:, 1, t, :].unsqueeze(2).broadcast_to([P, HEADS, DH]), ALU.mult)\
                       .then_inc(normed.sem, 1)

        @block.tensor
        def _(pe):
            for t in range(NT):
                if norm:
                    pe.wait_ge(normed.sem, t + 1)
                if t >= 4:
                    pe.wait_ge(kept.sem, 2 * (t - 3))
                flat = src[:, t, :, :].rearrange("p h d -> p (h d)")
                for c in range(2):
                    last = pe.transpose(ps[:, t % 4, c * P:(c + 1) * P], flat[:, c * P:(c + 1) * P], C(env, "ident"))
                last.then_inc(turned.sem, 1)

        @block.scalar
        def _(act):
            if norm:
                for t in range(NT):
                    if t >= 2:
                        act.wait_ge(dv.sem, t - 1)
                    act.activation(sq[:, t % 2, :, :], src[:, t, :, :], ACT.Square).then_inc(sq_ready.sem, 1)
                act.wait_ge(ms_ready.sem, 1)
                root.link(act, act.activation(stat[:, 1, :, :], stat[:, 0, :, :], ACT.Ln))
                root.mark(act.activation(stat[:, 1, :, :], stat[:, 1, :, :], ACT.Exp, scale=-0.5))
            for t in range(NT):
                act.wait_ge(turned.sem, t + 1)
                for c in range(2):
                    act.activation(yT[:, tile0 + c, t * P:(t + 1) * P], ps[:, t % 4, c * P:(c + 1) * P], ACT.Copy,
                                   scale=gain[:, tile0 + c:tile0 + c + 1]).then_inc(kept.sem, 1)
            act.wait_ge(kept.sem, 2 * NT)


def stage_gla(nc, env):
    ps, signal, hT, yT = (env[n] for n in ("ps", "signal", "hT", "yT"))
    loaded, slab_used = env["loaded"], env["slab_used"]
    outer = ExitStack()
    with outer:
        vC = outer.enter_context(nc.sbuf_tensor("c_v", [P, NT, GW], F32))
        qT = outer.enter_context(nc.sbuf_tensor("c_qT", [P, T], F32))
        kT = outer.enter_context(nc.sbuf_tensor("c_kT", [P, T], F32))
        hC = yT[:, 0:2, :].rearrange("p a t -> p (a t)").rearrange("p (t h d) -> p t h d", t=NT, h=HEADS)
        sums = yT[:, 6:8, :]
        mm, ev, logs, dv = (signal(n) for n in ("c_product", "c_kept", "c_logs", "c_dve"))
        jobs = [(kind, 0, b) for kind in ("q", "k", "lr") for b in BLOCKS] + [("v", t, None) for t in range(NT)] + \
            [("la", z, b) for z in range(2) for b in BLOCKS]
        with ExitStack() as own, nc.Block() as block:
            lrT = own.enter_context(nc.sbuf_tensor("c_lrT", [2 * RANK, T], F32))
            la = own.enter_context(nc.sbuf_tensor("c_la", [P, 2, T], F32))

            @block.sync
            def _(sp):
                load_slabs(sp, env, 10, 12)

            @block.tensor
            def _(pe):
                for n, (kind, c, b) in enumerate(jobs):
                    if n == 0:
                        pe.wait_ge(loaded[S_CQK].sem, 16)
                    if n == 9:
                        pe.wait_ge(loaded[S_CV].sem, 16)
                    if n >= 4:
                        pe.wait_ge(ev.sem, n - 3)
                    bank = ps[:, n % 4, :]
                    if kind in ("q", "k"):
                        c0 = 0 if kind == "q" else P
                        last = proj_channels(pe, env, bank[:, 0:b[1]], S_CQK, c0, c0 + P, *b)
                    elif kind == "lr":
                        last = proj_channels(pe, env, bank[0:2 * RANK, 0:b[1]], S_CQK, GW, GW + 2 * RANK, *b)
                    elif kind == "v":
                        last = proj_tokens(pe, env, bank[:, 0:GW], S_CV, 0, GW, c)
                    else:
                        wg = W(env, "c_wg", 2 * RANK)[:, c * P:(c + 1) * P]
                        last = pe.matmul(bank[:, 0:b[1]], wg, lrT[:, b[0]:b[0] + b[1]], start=True, stop=True)
                    last.then_inc(mm.sem, 1)
                    if n in (8, 18):
                        pe.wait_ge(mm.sem, n + 1)
                        pe.sem_inc(slab_used.sem, 1)

            @block.scalar
            def _(act):
                for n, (kind, c, b) in enumerate(jobs):
                    act.wait_ge(mm.sem, n + 1)
                    bank = ps[:, n % 4, :]
                    if kind == "v":
                        ins = act.activation(vC[:, c, :], bank[:, 0:GW], ACT.Copy)
                    elif kind == "la":
                        ins = act.activation(la[:, c, b[0]:b[0] + b[1]], bank[:, 0:b[1]], ACT.Identity,
                                             bias=W(env, "c_bg")[:, c:c + 1])
                    else:
                        rows = 2 * RANK if kind == "lr" else P
                        out = {"q": qT, "k": kT, "lr": lrT}[kind]
                        ins = act.activation(out[:, b[0]:b[0] + b[1]], bank[0:rows, 0:b[1]], ACT.Copy,
                                             scale=(DH // 2) ** -0.5 if kind == "q" else 1.0)
                    ins.then_inc(ev.sem, 1)
                act.wait_ge(ev.sem, len(jobs))
                logs.link(act, act.activation(sums[:, :, :], la[:, :, :], ACT.Abs))
                logs.link(act, act.activation(sums[:, :, :], sums[:, :, :], ACT.Exp, scale=-1.0))
                logs.mark(act.activation(sums[:, :, :], sums[:, :, :], ACT.Ln, bias=1.0))

            @block.vector
            def _(dve):
                dve.wait_ge(logs.sem, 3)
                dv.link(dve, dve.scalar_tensor_tensor(out=la[:, :, :], in0=la[:, :, :], scalar=0.0, in1=sums[:, :, :],
                                                      op0=ALU.min, op1=ALU.subtract))
                dv.link(dve, dve.tensor_scalar(la[:, :, :], la[:, :, :], 1.0 / TAU, LA_MIN, ALU.mult, ALU.max))
                for t in range(NT):
                    a, b = t * P, (t + 1) * P
                    dv.mark(dve.tensor_tensor_scan(sums[:, 0, a:b], C(env, "ones"), la[:, 0, a:b], 0.0, ALU.mult, ALU.add))
                    dv.mark(dve.tensor_tensor_scan(sums[:, 1, a:b][:, ::-1], C(env, "ones"), la[:, 1, a:b][:, ::-1], 0.0,
                                                   ALU.mult, ALU.add))
                dve.wait_ge(dv.sem, dv.n)

        (diff_ready, decay_ready, scaled, level_mm, src_turned, src_kept, far_kept, picked, o_mm, u_mm, finished,
         zeroed, dv2, act2) = (
            signal(n) for n in ("c_diff", "c_decay", "c_scaled", "c_level_mm", "c_src_turned", "c_src_kept",
                                "c_far_kept", "c_picked", "c_out_mm", "c_new_mm", "c_finished", "c_zeroed", "c_dve2", "c_act2"))
        HALVES = (64, 32, 16, 8)
        NU = len(UNITS)
        with ExitStack() as own, nc.Block() as block:
            def tile(name, shape):
                return own.enter_context(nc.sbuf_tensor(name, shape, F32))

            diff = tile("c_diffs", [P, 5, P])
            decays = tile("c_decays", [P, 8, P])
            qx = tile("c_qx", [P, 2, 6, P])
            kx = tile("c_kx", [P, 2, 6, P])
            acc = tile("c_acc", [P, 2, HEADS, P])
            src = tile("c_src", [P, P])
            state = tile("c_state", [P, 2, GW])
            new = tile("c_new", [P, GW])
            start = tile("c_start", [P, 4])

            def span(u):
                return slice(UNITS[u][2] * P, (UNITS[u][2] + 1) * P)

            @block.gpsimd
            def _(pool):
                pool.memset(acc[:, :, :, :], 0.0).then_inc(zeroed.sem, 1)
                pool.memset(state[:, :, :], 0.0).then_inc(zeroed.sem, 1)
                for u, (way, i, j) in enumerate(UNITS):
                    if u >= 1:
                        pool.wait_ge(decay_ready.sem, u)
                    for lev, half in enumerate(HALVES + (4,)):
                        mid = half - 1 + way
                        view = sums[:, way, span(u)].rearrange("p (b t) -> p b t", t=2 * half)
                        out = diff[:, lev, :].rearrange("p (b t) -> p b t", t=2 * half)
                        pool.tensor_tensor(out, view, view[:, :, mid:mid + 1].broadcast_to([P, P // (2 * half), 2 * half]),
                                           ALU.subtract).then_inc(diff_ready.sem, 1)

            @block.scalar
            def _(act):
                def decay(u):
                    way, i, j = UNITS[u]
                    s = sums[:, way, span(u)]
                    end = P - 1 if way == 0 else 0
                    act.wait_ge(diff_ready.sem, 5 * (u + 1))
                    if u >= 1:
                        act.wait_ge(scaled.sem, 2 * u)
                    act2.link(act, act.activation(decays[:, 2:6, :], diff[:, 0:4, :], ACT.Abs))
                    act.activation(decays[:, 2:6, :], decays[:, 2:6, :], ACT.Exp, scale=-1.0)
                    act.activation(decays[:, 0, :], diff[:, 4, :], ACT.Exp, scale=-1.0)
                    act.activation(decays[:, 6, :], diff[:, 4, :], ACT.Exp)
                    act.activation(decays[:, 7, :], s, ACT.Exp)
                    act.activation(decays[:, 1, :], s, ACT.Exp, scale=-1.0, bias=s[:, end:end + 1])\
                       .then_inc(decay_ready.sem, 1)

                decay(0)
                for u, (way, i, j) in enumerate(UNITS):
                    if u + 1 < NU:
                        decay(u + 1)
                    act.wait_ge(src_turned.sem, u + 1)
                    if u >= 1:
                        act.wait_ge(u_mm.sem, u)
                    act.activation(src[:, :], ps[:, 7, 0:P], ACT.Copy).then_inc(src_kept.sem, 1)
                    act.wait_ge(level_mm.sem, u + 1)
                    if u >= 2:
                        act.wait_ge(o_mm.sem, u - 1)
                    if u == 0:
                        act.wait_ge(zeroed.sem, 1)
                    s0, t0 = (0, 64) if way == 0 else (64, 0)
                    act.activation(acc[s0:s0 + 64, way, :, t0:t0 + 64],
                                   ps[s0:s0 + 64, 0:HEADS, 384:448], ACT.Copy)\
                       .then_inc(far_kept.sem, 1)
                    for blk in (0, 64):
                        s0, t0 = (blk, blk + 32) if way == 0 else (blk + 32, blk)
                        act.activation(acc[s0:s0 + 32, way, :, t0:t0 + 32],
                                       ps[s0:s0 + 32, 0:HEADS, 448:480], ACT.Copy).then_inc(far_kept.sem, 1)

            @block.tensor
            def _(pe):
                def levels(u):
                    way, i, j = UNITS[u]
                    q, k = qx[:, u % 2, :, :], kx[:, u % 2, :, :]
                    pe.wait_ge(scaled.sem, 2 * (u + 1))
                    if u >= 1:
                        pe.wait_ge(src_kept.sem, u)
                        pe.wait_ge(far_kept.sem, 3 * u)
                    pe.transpose(ps[:, 7, 0:P], k[:, 1, :], C(env, "ident")).then_inc(src_turned.sem, 1)
                    if u >= 1:
                        pe.wait_ge(picked.sem, 3 * u)
                    s0, t0 = (0, 64) if way == 0 else (64, 0)
                    for h in range(HEADS):
                        r = slice(32 * h, 32 * h + 32)
                        pe.matmul(ps[s0:s0 + 64, h, 384:448], k[r, 2, s0:s0 + 64], q[r, 0, t0:t0 + 64],
                                  start=True, stop=True, tile_position=(32 * h, s0))
                    for blk in (0, 64):
                        s0, t0 = (blk, blk + 32) if way == 0 else (blk + 32, blk)
                        for h in range(HEADS):
                            r = slice(32 * h, 32 * h + 32)
                            pe.matmul(ps[s0:s0 + 32, h, 448:480], k[r, 3, s0:s0 + 32], q[r, 1, t0:t0 + 32],
                                      start=True, stop=True, tile_position=(32 * h, s0))
                    for n, (a, b) in enumerate(((4, 2), (5, 3), (0, 4))):
                        for h in range(HEADS):
                            r = slice(32 * h, 32 * h + 32)
                            last = pe.matmul(ps[:, h, n * P:(n + 1) * P], k[r, a, :], q[r, b, :], start=True, stop=True,
                                             tile_position=(32 * h, 0))
                    last.then_inc(level_mm.sem, 1)

                def out(u):
                    way, i, j = UNITS[u]
                    pe.wait_ge(src_kept.sem, u + 1)
                    pe.wait_ge(zeroed.sem, 2)
                    if u >= 1:
                        pe.wait_ge(finished.sem, u)
                    pe.matmul(ps[:, 6, 0:GW], src[:, :], vC[:, j, :], start=True, stop=True).then_inc(u_mm.sem, 1)
                    pe.matmul(ps[:, 5, 0:GW], qx[:, u % 2, 5, :], state[:, way, :], start=True, stop=False,
                              skip_group_check=True)
                    pe.wait_ge(far_kept.sem, 3 * (u + 1))
                    pe.wait_ge(picked.sem, 3 * (u + 1))
                    for h in range(HEADS):
                        last = pe.matmul(ps[:, 5, h * DH:(h + 1) * DH], acc[:, way, h, :], vC[:, j, h * DH:(h + 1) * DH],
                                         start=False, stop=h == HEADS - 1, skip_group_check=True)
                    last.then_inc(o_mm.sem, 1)

                for u in range(NU):
                    levels(u)
                    if u >= 1:
                        out(u - 1)
                out(NU - 1)

            @block.vector
            def _(dve):
                def scale(u):
                    way, i, j = UNITS[u]
                    dve.wait_ge(decay_ready.sem, u + 1)
                    if u >= 2:
                        dve.wait_ge(o_mm.sem, u - 1)
                    end = P - 1 if way == 0 else 0
                    dve.tensor_copy(start[:, u % 4:u % 4 + 1], decays[:, 7, end:end + 1])
                    dve.tensor_tensor(kx[:, u % 2, :, :], decays[:, 0:6, :],
                                      kT[:, span(u)].unsqueeze(1).broadcast_to([P, 6, P]), ALU.mult).then_inc(scaled.sem, 1)
                    dve.tensor_tensor(qx[:, u % 2, :, :], decays[:, 2:8, :],
                                      qT[:, span(u)].unsqueeze(1).broadcast_to([P, 6, P]), ALU.mult).then_inc(scaled.sem, 1)

                def finish(u):
                    way, i, j = UNITS[u]
                    dve.wait_ge(u_mm.sem, u + 1)
                    dv2.link(dve, dve.tensor_tensor(new[:, :], ps[:, 6, 0:GW], C(env, "diag"), ALU.mult))
                    dve.wait_ge(o_mm.sem, u + 1)
                    dv2.mark(dve.scalar_tensor_tensor(out=state[:, way, :], in0=state[:, way, :], scalar=start[:, u % 4:u % 4 + 1],
                                                      in1=new[:, :], op0=ALU.mult, op1=ALU.add))
                    o = ps[:, 5, 0:GW].rearrange("p (h d) -> p h d", h=HEADS)
                    if second_visit(u):
                        dv2.mark(dve.tensor_tensor(hC[:, j, :, :], o, hC[:, j, :, :], ALU.add))
                    else:
                        dv2.mark(dve.tensor_copy(hC[:, j, :, :], o))
                    dve.wait_ge(dv2.sem, dv2.n)
                    dve.sem_inc(finished.sem, 1)

                pick = C(env, "pick").bitcast(mybir.dt.uint32).rearrange("p (a b c) -> p a b c", a=2, b=3)
                scale(0)
                for u, (way, i, j) in enumerate(UNITS):
                    if u + 1 < NU:
                        scale(u + 1)
                    if u == 0:
                        dve.wait_ge(zeroed.sem, 2)
                    dve.wait_ge(far_kept.sem, 3 * (u + 1))
                    for n in range(3):
                        if n:
                            dve.wait_ge(picked.sem, 3 * u + n)
                        mask = pick[:, way, n, :].unsqueeze(1).broadcast_to([P, HEADS, P])
                        dve.copy_predicated(acc[:, way, :, :], mask, ps[:, 0:HEADS, n * P:(n + 1) * P])\
                           .then_inc(picked.sem, 1)
                    if u >= 1:
                        finish(u - 1)
                finish(NU - 1)

        turn_out(nc, env, hC, 4, "c", norm=True)


def project_qk(nc, env, name, s_qk, groups, width, qkT, v_of, last_slab_next):
    ps, signal = env["ps"], env["signal"]
    n_qk = groups * width
    nch = n_qk // P
    mm, ev, sq_ready, ms_ready, root, normed, gained, cos_ready, rotated, dv, turned, kept, v_mm, v_ev = (
        signal(f"{name}_{n}") for n in ("product", "kept", "square", "mean", "root", "normed", "gained", "cos", "rotated",
                                        "dve", "turned", "turned_kept", "v_product", "v_kept"))
    loaded, slab_used = env["loaded"], env["slab_used"]
    s_v, v0, nv, v_dst = v_of
    with ExitStack() as own, nc.Block() as block:
        def tile(n, shape):
            return own.enter_context(nc.sbuf_tensor(f"{name}_{n}", shape, F32))

        raw = tile("raw", [P, 2, n_qk])
        sq = tile("sq", [P, n_qk])
        turn = tile("turn", [P, n_qk])
        rot = tile("rot", [P, 2, n_qk])
        stat = tile("stat", [P, 3, groups])
        ms, rstd, tmp = (stat[:, i, :] for i in range(3))
        cos = C(env, f"cos_{name}").rearrange("p (t w) -> p t w", t=NT)
        sin = C(env, f"sin_{name}").rearrange("p (t w) -> p t w", t=NT)
        q4 = width // 4

        def grouped(x):
            return x.rearrange("p (g w) -> p g w", g=groups)

        def quarters(x):
            return x.rearrange("p (g f s w) -> p g f s w", g=groups, f=2, s=2)

        @block.sync
        def _(sp):
            load_slabs(sp, env, *last_slab_next)

        @block.tensor
        def _(pe):
            def turns(t):
                pe.wait_ge(rotated.sem, t + 1)
                if t >= 2:
                    pe.wait_ge(kept.sem, t - 1)
                for c in range(nch):
                    last = pe.transpose(ps[:, 2 + t % 2, c * P:(c + 1) * P], rot[:, t % 2, c * P:(c + 1) * P], C(env, "ident"))
                last.then_inc(turned.sem, 1)

            pe.wait_ge(loaded[s_qk].sem, 16)
            for t in range(NT):
                if t >= 2:
                    pe.wait_ge(sq_ready.sem, t - 1)
                    pe.wait_ge(ev.sem, t - 1)
                proj_tokens(pe, env, ps[:, t % 2, 0:n_qk], s_qk, 0, n_qk, t).then_inc(mm.sem, 1)
                if t >= 2:
                    turns(t - 2)
                if s_v != s_qk and t == NT - 1:
                    pe.wait_ge(mm.sem, NT)
                    pe.sem_inc(slab_used.sem, 1)
            if s_v != s_qk:
                pe.wait_ge(loaded[s_v].sem, 16)
            for t in range(NT):
                if t >= 2:
                    pe.wait_ge(v_ev.sem, t - 1)
                proj_tokens(pe, env, ps[:, 4 + t % 2, 0:nv], s_v, v0, v0 + nv, t).then_inc(v_mm.sem, 1)
                if t < 2:
                    turns(NT - 2 + t)
            pe.wait_ge(v_mm.sem, NT)
            pe.sem_inc(slab_used.sem, 1)

        @block.scalar
        def _(act):
            def keep_turned(t):
                act.wait_ge(turned.sem, t + 1)
                act.activation(qkT[:, 0:nch, t * P:(t + 1) * P], ps[:, 2 + t % 2, 0:n_qk].rearrange("p (c t) -> p c t", c=nch),
                               ACT.Copy).then_inc(kept.sem, 1)

            for t in range(NT):
                act.wait_ge(mm.sem, t + 1)
                if t >= 1:
                    act.wait_ge(ms_ready.sem, t)
                act.activation(sq[:, :], ps[:, t % 2, 0:n_qk], ACT.Square).then_inc(sq_ready.sem, 1)
                if t >= 2:
                    act.wait_ge(rotated.sem, t - 1)
                act.activation(raw[:, t % 2, :], ps[:, t % 2, 0:n_qk], ACT.Copy).then_inc(ev.sem, 1)
                act.wait_ge(ms_ready.sem, t + 1)
                if t >= 1:
                    act.wait_ge(normed.sem, t)
                root.link(act, act.activation(rstd, ms, ACT.Ln))
                root.link(act, act.activation(rstd, rstd, ACT.Exp, scale=-0.5))
                if t >= 2:
                    keep_turned(t - 2)
            for t in range(NT):
                if t < 2:
                    act.wait_ge(v_mm.sem, t + 1)
                    act.activation(v_dst(t), ps[:, 4 + t % 2, 0:nv], ACT.Copy).then_inc(v_ev.sem, 1)
                    keep_turned(NT - 2 + t)
                else:
                    act.wait_ge(v_mm.sem, t + 1)
                    act.activation(v_dst(t), ps[:, 4 + t % 2, 0:nv], ACT.Copy).then_inc(v_ev.sem, 1)
            act.wait_ge(v_ev.sem, NT)
            act.wait_ge(kept.sem, NT)

        @block.gpsimd
        def _(pool):
            for t in range(NT):
                pool.wait_ge(normed.sem, t + 1)
                pool.tensor_tensor(raw[:, t % 2, :], raw[:, t % 2, :], W(env, f"{name}_gain"), ALU.mult)\
                    .then_inc(gained.sem, 1)
                pool.wait_ge(gained.sem, t + 1)
                if t >= 2:
                    pool.wait_ge(turned.sem, t - 1)
                pool.tensor_tensor(grouped(rot[:, t % 2, :]), grouped(raw[:, t % 2, :]),
                                   cos[:, t, :].unsqueeze(1).broadcast_to([P, groups, width]), ALU.mult)\
                    .then_inc(cos_ready.sem, 1)

        @block.vector
        def _(dve):
            for t in range(NT):
                dve.wait_ge(sq_ready.sem, t + 1)
                if t >= 1:
                    dve.wait_ge(root.sem, 2 * t)
                dv.link(dve, dve.tensor_reduce(ms, grouped(sq[:, :]), AX.X, ALU.add))
                dv.link(dve, dve.tensor_scalar(ms, ms, 1.0 / width, EPS, ALU.mult, ALU.add))
                dve.sem_inc(ms_ready.sem, 1)
                dve.wait_ge(root.sem, 2 * (t + 1))
                rsqrt_newton(dve, dv, rstd, ms, tmp)
                dve.wait_ge(ev.sem, t + 1)
                dve.tensor_tensor(grouped(raw[:, t % 2, :]), grouped(raw[:, t % 2, :]),
                                  rstd.unsqueeze(2).broadcast_to([P, groups, width]), ALU.mult).then_inc(normed.sem, 1)
                dve.wait_ge(gained.sem, t + 1)
                x, y = quarters(raw[:, t % 2, :]), quarters(turn[:, :])
                s = sin[:, t, :].rearrange("p (f s w) -> p f s w", f=2, s=2)
                for i in range(2):
                    for f in range(2):
                        ins = dve.tensor_tensor(y[:, :, f, i, :], x[:, :, f, 1 - i, :],
                                                s[:, f, i, :].unsqueeze(1).broadcast_to([P, groups, q4]), ALU.mult)
                        dv.mark(ins)
                dve.wait_ge(dv.sem, dv.n)
                dve.wait_ge(cos_ready.sem, t + 1)
                dve.tensor_tensor(rot[:, t % 2, :], rot[:, t % 2, :], turn[:, :], ALU.add).then_inc(rotated.sem, 1)
                dve.wait_ge(rotated.sem, t + 1)


def stage_diff_attention(nc, env):
    ps, signal = env["ps"], env["signal"]
    SCALE = (DH // 2) ** -0.5
    with ExitStack() as outer:
        qkT = outer.enter_context(nc.sbuf_tensor("a_qkT", [P, 4, T], F32))
        vA = outer.enter_context(nc.sbuf_tensor("a_v", [P, NT, GW], F32))
        yA = env["yT"][:, 6:8, :].rearrange("p a t -> p (a t)").rearrange("p (t h d) -> p t h d", t=NT, h=HEADS)
        project_qk(nc, env, "a", S_AQK, 16, 32, qkT, (S_AV, 0, GW, lambda t: vA[:, t, :]), (12, 14))
        (s_mm, mx, exped, comb, t_mm, t_act, t_dve, o_mm, o_kept, dv, lam_a) = (
            signal(n) for n in ("a_scores", "a_max", "a_exp", "a_combined", "a_turns", "a_turn_act", "a_turn_dve",
                                "a_out_mm", "a_out_read", "a_dve2", "a_lam"))
        units = [(t, h) for t in range(NT) for h in range(HEADS)]
        NU = len(units)

        def keys(t):
            return NC if t < NC else NT

        def chunks(t):
            n = keys(t)
            return [(a, min(a + 4, n)) for a in range(0, n, 4)]

        def before(u, f):
            return sum(f(units[i][0]) for i in range(u))

        n_act = lambda t: len(chunks(t)) - (1 if len(chunks(t)) > 1 else 0)
        n_dve = lambda t: 1 if len(chunks(t)) > 1 else 0
        with ExitStack() as own, nc.Block() as block:
            def tile(n, shape):
                return own.enter_context(nc.sbuf_tensor(f"a_{n}", shape, F32))

            p = tile("p", [P, 2, 2, T])
            aT = tile("aT", [P, NT, P])
            stat = tile("st", [P, 2, 2, 4])
            lam = tile("lm", [P, 2, 32])
            lam2 = tile("lm2", [P, 2])
            nlam = tile("nlam", [P, 1])

            @block.tensor
            def _(pe):
                def scores(u, c):
                    t, h = units[u]
                    if u >= 1:
                        pe.wait_ge(exped.sem, 2 * (u - 1) + c + 1)
                    at = 2 * h + c
                    r = slice(32 * (at % 4), 32 * (at % 4) + 32)
                    n = keys(t) * P
                    for b, k0 in enumerate(range(0, n, BANK)):
                        w = min(BANK, n - k0)
                        last = pe.matmul(ps[:, 3 * c + b, 0:w], qkT[r, at // 4, t * P:(t + 1) * P],
                                         qkT[r, 2 + at // 4, k0:k0 + w], start=True, stop=True,
                                         tile_position=(32 * (at % 4), 0))
                    last.then_inc(s_mm.sem, 1)

                def value(u):
                    t, h = units[u]
                    pe.wait_ge(comb.sem, u + 1)
                    for n, (a, b) in enumerate(chunks(t)):
                        if n == 0 and u >= 1:
                            pe.wait_ge(t_act.sem, before(u, n_act))
                        if n == 1:
                            pe.wait_ge(o_kept.sem, u)
                        if n == 2:
                            pe.wait_ge(t_act.sem, before(u, n_act) + 1)
                        for k in range(a, b):
                            last = pe.transpose(ps[:, 6 + n % 2, (k - a) * P:(k - a + 1) * P],
                                                p[:, u % 2, 0, k * P:(k + 1) * P], C(env, "ident"))
                        last.then_inc(t_mm.sem, 1)
                    pe.wait_ge(t_act.sem, before(u + 1, n_act))
                    pe.wait_ge(t_dve.sem, before(u + 1, n_dve))
                    if u >= 1:
                        pe.wait_ge(o_kept.sem, u)
                    n = keys(t)
                    for k in range(n):
                        last = pe.matmul(ps[:, 7, 0:DH], aT[:, k, :], vA[:, k, h * DH:(h + 1) * DH], start=k == 0, stop=k == n - 1)
                    last.then_inc(o_mm.sem, 1)

                for u in range(NU):
                    scores(u, 0)
                    scores(u, 1)
                    if u >= 1:
                        value(u - 1)
                value(NU - 1)

            @block.scalar
            def _(act):
                def exp(u, c):
                    t, h = units[u]
                    act.wait_ge(mx.sem, 2 * u + c + 1)
                    if u >= 2:
                        act.wait_ge(t_mm.sem, before(u - 1, lambda t: len(chunks(t))))
                    n = keys(t) * P
                    st = stat[:, u % 2, c, :]
                    act.activation(p[:, u % 2, c, 0:n], ps[:, 3 * c:3 * c + 3, :].rearrange("p b n -> p (b n)")[:, 0:n], ACT.Exp,
                                   bias=st[:, 0:1], scale=SCALE, accum_out=st[:, 1:2]).then_inc(exped.sem, 1)

                def keep(u, n):
                    t, h = units[u]
                    if n >= len(chunks(t)):
                        return
                    a, b = chunks(t)[n]
                    act.wait_ge(t_mm.sem, before(u, lambda t: len(chunks(t))) + n + 1)
                    if n == 0 and u >= 1:
                        act.wait_ge(o_mm.sem, u)
                    act.activation(aT[:, a:b, :], ps[:, 6, 0:(b - a) * P].rearrange("p (k t) -> p k t", t=P), ACT.Copy)\
                       .then_inc(t_act.sem, 1)

                act.wait_ge(lam_a.sem, 2)
                act.activation(lam2[:, :], lam2[:, :], ACT.Exp).then_inc(lam_a.sem, 1)
                for u in range(NU):
                    exp(u, 0)
                    if u >= 1:
                        keep(u - 1, 0)
                    exp(u, 1)
                    if u >= 1:
                        keep(u - 1, 2)
                keep(NU - 1, 0)
                keep(NU - 1, 2)

            @block.vector
            def _(dve):
                def maximum(u, c):
                    t, h = units[u]
                    dve.wait_ge(s_mm.sem, 2 * u + c + 1)
                    n = keys(t) * P
                    st = stat[:, u % 2, c, :]
                    dv.link(dve, dve.tensor_reduce(st[:, 0:1], ps[:, 3 * c:3 * c + 3, :].rearrange("p b n -> p (b n)")[:, 0:n],
                                                   AX.X, ALU.max))
                    dve.tensor_scalar(st[:, 0:1], st[:, 0:1], -SCALE, None, ALU.mult).then_inc(mx.sem, 1)

                def combine(u):
                    t, h = units[u]
                    st = stat[:, u % 2, :, :]
                    dve.wait_ge(exped.sem, 2 * u + 2)
                    dv.link(dve, dve.reciprocal(st[:, :, 2:3], st[:, :, 1:2]))
                    dv.link(dve, dve.tensor_tensor(st[:, 0, 3:4], st[:, 0, 1:2], st[:, 1, 2:3], ALU.mult))
                    dv.link(dve, dve.tensor_tensor(st[:, 0, 3:4], st[:, 0, 3:4], nlam[:, :], ALU.mult))
                    n = keys(t) * P
                    dve.scalar_tensor_tensor(out=p[:, u % 2, 0, 0:n], in0=p[:, u % 2, 1, 0:n], scalar=st[:, 0, 3:4],
                                             in1=p[:, u % 2, 0, 0:n], op0=ALU.mult, op1=ALU.add).then_inc(comb.sem, 1)

                def keep(u):
                    t, h = units[u]
                    if len(chunks(t)) > 1:
                        a, b = chunks(t)[1]
                        dve.wait_ge(t_mm.sem, before(u, lambda t: len(chunks(t))) + 2)
                        dve.tensor_copy(aT[:, a:b, :], ps[:, 7, 0:(b - a) * P].rearrange("p (k t) -> p k t", t=P))\
                           .then_inc(t_dve.sem, 1)
                    dve.wait_ge(o_mm.sem, u + 1)
                    dve.tensor_scalar(yA[:, t, h, :], ps[:, 7, 0:DH], stat[:, u % 2, 0, 2:3], None, ALU.mult)\
                       .then_inc(o_kept.sem, 1)

                lp = W(env, "a_lam").rearrange("p (a b w) -> p a b w", a=2, b=2)
                lam_a.link(dve, dve.tensor_tensor(lam[:, :, :], lp[:, :, 0, :], lp[:, :, 1, :], ALU.mult))
                lam_a.mark(dve.tensor_reduce(lam2[:, :], lam[:, :, :], AX.X, ALU.add))
                dve.wait_ge(lam_a.sem, 3)
                dv.link(dve, dve.tensor_tensor(nlam[:, :], lam2[:, 1:2], lam2[:, 0:1], ALU.subtract))
                dv.link(dve, dve.tensor_tensor(nlam[:, :], nlam[:, :], W(env, "lam_init")[:, 0:1], ALU.subtract))
                for u in range(NU):
                    maximum(u, 0)
                    maximum(u, 1)
                    if u >= 1:
                        keep(u - 1)
                    combine(u)
                keep(NU - 1)
                dve.wait_ge(o_kept.sem, NU)

        turn_out(nc, env, yA, 0, "a", norm=True)


def stage_window_attention(nc, env):
    ps, signal = env["ps"], env["signal"]
    SCALE = DH ** -0.5
    with ExitStack() as outer:
        qkT = outer.enter_context(nc.sbuf_tensor("d_qkT", [P, 3, T], F32))
        vD = outer.enter_context(nc.sbuf_tensor("d_v", [P, NT, P], F32))
        yD = outer.enter_context(nc.sbuf_tensor("d_y", [P, NT, HEADS, DH], F32))
        project_qk(nc, env, "d", S_D, 6, 64, qkT, (S_D, 384, P, lambda t: vD[:, t, :]), (14, 15))
        (s_mm, mx, exped, summed, t_mm, t_kept, o_mm, o_kept, dv, sunk) = (
            signal(n) for n in ("d_scores", "d_max", "d_exp", "d_sum", "d_turns", "d_turn_kept", "d_out_mm", "d_out_read",
                                "d_dve2", "d_sink"))
        units = [(t, h) for t in range(NT) for h in range(HEADS)]
        NU = len(units)

        def key_tiles(t):
            ctx = [(k, None) for k in range(NC)]
            return ctx if t < NC else ctx + [(k, {-1: 0, 0: None, 1: 1}[k - t]) for k in (t - 1, t, t + 1) if NC <= k < NT]

        def nch(t):
            return 1 if len(key_tiles(t)) <= 4 else 2

        def before(u):
            return sum(nch(units[i][0]) for i in range(u))

        with ExitStack() as own, nc.Block() as block:
            def tile(n, shape):
                return own.enter_context(nc.sbuf_tensor(f"d_{n}", shape, F32))

            p = tile("p", [P, 2, 5 * P])
            aT = tile("aT", [P, 5, P])
            stat = tile("st", [P, 2, 4])
            band = C(env, "band").rearrange("p (a b) -> p a b", a=2)

            @block.tensor
            def _(pe):
                def scores(u):
                    t, h = units[u]
                    kv, g = h // 2, h % 2
                    r = slice(64 * kv, 64 * kv + 64)
                    if u >= 2:
                        pe.wait_ge(exped.sem, u - 1)
                    for n, (k, mask) in enumerate(key_tiles(t)):
                        out = ps[:, 2 * (u % 2) + n // 4, (n % 4) * P:(n % 4 + 1) * P]
                        last = pe.matmul(out, qkT[r, g, t * P:(t + 1) * P], qkT[r, 2, k * P:(k + 1) * P],
                                         start=True, stop=mask is None)
                        if mask is not None:
                            last = pe.matmul(out, C(env, "ident"), band[:, mask, :], start=False, stop=True)
                    last.then_inc(s_mm.sem, 1)

                def value(u):
                    t, h = units[u]
                    kv = h // 2
                    kt = key_tiles(t)
                    pe.wait_ge(exped.sem, u + 1)
                    if u >= 1:
                        pe.wait_ge(t_kept.sem, before(u))
                    for c in range(nch(t)):
                        for n in range(4 * c, min(4 * c + 4, len(kt))):
                            last = pe.transpose(ps[:, 4 + c, (n % 4) * P:(n % 4 + 1) * P], p[:, u % 2, n * P:(n + 1) * P],
                                                C(env, "ident"))
                        last.then_inc(t_mm.sem, 1)
                    pe.wait_ge(t_kept.sem, before(u + 1))
                    if u >= 2:
                        pe.wait_ge(o_kept.sem, u - 1)
                    for n, (k, _) in enumerate(kt):
                        last = pe.matmul(ps[:, 6 + u % 2, 0:DH], aT[:, n, :], vD[:, k, kv * DH:(kv + 1) * DH],
                                         start=n == 0, stop=n == len(kt) - 1)
                    last.then_inc(o_mm.sem, 1)

                for u in range(NU):
                    scores(u)
                    if u >= 1:
                        value(u - 1)
                value(NU - 1)

            @block.scalar
            def _(act):
                def keep(u):
                    t, h = units[u]
                    if u >= 1:
                        act.wait_ge(o_mm.sem, u)
                    for c in range(nch(t)):
                        n = min(4, len(key_tiles(t)) - 4 * c)
                        act.wait_ge(t_mm.sem, before(u) + c + 1)
                        act.activation(aT[:, 4 * c:4 * c + n, :], ps[:, 4 + c, 0:n * P].rearrange("p (k t) -> p k t", t=P),
                                       ACT.Copy).then_inc(t_kept.sem, 1)

                for u in range(NU):
                    t, h = units[u]
                    n = len(key_tiles(t)) * P
                    st = stat[:, u % 2, :]
                    act.wait_ge(mx.sem, u + 1)
                    if u >= 2:
                        act.wait_ge(t_mm.sem, before(u - 1))
                    act.activation(p[:, u % 2, 0:n], ps[:, 2 * (u % 2):2 * (u % 2) + 2, :].rearrange("p b n -> p (b n)")[:, 0:n],
                                   ACT.Exp, bias=st[:, 0:1], scale=SCALE, accum_out=st[:, 1:2]).then_inc(exped.sem, 1)
                    act.activation(st[:, 2:3], W(env, "d_sink")[:, h:h + 1], ACT.Exp, bias=st[:, 0:1]).then_inc(sunk.sem, 1)
                    if u >= 1:
                        keep(u - 1)
                keep(NU - 1)

            @block.vector
            def _(dve):
                def maximum(u):
                    t, h = units[u]
                    n = len(key_tiles(t)) * P
                    st = stat[:, u % 2, :]
                    dve.wait_ge(s_mm.sem, u + 1)
                    dv.link(dve, dve.tensor_reduce(st[:, 0:1], ps[:, 2 * (u % 2):2 * (u % 2) + 2, :]
                                                   .rearrange("p b n -> p (b n)")[:, 0:n], AX.X, ALU.max))
                    dv.link(dve, dve.tensor_scalar(st[:, 0:1], st[:, 0:1], SCALE, W(env, "d_sink")[:, h:h + 1], ALU.mult, ALU.max))
                    dve.tensor_scalar(st[:, 0:1], st[:, 0:1], -1.0, None, ALU.mult).then_inc(mx.sem, 1)

                def finish(u):
                    t, h = units[u]
                    st = stat[:, u % 2, :]
                    dve.wait_ge(exped.sem, u + 1)
                    dve.wait_ge(sunk.sem, u + 1)
                    dv.link(dve, dve.tensor_tensor(st[:, 3:4], st[:, 1:2], st[:, 2:3], ALU.add))
                    dv.link(dve, dve.reciprocal(st[:, 3:4], st[:, 3:4]))
                    dve.wait_ge(o_mm.sem, u + 1)
                    dve.tensor_scalar(yD[:, t, h, :], ps[:, 6 + u % 2, 0:DH], st[:, 3:4], None, ALU.mult)\
                       .then_inc(o_kept.sem, 1)

                for u in range(NU):
                    maximum(u)
                    if u >= 1:
                        finish(u - 1)
                finish(NU - 1)
                dve.wait_ge(o_kept.sem, NU)

        turn_out(nc, env, yD, 6, "d", norm=False)


def stage_gates(nc, env):
    ps, signal, yT = env["ps"], env["signal"], env["yT"]
    mm, sg, made, done, last_bo = (signal(n) for n in ("g_product", "g_sigmoid", "g_made", "g_done", "g_bo"))
    jobs = [(S_BO, c, 2 + c, b) for c in range(2) for b in BLOCKS] + \
        [(S_G0 + c // 4, c % 4, c, b) for c in range(KT) for b in BLOCKS]
    NJ = len(jobs)
    with ExitStack() as own, nc.Block() as block:
        sig = own.enter_context(nc.sbuf_tensor("g_sig", [P, 2, BANK], F32))
        gate = own.enter_context(nc.sbuf_tensor("g_gate", [P, 2, BANK], F32))

        @block.sync
        def _(sp):
            load_slabs(sp, env, 15, 18)

        @block.tensor
        def _(pe):
            for n, (s, c, k, b) in enumerate(jobs):
                if n == 0 or jobs[n - 1][0] != s:
                    pe.wait_ge(env["loaded"][s].sem, 16)
                if n >= 4:
                    pe.wait_ge(made.sem, n - 3)
                proj_channels(pe, env, ps[:, n % 4, 0:b[1]], s, c * P, (c + 1) * P, *b).then_inc(mm.sem, 1)
                if n == NJ - 1 or jobs[n + 1][0] != s:
                    pe.wait_ge(mm.sem, n + 1)
                    pe.sem_inc(env["slab_used"].sem, 1)

        @block.scalar
        def _(act):
            for n, (s, c, k, b) in enumerate(jobs):
                act.wait_ge(mm.sem, n + 1)
                if n >= 2:
                    act.wait_ge(made.sem, n - 1)
                act.activation(sig[:, n % 2, 0:b[1]], ps[:, n % 4, 0:b[1]], ACT.Sigmoid).then_inc(sg.sem, 1)

        @block.vector
        def _(dve):
            for n, (s, c, k, b) in enumerate(jobs):
                dve.wait_ge(sg.sem, n + 1)
                if n >= 2:
                    dve.wait_ge(done.sem, n - 1)
                if s == S_BO:
                    ins = dve.tensor_copy(gate[:, n % 2, 0:b[1]], sig[:, n % 2, 0:b[1]])
                else:
                    ins = dve.tensor_tensor(gate[:, n % 2, 0:b[1]], ps[:, n % 4, 0:b[1]], sig[:, n % 2, 0:b[1]], ALU.mult)
                ins.then_inc(made.sem, 1)

        @block.gpsimd
        def _(pool):
            for n, (s, c, k, b) in enumerate(jobs):
                pool.wait_ge(made.sem, n + 1)
                y = yT[:, k, b[0]:b[0] + b[1]]
                pool.tensor_tensor(y, y, gate[:, n % 2, 0:b[1]], ALU.mult).then_inc(done.sem, 1)
                if s == S_BO:
                    pool.wait_ge(done.sem, n + 1)
            pool.wait_ge(done.sem, NJ)


def stage_output(nc, env):
    ps, signal, yT, dram = (env[n] for n in ("ps", "signal", "yT", "dram"))
    NB = 4
    x_in = [signal(f"res{i}_loaded") for i in range(NB)]
    x_out = [signal(f"res{i}_stored") for i in range(NB)]
    mm, gated, added = (signal(n) for n in ("o_product", "o_gated", "o_added"))
    jobs = [(n, t) for n in range(2) for t in range(NT)]
    NJ = len(jobs)

    def rows(n, t):
        cols = slice(n * 512, (n + 1) * 512)
        return dram["ctx_now"][t * P:(t + 1) * P, cols] if t < NC else dram["out"][(t - NC) * P:(t - NC + 1) * P, cols]

    with ExitStack() as own, nc.Block() as block:
        res = own.enter_context(nc.sbuf_tensor("o_res", [P, NB, 512], F32))
        prod = own.enter_context(nc.sbuf_tensor("o_prod", [P, 2, 512], F32))

        @block.sync
        def _(sp):
            for i, (n, t) in enumerate(jobs):
                if i >= NB:
                    sp.wait_ge(x_out[i % NB].sem, 16 * (i // NB))
                sp.dma_start(res[:, i % NB, :], rows(n, t)).then_inc(x_in[i % NB].sem, 16)

        @block.tensor
        def _(pe):
            for i, (n, t) in enumerate(jobs):
                if t == 0:
                    pe.wait_ge(env["loaded"][S_OUT + n].sem, 16)
                if i >= 4:
                    pe.wait_ge(gated.sem, i - 3)
                for k in range(KT):
                    last = pe.matmul(ps[:, i % 4, :], yT[:, k, t * P:(t + 1) * P], slab(env, S_OUT + n)[:, k, :],
                                     start=k == 0, stop=k == KT - 1)
                last.then_inc(mm.sem, 1)

        @block.vector
        def _(dve):
            for i, (n, t) in enumerate(jobs):
                dve.wait_ge(mm.sem, i + 1)
                if i >= 2:
                    dve.wait_ge(added.sem, i - 1)
                v = 0 if t < NC else 1
                dve.tensor_tensor(prod[:, i % 2, :], ps[:, i % 4, :], env["gate_rows"][:, v, n * 512:(n + 1) * 512], ALU.mult)\
                   .then_inc(gated.sem, 1)

        @block.gpsimd
        def _(pool):
            for i, (n, t) in enumerate(jobs):
                pool.wait_ge(gated.sem, i + 1)
                pool.wait_ge(x_in[i % NB].sem, 16 * (i // NB + 1))
                pool.tensor_tensor(res[:, i % NB, :], res[:, i % NB, :], prod[:, i % 2, :], ALU.add).then_inc(added.sem, 1)

        @block.scalar
        def _(act):
            for i, (n, t) in enumerate(jobs):
                act.wait_ge(added.sem, i + 1)
                act.dma_start(rows(n, t), res[:, i % NB, :]).then_inc(x_out[i % NB].sem, 16)
            for b in range(NB):
                act.wait_ge(x_out[b].sem, 16 * (NJ // NB))


def constants():
    c = np.zeros((P, NCST), np.float32)

    def put(name, rows=P):
        a, b = CST[name]
        return c[0:rows, a:b]

    i, j = np.arange(P)[:, None], np.arange(P)[None, :]
    put("ident")[:] = i == j
    put("neg")[:, 0:P] = np.where(j >= i, 0.0, NEG)
    put("neg")[:, P:] = np.where(j <= i, 0.0, NEG)
    put("band")[:, 0:P] = np.where(j >= i, 0.0, NEG)
    put("band")[:, P:] = np.where(j <= i, 0.0, NEG)
    pos = np.arange(SEQ)
    for name, width in (("a", 32), ("d", 64)):
        nq = width // 4
        inv = np.float32(10000.0) ** (-np.arange(nq, dtype=np.float32) / np.float32(nq))
        r = (pos // GRID_W).astype(np.float32)[:, None] * inv
        q = (pos % GRID_W).astype(np.float32)[:, None] * inv
        cos = np.ones((T, width), np.float32)
        sin = np.zeros((T, width), np.float32)
        cos[CTX:] = np.concatenate([np.cos(r), np.cos(r), np.cos(q), np.cos(q)], 1)
        sin[CTX:] = np.concatenate([-np.sin(r), np.sin(r), -np.sin(q), np.sin(q)], 1)
        put(f"cos_{name}")[:] = cos.reshape(NT, P, width).transpose(1, 0, 2).reshape(P, -1)
        put(f"sin_{name}")[:] = sin.reshape(NT, P, width).transpose(1, 0, 2).reshape(P, -1)
    sel = put("sel_row").reshape(P, 8, P)
    pair = put("sel_pair").reshape(P, 4, P)
    for way in range(2):
        for h in range(HEADS):
            sel[32 * way + h, way * HEADS + h, :] = 1.0
            pair[32 * way + h, way * 2 + h // 2, 64 * (h % 2):64 * (h % 2) + 64] = 1.0
    put("sel_row")[:] = sel.reshape(P, -1)
    put("sel_pair")[:] = pair.reshape(P, -1)
    mod = put("sel_mod")
    mod[0, 0:P] = 1.0
    mod[1, P:] = 1.0
    put("ones")[:] = 1.0
    put("diag")[:] = (np.arange(P)[:, None] // 32) == (np.arange(GW)[None, :] // DH)
    pick = np.zeros((P, 2, 3, P), np.float32)
    for n, half in enumerate((16, 8)):
        same = (i // (2 * half)) == (j // (2 * half))
        pick[:, 0, n] = same & (i % (2 * half) < half) & (j % (2 * half) >= half)
        pick[:, 1, n] = same & (i % (2 * half) >= half) & (j % (2 * half) < half)
    pick[:, 0, 2] = ((i // 8) == (j // 8)) & (i <= j)
    pick[:, 1, 2] = ((i // 8) == (j // 8)) & (i >= j)
    put("pick")[:] = pick.reshape(P, -1)
    return c


def layout(w):
    return w.reshape(KT, P, w.shape[1]).transpose(1, 0, 2).reshape(P, -1)


def column(v):
    return v.reshape(-1, P).T


def pack(inputs):
    x = {k: np.asarray(v) for k, v in inputs.items()}
    w_all, par_all = [], []
    for l in range(DEPTH):
        wi = x["w_in"][l]
        gates = wi[:, B_G:B_G + 16].reshape(D, 4, HEADS)
        gap = np.zeros((D, 32 - HEADS), np.float32)
        li = np.concatenate([gates[:, 0], gap, gates[:, 2]], 1)
        lf = np.concatenate([gates[:, 1], gap, gates[:, 3]], 1)
        take = lambda a, n: wi[:, a:a + n]
        dq = take(D0, 256).reshape(D, 2, 2, DH).transpose(0, 2, 1, 3).reshape(D, 256)
        slabs = [x["w_mod"][l][:, i * 512:(i + 1) * 512] for i in range(6)]
        slabs += [take(*B_QK), np.concatenate([take(*B_V), li, lf], 1), np.concatenate([take(*C_QK), take(*C_LR)], 1),
                  take(*C_V), take(*A_QK), take(*A_V), np.concatenate([dq, take(D0 + 256, 256)], 1), take(*B_O),
                  take(G0, 512), take(G0 + 512, 512)]
        slabs += [x["w_out"][l][:, i * 512:(i + 1) * 512] for i in range(2)]
        w_all.append(np.concatenate([layout(s) for s in slabs], 1))
        p = np.zeros((P, NPAR), np.float32)

        def put(name):
            a, b = PAR[name]
            return p[:, a:b]

        put("norm_g")[:] = column(x["norm_g"][l])
        put("b_sh")[:] = column(x["b_mod"][l][0:D])
        put("b_sc")[:] = column(x["b_mod"][l][D:2 * D])
        put("b_gt")[:] = x["b_mod"][l][None, 2 * D:]
        put("a_gain")[:] = np.concatenate([np.tile(x["a_qn"][l], 8), np.tile(x["a_kn"][l], 8)])[None]
        put("d_gain")[:] = np.concatenate([np.tile(x["d_qn"][l], 4), np.tile(x["d_kn"][l], 2)])[None]
        put("conv_w")[:] = x["b_conv_w"][l].reshape(3, 4, P).transpose(2, 1, 0).reshape(P, 12)
        put("conv_b")[:] = column(x["b_conv_b"][l])
        for way in range(2):
            put("gate_li")[32 * way:32 * way + HEADS, 0] = x["b_gate_b"][l][2 * way]
            put("gate_lf")[32 * way:32 * way + HEADS, 0] = x["b_gate_b"][l][2 * way + 1]
        put("c_bg")[:] = x["c_bg"][l].T
        for z in range(2):
            put("c_wg")[z * RANK:(z + 1) * RANK, z * P:(z + 1) * P] = x["c_wg"][l][z]
        put("out_gain")[:] = 1.0
        for k, name in ((0, "a_subln"), (2, "b_outn"), (4, "c_outn")):
            put("out_gain")[:, k:k + 2] = np.tile(x[name][l], 2)[:, None]
        put("a_lam")[:] = x["a_lam"][l].reshape(1, -1)
        put("d_sink")[:] = x["d_sink"][l][None]
        lam_init = 0.8 - 0.6 * float(np.exp(-0.3 * l))
        put("lam_init")[:] = np.array([[lam_init, 1.0 - lam_init]], np.float32)
        par_all.append(p)
    return {
        "w": np.concatenate(w_all, 0), "par": np.concatenate(par_all, 0), "cst": constants(),
        "tok": np.concatenate([x["ctx"][0], x["x"][0]], 0),
        "c": np.stack([column(x["c_ctx"]), column(x["c"][0])], 2).reshape(P, 2 * KT),
    }


def kernel(**inputs):
    import concourse.bacc as bacc
    from concourse.bass_utils import run_bass_kernel_spmd

    nc = bacc.Bacc("TRN2", target_bir_lowering=False, num_devices=1)
    arrays = {f"in_{k}": np.ascontiguousarray(v) for k, v in pack(inputs).items()}
    dram = {k[3:]: nc.dram_tensor(k, v.shape, mybir.dt.from_np(v.dtype), kind="ExternalInput").ap()
            for k, v in arrays.items()}
    dram["ctx_now"] = nc.dram_tensor("ctx_now", (CTX, D), F32, kind="Internal").ap()
    dram["out"] = nc.dram_tensor("latents", (SEQ, D), F32, kind="ExternalOutput").ap()
    layer_program(nc, dram)
    r = run_bass_kernel_spmd(nc, [arrays], core_ids=[0])
    return r.results[0]["latents"].reshape(1, SEQ, D)
```

```python
from contextlib import ExitStack

import numpy as np

import concourse.bass as bass
from concourse import mybir

F32 = mybir.dt.float32
F32R = mybir.dt.float32r
ALU = mybir.AluOpType
ACT = mybir.ActivationFunctionType
AX = mybir.AxisListType

P = 128
DEPTH = 2
D = 1024
KT = D // P
CTX = 256
SEQ = 1024
T = CTX + SEQ
NT = T // P
NC = CTX // P
GRID_W = 64
HEADS = 4
DH = 64
GW = HEADS * DH
RANK = 16
TAU = 16.0
EPS = 1e-6
NEG = -1e30
LA_MIN = -19.0
BANK = 512
ROWS = 36
BLOCKS = [(0, 512), (512, 512), (1024, 256)]

A0, B0, C0, D0, G0 = 0, 768, 1808, 2352, 2864
A_QK, A_V = (A0, 512), (A0 + 512, 256)
B_QK, B_V, B_G, B_O = (B0, 512), (B0 + 512, 256), B0 + 768, (B0 + 784, 256)
C_QK, C_V, C_LR = (C0, 256), (C0 + 256, 256), (C0 + 512, 32)

SLAB_W = [512] * 6 + [512, 328, 288, 256, 512, 256, 512, 256, 512, 512] + [512] * 2
SLAB_AT = [sum(SLAB_W[:i]) * KT for i in range(len(SLAB_W) + 1)]
(S_BQK, S_BV, S_CQK, S_CV, S_AQK, S_AV, S_D, S_BO, S_G0, S_G1) = range(6, 16)
S_OUT = 16
NSLAB = len(SLAB_W)
RING = 2

PAR = {}
_at = 0
for _n, _w in [("norm_g", KT), ("b_sh", KT), ("b_sc", KT), ("b_gt", D), ("a_gain", 512), ("d_gain", 384),
               ("conv_w", 12), ("conv_b", 4), ("gate_li", 1), ("gate_lf", 1), ("c_bg", 2), ("c_wg", 256),
               ("out_gain", KT), ("a_lam", 128), ("d_sink", 4), ("lam_init", 2)]:
    PAR[_n] = (_at, _at + _w)
    _at += _w
NPAR = _at

CST = {}
_at = 0
for _n, _w in [("ident", P), ("neg", 2 * P), ("band", 2 * P), ("cos_a", NT * 32), ("sin_a", NT * 32),
               ("cos_d", NT * 64), ("sin_d", NT * 64), ("sel_row", 8 * P), ("sel_pair", 4 * P),
               ("sel_mod", 2 * P), ("ones", P), ("diag", GW), ("pick", 6 * P)]:
    CST[_n] = (_at, _at + _w)
    _at += _w
NCST = _at


class Signal:

    def __init__(self, sem):
        self.sem, self.n = sem, 0

    def mark(self, ins, by=1):
        ins.then_inc(self.sem, by)
        self.n += by
        return self.n

    def link(self, eng, ins):
        self.mark(ins)
        eng.wait_ge(self.sem, self.n)


def layer_program(nc, dram):
    ctx = ExitStack()
    with ctx:
        def keep(name, shape, dt=F32):
            return ctx.enter_context(nc.sbuf_tensor(name, shape, dt))

        def signal(name):
            s = stage_ctx[-1].enter_context(nc.semaphore(name, num=first_free + len(stage_sems)))
            stage_sems.append(s)
            return Signal(s)

        stage_ctx, stage_sems = [], []
        ps = ctx.enter_context(nc.psum_tensor("ps", [P, 8, BANK], F32))
        hT = keep("hT", [P, KT, T])
        yT = keep("yT", [P, KT, T])
        ring = keep("ring", [P, RING, KT * 512])
        gate_rows = keep("gate_rows", [P, 2, D])
        par = keep("par", [P, NPAR])
        cst = keep("cst", [P, NCST])
        csil = keep("csil", [P, KT, 2])
        setup_sem = [Signal(ctx.enter_context(nc.semaphore(n))) for n in ("const_loaded", "setup_act", "setup_dve")]

        loaded = [Signal(ctx.enter_context(nc.semaphore(f"slab{i}_loaded"))) for i in range(NSLAB)]
        slab_used = Signal(ctx.enter_context(nc.semaphore("slab_used")))
        first_free = slab_used.sem.num + 1
        env = dict(nc=nc, ps=ps, hT=hT, yT=yT, ring=ring, gate_rows=gate_rows, par=par, cst=cst,
                   csil=csil, mod_cols=keep("mod_cols", [P, 2, KT, 2]), loaded=loaded, slab_used=slab_used,
                   signal=signal, dram=dram)
        setup(nc, env, setup_sem)
        with nc.Fori(0, DEPTH) as layer:
            env["layer"] = layer
            for stage in (stage_modulation, stage_norm, stage_mlstm, stage_gla, stage_diff_attention,
                          stage_window_attention, stage_gates, stage_output):
                with ExitStack() as own:
                    stage_ctx.append(own)
                    stage(nc, env)
                    first = loaded[0].sem.num if stage is stage_output else first_free
                    nc.all_engine_barrier(sems_to_clear=range(first, first_free + len(stage_sems)))
                stage_sems.clear()


def C(env, name, rows=P):
    a, b = CST[name]
    return env["cst"][0:rows, a:b]


def W(env, name, rows=P):
    a, b = PAR[name]
    return env["par"][0:rows, a:b]


def slab(env, i):
    w = SLAB_W[i]
    return env["ring"][:, i % RING, 0:KT * w].rearrange("p (k n) -> p k n", k=KT)


def load_slabs(sp, env, first, last):
    for i in range(first, last):
        if i >= RING:
            sp.wait_ge(env["slab_used"].sem, i - RING + 1)
        src = env["dram"]["w"][bass.ds(env["layer"] * P, P), SLAB_AT[i]:SLAB_AT[i + 1]]
        sp.dma_start(env["ring"][:, i % RING, 0:KT * SLAB_W[i]], src).then_inc(env["loaded"][i].sem, 16)


def rsqrt_newton(dve, sig, y, x, t):
    sig.link(dve, dve.tensor_tensor(t, y, y, ALU.mult))
    sig.link(dve, dve.tensor_tensor(t, t, x, ALU.mult))
    sig.link(dve, dve.tensor_scalar(t, t, -0.5, 1.5, ALU.mult, ALU.add))
    sig.link(dve, dve.tensor_tensor(y, y, t, ALU.mult))


def setup(nc, env, sems):
    dram = env["dram"]
    const_loaded, act_done, dve_done = sems
    with ExitStack() as own, nc.Block() as block:
        craw = own.enter_context(nc.sbuf_tensor("craw", [P, KT, 2], F32))
        csig = own.enter_context(nc.sbuf_tensor("csig", [P, KT, 2], F32))

        @block.sync
        def _(sp):
            sp.dma_start(env["cst"][:, :], dram["cst"][:, :]).then_inc(const_loaded.sem, 16)
            sp.dma_start(craw[:, :, :], dram["c"].rearrange("p (k c) -> p k c", k=KT)).then_inc(const_loaded.sem, 16)
            sp.dma_start(dram["ctx_now"][:, :], dram["tok"][0:CTX, :]).then_inc(const_loaded.sem, 16)
            sp.dma_start(dram["out"][:, :], dram["tok"][CTX:T, :]).then_inc(const_loaded.sem, 16)
            sp.wait_ge(const_loaded.sem, 64)

        @block.scalar
        def _(act):
            act.wait_ge(const_loaded.sem, 64)
            act.activation(csig[:, :, :], craw[:, :, :], ACT.Sigmoid).then_inc(act_done.sem, 1)

        @block.vector
        def _(dve):
            dve.wait_ge(act_done.sem, 1)
            dve.tensor_tensor(env["csil"][:, :, :], craw[:, :, :], csig[:, :, :], ALU.mult)\
               .then_inc(dve_done.sem, 1)
            dve.wait_ge(dve_done.sem, 1)


def stage_modulation(nc, env):
    ps, signal = env["ps"], env["signal"]
    par_loaded, mm, ev, tr, dv, gate_mm, gate_ev = (
        signal(n) for n in ("par_loaded", "mod_product", "mod_rows", "mod_turned", "mod_dve", "gate_spread", "gate_kept"))
    own = ExitStack()
    mod_cols = env["mod_cols"]
    with own, nc.Block() as block:
        rows = own.enter_context(nc.sbuf_tensor("mod_row", [2, 3 * D], F32))

        @block.sync
        def _(sp):
            sp.dma_start(env["par"][:, :], env["dram"]["par"][bass.ds(env["layer"] * P, P), :])\
              .then_inc(par_loaded.sem, 16)
            load_slabs(sp, env, 0, 8)
            sp.wait_ge(par_loaded.sem, 16)

        @block.tensor
        def _(pe):
            for s in range(6):
                pe.wait_ge(env["loaded"][s].sem, 16)
                if s >= 2:
                    pe.wait_ge(ev.sem, s - 1)
                for k in range(KT):
                    last = pe.matmul(ps[0:2, s % 2, :], env["csil"][:, k, :], slab(env, s)[:, k, :],
                                     start=k == 0, stop=k == KT - 1)
                last.then_inc(mm.sem, 1)
                pe.wait_ge(mm.sem, s + 1)
                pe.sem_inc(env["slab_used"].sem, 1)
            pe.wait_ge(ev.sem, 4)
            for i in range(2 * KT):
                last = pe.transpose(ps[:, 2, 2 * i:2 * i + 2], rows[:, i * P:(i + 1) * P], C(env, "ident")[0:2, 0:2])
            last.then_inc(tr.sem, 1)
            pe.wait_ge(dv.sem, 1)
            sel = C(env, "sel_mod", 2).rearrange("p (a b) -> p a b", a=2)
            for v in range(2):
                for n in range(2):
                    last = pe.matmul(ps[:, 3 + 2 * v + n, :], sel[:, v, :], rows[:, 2 * D + n * 512:2 * D + (n + 1) * 512],
                                     start=True, stop=True)
                    last.then_inc(gate_mm.sem, 1)

        @block.scalar
        def _(act):
            for s in range(6):
                act.wait_ge(mm.sem, s + 1)
                act.activation(rows[:, s * 512:(s + 1) * 512], ps[0:2, s % 2, :], ACT.Copy).then_inc(ev.sem, 1)
            for i in range(4):
                act.wait_ge(gate_mm.sem, i + 1)
                act.activation(env["gate_rows"][:, i // 2, (i % 2) * 512:(i % 2 + 1) * 512], ps[:, 3 + i, :], ACT.Copy)\
                   .then_inc(gate_ev.sem, 1)
            act.wait_ge(gate_ev.sem, 4)

        @block.vector
        def _(dve):
            dve.wait_ge(par_loaded.sem, 16)
            dve.wait_ge(ev.sem, 6)
            dv.mark(dve.tensor_tensor(rows[:, 2 * D:], rows[:, 2 * D:], W(env, "b_gt", 2), ALU.add))
            dve.wait_ge(tr.sem, 1)
            turned = ps[:, 2, 0:4 * KT].rearrange("p (s k v) -> p s k v", s=2, k=KT)
            for s, b in ((0, "b_sh"), (1, "b_sc")):
                dv.link(dve, dve.tensor_tensor(mod_cols[:, s, :, :], turned[:, s, :, :],
                                               W(env, b).unsqueeze(2).broadcast_to([P, KT, 2]), ALU.add))
            dv.link(dve, dve.tensor_scalar(mod_cols[:, 1, :, :], mod_cols[:, 1, :, :], 1.0, None, ALU.add))
            dv.link(dve, dve.tensor_tensor(mod_cols[:, 1, :, :], mod_cols[:, 1, :, :],
                                           W(env, "norm_g").unsqueeze(2).broadcast_to([P, KT, 2]), ALU.mult))
            dv.link(dve, dve.tensor_scalar(W(env, "out_gain")[:, 0:2], W(env, "out_gain")[:, 0:2],
                                           W(env, "lam_init")[:, 1:2], None, ALU.mult))


def stage_norm(nc, env):
    ps, signal, hT = env["ps"], env["signal"], env["hT"]
    rowsx = env["yT"][:, :, :].rearrange("p k t -> p (k t)").rearrange("p (t d) -> p t d", t=NT)
    x_loaded = [signal(f"x{t}_loaded") for t in range(NT)]
    squares, ms_ready, root, rstd_ready, scaled_a, scaled_d, turned, kept_a, kept_d, dv = (
        signal(n) for n in ("x_squares", "x_mean", "x_root", "x_rstd", "x_scaled_act", "x_scaled_dve",
                            "x_turned", "h_kept_act", "h_kept_dve", "norm_dve"))
    mod_cols = env["mod_cols"]
    groups = [(0, 0, 2), (1, 2, 4), (1, 6, 4)]
    jobs = [(k, g) for g in groups for k in range(KT)]
    own = ExitStack()
    with own, nc.Block() as block:
        junk = hT[:, :, :].rearrange("p k t -> p (k t)").rearrange("p (t d) -> p t d", t=NT)
        small = own.enter_context(nc.sbuf_tensor("x_stats", [P, 4, NT], F32))
        ss, ms, rstd, tmp = (small[:, i, :] for i in range(4))

        @block.sync
        def _(sp):
            for t in range(NT):
                src = env["dram"]["ctx_now"][t * P:(t + 1) * P, :] if t < NC else \
                    env["dram"]["out"][(t - NC) * P:(t - NC + 1) * P, :]
                sp.dma_start(rowsx[:, t, :], src).then_inc(x_loaded[t].sem, 16)

        @block.scalar
        def _(act):
            for t in range(NT):
                act.wait_ge(x_loaded[t].sem, 16)
                act.activation(junk[:, t, :], rowsx[:, t, :], ACT.Square, accum_out=ss[:, t:t + 1]).then_inc(squares.sem, 1)
            act.wait_ge(ms_ready.sem, 1)
            root.link(act, act.activation(rstd, ms, ACT.Ln))
            root.mark(act.activation(rstd, rstd, ACT.Exp, scale=-0.5))
            act.wait_ge(rstd_ready.sem, 1)
            for t in range(0, NT, 2):
                act.activation(rowsx[:, t, :], rowsx[:, t, :], ACT.Copy, scale=rstd[:, t:t + 1]).then_inc(scaled_a.sem, 1)
            for n, (k, (v, t0, m)) in enumerate(jobs):
                if n % 2 == 0:
                    act.wait_ge(turned.sem, n + 1)
                    act.activation(hT[:, k, t0 * P:(t0 + m) * P], ps[:, n % 4, 0:m * P], ACT.Identity,
                                   bias=mod_cols[:, 0, k, v:v + 1], scale=mod_cols[:, 1, k, v:v + 1]).then_inc(kept_a.sem, 1)

        @block.vector
        def _(dve):
            dve.wait_ge(squares.sem, NT)
            dve.tensor_scalar(ms, ss, 1.0 / D, EPS, ALU.mult, ALU.add).then_inc(ms_ready.sem, 1)
            dve.wait_ge(root.sem, 2)
            rsqrt_newton(dve, dv, rstd, ms, tmp)
            dve.sem_inc(rstd_ready.sem, 1)
            for t in range(1, NT, 2):
                dve.tensor_scalar(rowsx[:, t, :], rowsx[:, t, :], rstd[:, t:t + 1], None, ALU.mult)\
                   .then_inc(scaled_d.sem, 1)
            for n, (k, (v, t0, m)) in enumerate(jobs):
                if n % 2 == 1:
                    dve.wait_ge(turned.sem, n + 1)
                    dve.tensor_scalar(hT[:, k, t0 * P:(t0 + m) * P], ps[:, n % 4, 0:m * P],
                                      mod_cols[:, 1, k, v:v + 1], mod_cols[:, 0, k, v:v + 1], ALU.mult, ALU.add)\
                       .then_inc(kept_d.sem, 1)

        @block.tensor
        def _(pe):
            for n, (k, (v, t0, m)) in enumerate(jobs):
                pe.wait_ge(scaled_a.sem, (t0 + m) // 2)
                pe.wait_ge(scaled_d.sem, (t0 + m) // 2)
                if n >= 4:
                    pe.wait_ge((kept_a if n % 2 == 0 else kept_d).sem, (n - 4) // 2 + 1)
                for t in range(t0, t0 + m):
                    last = pe.transpose(ps[:, n % 4, (t - t0) * P:(t - t0 + 1) * P],
                                        rowsx[:, t, k * P:(k + 1) * P], C(env, "ident"))
                last.then_inc(turned.sem, 1)


def proj_channels(pe, env, out, s, c0, c1, t0, n):
    for k in range(KT):
        last = pe.matmul(out, slab(env, s)[:, k, c0:c1], env["hT"][:, k, t0:t0 + n], start=k == 0, stop=k == KT - 1)
    return last


def proj_tokens(pe, env, out, s, c0, c1, t):
    for k in range(KT):
        last = pe.matmul(out, env["hT"][:, k, t * P:(t + 1) * P], slab(env, s)[:, k, c0:c1],
                         start=k == 0, stop=k == KT - 1)
    return last


def scan_order(way):
    return list(range(NT)) if way == 0 else list(range(NC - 1, -1, -1)) + list(range(NT - 1, NC - 1, -1))


UNITS = [(way, i, scan_order(way)[i]) for i in range(NT) for way in range(2)]


def second_visit(u):
    return any(UNITS[n][2] == UNITS[u][2] for n in range(u))


def stage_mlstm(nc, env):
    ps, signal, hT, yT, ring = (env[n] for n in ("ps", "signal", "hT", "yT", "ring"))
    loaded, slab_used = env["loaded"], env["slab_used"]
    outer = ExitStack()
    with outer:
        v1 = outer.enter_context(nc.sbuf_tensor("b_v", [P, NT, HEADS, DH + 1], F32))
        qkT = outer.enter_context(nc.sbuf_tensor("b_qkT", [P, 4, T], F32))
        row_b = outer.enter_context(nc.sbuf_tensor("b_row_b", [ROWS, T], F32))[:, :]
        cols = outer.enter_context(nc.sbuf_tensor("b_cols", [P, NT, 4, ROWS], F32))
        ends = outer.enter_context(nc.sbuf_tensor("b_ends", [ROWS, 4, NT], F32))
        decay = outer.enter_context(nc.sbuf_tensor("b_decay", [P, 4, NT], F32))
        conv_in = yT[:, 4:8, :]
        ktm = yT[:, 4:6, :].rearrange("p a t -> p (a t)").rearrange("p (t c) -> p t c", t=NT)
        hB = yT[:, 0:2, :].rearrange("p a t -> p (a t)").rearrange("p (t h d) -> p t h d", t=NT, h=HEADS)
        row_e = yT[0:ROWS, 2, :]
        q_of = [yT[:, 6 + h // 2, :] if h % 2 else qkT[:, h // 2, :] for h in range(HEADS)]

        mm, ev, act_s, act_l, dv, conv_ready, silu_ready, logsig, rows_ready, turned, turned_kept, dec_ready, v_ones = (
            signal(n) for n in ("b_product", "b_kept", "b_sigmoid", "b_logs", "b_dve", "b_conv", "b_silu", "b_logsig_in",
                                "b_rows", "b_turned", "b_turned_kept", "b_dec", "b_ones"))
        jobs = [("qk", c, b) for c in range(4) for b in BLOCKS] + [(g, 0, b) for g in ("li", "lf") for b in BLOCKS] + \
            [("v", t, None) for t in range(NT)]
        n_qk, n_gate = 12, 6

        with ExitStack() as own, nc.Block() as block:
            row_a, row_c, row_d = (own.enter_context(nc.sbuf_tensor(f"b_row_{i}", [ROWS, T], F32))[:, :] for i in "acd")
            chunked = [r.rearrange("p (c t) -> p c t", c=NT) for r in (row_a, row_b, row_c, row_d, row_e)]

            @block.sync
            def _(sp):
                load_slabs(sp, env, 8, 10)

            @block.gpsimd
            def _(pool):
                pool.memset(v1[:, :, :, DH:DH + 1], 1.0).then_inc(v_ones.sem, 1)
                pool.wait_ge(v_ones.sem, 1)

            @block.tensor
            def _(pe):
                for n, (kind, c, b) in enumerate(jobs):
                    if n == 0:
                        pe.wait_ge(loaded[S_BQK].sem, 16)
                    if n == n_qk:
                        pe.wait_ge(loaded[S_BV].sem, 16)
                    if n >= 4:
                        pe.wait_ge(ev.sem, n - 3)
                    if kind == "qk":
                        last = proj_channels(pe, env, ps[:, n % 4, 0:b[1]], S_BQK, c * P, (c + 1) * P, *b)
                    elif kind == "v":
                        last = proj_tokens(pe, env, ps[:, n % 4, 0:GW], S_BV, 0, GW, c)
                    else:
                        c0 = GW + (0 if kind == "li" else ROWS)
                        last = proj_channels(pe, env, ps[0:ROWS, n % 4, 0:b[1]], S_BV, c0, c0 + ROWS, *b)
                    last.then_inc(mm.sem, 1)
                    if n in (n_qk - 1, len(jobs) - 1):
                        pe.wait_ge(mm.sem, n + 1)
                        pe.sem_inc(slab_used.sem, 1)
                pe.wait_ge(silu_ready.sem, 6)
                pe.wait_ge(ev.sem, len(jobs))
                for t in range(NT):
                    if t >= 4:
                        pe.wait_ge(turned_kept.sem, t - 3)
                    for c in range(2):
                        last = pe.transpose(ps[:, t % 4, c * P:(c + 1) * P], qkT[:, 2 + c, t * P:(t + 1) * P], C(env, "ident"))
                    last.then_inc(turned.sem, 1)
                pe.wait_ge(rows_ready.sem, 1)
                for t in range(NT):
                    for q, r in enumerate((row_a, row_c, row_d, row_e)):
                        at = (t % 3) * 4 * ROWS + q * ROWS
                        last = pe.transpose(ps[:, 4 + t // 3, at:at + ROWS], r[:, t * P:(t + 1) * P],
                                            C(env, "ident")[0:ROWS, 0:ROWS])
                last.then_inc(turned.sem, 1)
                pe.wait_ge(dec_ready.sem, 1)
                pe.wait_ge(turned_kept.sem, NT)
                sel = C(env, "sel_pair", ROWS).rearrange("p (a b) -> p a b", a=4)
                for i in range(4):
                    last = pe.matmul(ps[:, 0, i * NT:(i + 1) * NT], sel[:, i, :], ends[:, 3, :], start=True, stop=True)
                last.then_inc(turned.sem, 1)

            @block.scalar
            def _(act):
                for n, (kind, c, b) in enumerate(jobs):
                    act.wait_ge(mm.sem, n + 1)
                    if kind == "qk":
                        ins = act.activation(conv_in[:, c, b[0]:b[0] + b[1]], ps[:, n % 4, 0:b[1]], ACT.Copy)
                    elif kind == "v":
                        ins = act.activation(v1[:, c, :, 0:DH], ps[:, n % 4, 0:GW].rearrange("p (h d) -> p h d", h=HEADS),
                                             ACT.Copy)
                    else:
                        ins = act.activation((row_a if kind == "li" else row_b)[:, b[0]:b[0] + b[1]],
                                             ps[0:ROWS, n % 4, 0:b[1]], ACT.Identity, bias=W(env, "gate_" + kind, ROWS))
                    ins.then_inc(ev.sem, 1)
                    if n == n_qk + n_gate - 1:
                        act.wait_ge(ev.sem, n_qk + n_gate)
                        act_l.link(act, act.activation(row_c, row_b, ACT.Abs))
                        act_l.link(act, act.activation(row_c, row_c, ACT.Exp, scale=-1.0))
                        act_l.mark(act.activation(row_c, row_c, ACT.Ln, bias=1.0))
                        for c in range(4):
                            act.wait_ge(conv_ready.sem, c + 1)
                            act.activation(conv_in[:, c, :], qkT[:, c, :], ACT.Sigmoid).then_inc(act_s.sem, 1)
                for t in range(NT):
                    act.wait_ge(turned.sem, t + 1)
                    act.activation(ktm[:, t, :], ps[:, t % 4, 0:GW], ACT.Copy).then_inc(turned_kept.sem, 1)
                act.wait_ge(rows_ready.sem, 1)
                act.activation(ends[:, 3, :], ends[:, 3, :], ACT.Exp).then_inc(dec_ready.sem, 1)
                act.wait_ge(turned.sem, NT + 1)
                for b in range(4):
                    m = min(3, NT - 3 * b)
                    src = ps[:, 4 + b, 0:m * 4 * ROWS].rearrange("p (t q r) -> p t q r", t=m, q=4)
                    for q, (f, scale) in enumerate(((ACT.Copy, 1.0), (ACT.Exp, 1.0), (ACT.Exp, -1.0), (ACT.Exp, 1.0))):
                        act.activation(cols[:, 3 * b:3 * b + m, q, :], src[:, :, q, :], f, scale=scale)\
                           .then_inc(turned_kept.sem, 1)
                act.wait_ge(turned.sem, NT + 2)
                act.activation(decay[:, :, :], ps[:, 0, 0:4 * NT].rearrange("p (a b) -> p a b", a=4), ACT.Copy)\
                   .then_inc(turned_kept.sem, 1)
                act.wait_ge(turned_kept.sem, NT + 17)

            @block.vector
            def _(dve):
                cw = W(env, "conv_w").rearrange("p (c j) -> p c j", c=4)
                for c in range(4):
                    dve.wait_ge(ev.sem, 3 * (c + 1))
                    y, x = qkT[:, c, :], conv_in[:, c, :]
                    dv.link(dve, dve.tensor_scalar(y, x, cw[:, c, 1:2], W(env, "conv_b")[:, c:c + 1], ALU.mult, ALU.add))
                    for a, b in ((0, CTX), (CTX, T)):
                        dv.link(dve, dve.scalar_tensor_tensor(out=y[:, a + 1:b], in0=x[:, a:b - 1], scalar=cw[:, c, 0:1],
                                                              in1=y[:, a + 1:b], op0=ALU.mult, op1=ALU.add))
                        ins = dve.scalar_tensor_tensor(out=y[:, a:b - 1], in0=x[:, a + 1:b], scalar=cw[:, c, 2:3],
                                                       in1=y[:, a:b - 1], op0=ALU.mult, op1=ALU.add)
                        dv.link(dve, ins)
                    dve.sem_inc(conv_ready.sem, 1)
                dve.wait_ge(act_l.sem, 3)
                dv.link(dve, dve.scalar_tensor_tensor(out=row_b, in0=row_b, scalar=0.0, in1=row_c,
                                                      op0=ALU.min, op1=ALU.subtract))
                ones = C(env, "ones")
                dv.mark(dve.memset(row_d, 0.0))
                dv.link(dve, dve.memset(ends[:, :, :], 0.0))
                for t in range(NT):
                    a, b = t * P, (t + 1) * P
                    dv.mark(dve.tensor_tensor_scan(row_c[0:HEADS, a:b], ones[0:HEADS, :], row_b[0:HEADS, a:b],
                                                   0.0, ALU.mult, ALU.add))
                    dv.mark(dve.tensor_tensor_scan(row_c[32:ROWS, a:b][:, ::-1], ones[32:ROWS, :],
                                                   row_b[32:ROWS, a:b][:, ::-1], 0.0, ALU.mult, ALU.add))
                dv.mark(dve.tensor_tensor_scan(row_d[0:HEADS, :], row_b[0:HEADS, :], row_a[0:HEADS, :], 0.0,
                                               ALU.add, ALU.max))
                dv.link(dve, dve.tensor_tensor_scan(row_d[32:ROWS, 0:CTX][:, ::-1], row_b[32:ROWS, 0:CTX][:, ::-1],
                                                    row_a[32:ROWS, 0:CTX][:, ::-1], 0.0, ALU.add, ALU.max))
                dv.link(dve, dve.tensor_tensor_scan(row_d[32:ROWS, CTX:T][:, ::-1], row_b[32:ROWS, CTX:T][:, ::-1],
                                                    row_a[32:ROWS, CTX:T][:, ::-1], row_d[32:ROWS, 0:1], ALU.add, ALU.max))
                cc, cd = chunked[2], chunked[3]
                for r, at in ((slice(0, HEADS), P - 1), (slice(32, ROWS), 0)):
                    dv.mark(dve.tensor_copy(ends[r, 0, :].unsqueeze(2), cc[r, :, at:at + 1]))
                    dv.link(dve, dve.tensor_copy(ends[r, 1, :].unsqueeze(2), cd[r, :, at:at + 1]))
                dv.mark(dve.tensor_copy(ends[0:HEADS, 2, 1:NT], ends[0:HEADS, 1, 0:NT - 1]))
                dv.mark(dve.tensor_copy(ends[32:ROWS, 2, 0:1], ends[32:ROWS, 1, 1:2]))
                dv.mark(dve.tensor_copy(ends[32:ROWS, 2, NT - 1:NT], ends[32:ROWS, 1, 0:1]))
                dv.link(dve, dve.tensor_copy(ends[32:ROWS, 2, NC:NT - 1], ends[32:ROWS, 1, NC + 1:NT]))
                dv.link(dve, dve.tensor_tensor(ends[:, 0, :], ends[:, 0, :], ends[:, 1, :], ALU.subtract))
                dv.link(dve, dve.tensor_tensor(ends[:, 3, :], ends[:, 0, :], ends[:, 2, :], ALU.add))
                wide = lambda i: ends[:, i, :].unsqueeze(2).broadcast_to([ROWS, NT, P])
                dv.link(dve, dve.tensor_tensor(row_a, row_a, row_c, ALU.subtract))
                dv.link(dve, dve.tensor_tensor(row_b, row_c, row_d, ALU.subtract))
                dv.mark(dve.tensor_tensor(chunked[2], chunked[1], wide(2), ALU.add))
                dv.link(dve, dve.tensor_tensor(chunked[4], chunked[0], wide(0), ALU.add))
                dve.sem_inc(rows_ready.sem, 1)
                for c in (2, 3):
                    dve.wait_ge(act_s.sem, c + 1)
                    dve.scalar_tensor_tensor(out=qkT[:, c, :], in0=qkT[:, c, :], scalar=DH ** -0.5,
                                             in1=conv_in[:, c, :], op0=ALU.mult, op1=ALU.mult).then_inc(silu_ready.sem, 1)
                dve.wait_ge(silu_ready.sem, 2)
                for c in range(2):
                    dve.memset(yT[0:64, 6 + c, :], 0.0)
                    dv.mark(dve.tensor_tensor(yT[64:P, 6 + c, :], qkT[64:P, c, :], conv_in[64:P, c, :], ALU.mult))
                    dve.tensor_tensor(qkT[0:64, c, :], qkT[0:64, c, :], conv_in[0:64, c, :], ALU.mult).then_inc(silu_ready.sem, 1)
                    dve.wait_ge(dv.sem, dv.n)
                    dve.memset(qkT[64:P, c, :], 0.0).then_inc(silu_ready.sem, 1)
                dve.wait_ge(silu_ready.sem, 6)

        (d_mm, s_mm, dm_ready, w_ready, sw_ready, u_mm, intra_mm, vw_ready, fin, dv2, finished, zeroed) = (
            signal(n) for n in ("b_logs_mm", "b_scores_mm", "b_logw", "b_weight", "b_weighted", "b_new_mm",
                                "b_intra_mm", "b_vw", "b_psum_read", "b_dve2", "b_state", "b_zeroed"))
        with ExitStack() as own, nc.Block() as block:
            def tile(name, shape):
                return own.enter_context(nc.sbuf_tensor(name, shape, F32))

            logw = tile("b_logw", [P, HEADS, P])
            wgt = tile("b_wgt", [P, HEADS, P])
            sw = tile("b_sw", [P, HEADS, P])
            vw = tile("b_vw", [P, 2, HEADS, DH + 1])
            state = tile("b_state", [P, 2, 2, DH + 1])
            tmp = tile("b_tmp", [P, HEADS, DH + 1])
            num = tile("b_num", [P, HEADS, DH + 1])
            den = tile("b_den", [P, HEADS])
            neg = C(env, "neg").rearrange("p (a b) -> p a b", a=2)
            sel = C(env, "sel_row", ROWS).rearrange("p (a b) -> p a b", a=8)
            NU = len(UNITS)

            def col(j, q, way):
                return cols[:, j, q, 32 * way:32 * way + HEADS]

            @block.gpsimd
            def _(pool):
                for u, (way, i, j) in enumerate(UNITS):
                    if u >= 2:
                        pool.wait_ge(u_mm.sem, u - 1)
                    pool.tensor_tensor(vw[:, u % 2, :, :], v1[:, j, :, :],
                                       col(j, 3, way).unsqueeze(2).broadcast_to([P, HEADS, DH + 1]), ALU.mult)\
                        .then_inc(vw_ready.sem, 1)

            @block.tensor
            def _(pe):
                def logs(u):
                    way, i, j = UNITS[u]
                    if u >= 2:
                        pe.wait_ge(dm_ready.sem, HEADS * (u - 1))
                    for h in range(HEADS):
                        last = pe.matmul(ps[:, u % 2, h * P:(h + 1) * P], sel[:, way * HEADS + h, :],
                                         row_b[:, j * P:(j + 1) * P], start=True, stop=True)
                    last.then_inc(d_mm.sem, 1)

                def scores(u):
                    j = UNITS[u][2]
                    t0, t1 = j * P, (j + 1) * P
                    if u >= 2:
                        pe.wait_ge(sw_ready.sem, u - 1)
                    for h in range(HEADS):
                        last = pe.matmul(ps[:, 2 + u % 2, h * P:(h + 1) * P], qkT[:, 2 + h // 2, t0:t1], q_of[h][:, t0:t1],
                                         start=True, stop=True)
                    last.then_inc(s_mm.sem, 1)

                logs(0)
                scores(0)
                for u, (way, i, j) in enumerate(UNITS):
                    t0, t1 = j * P, (j + 1) * P
                    if u + 1 < NU:
                        logs(u + 1)
                        scores(u + 1)
                    if u == 0:
                        pe.wait_ge(zeroed.sem, 1)
                    if u >= 2:
                        pe.wait_ge(finished.sem, u - 1)
                    for h in range(HEADS):
                        pe.matmul(ps[:, 5 + 2 * (u % 2), h * (DH + 1):(h + 1) * (DH + 1)], q_of[h][:, t0:t1],
                                  state[:, way, h // 2, :], start=True, stop=True)
                    pe.wait_ge(vw_ready.sem, u + 1)
                    for h in range(HEADS):
                        r = slice(64 * (h % 2), 64 * (h % 2) + 64)
                        a = (HEADS + h // 2) * (DH + 1)
                        last = pe.matmul(ps[r, 5 + 2 * (u % 2), a:a + DH + 1], ktm[:, j, h * DH:(h + 1) * DH],
                                         vw[:, u % 2, h, :], start=True, stop=True)
                    last.then_inc(u_mm.sem, 1)
                    pe.wait_ge(sw_ready.sem, u + 1)
                    for h in range(HEADS):
                        last = pe.matmul(ps[:, 4 + 2 * (u % 2), h * (DH + 1):(h + 1) * (DH + 1)], sw[:, h, :], v1[:, j, h, :],
                                         start=True, stop=True)
                    last.then_inc(intra_mm.sem, 1)

            @block.scalar
            def _(act):
                for u in range(NU):
                    act.wait_ge(dm_ready.sem, HEADS * (u + 1))
                    if u >= 1:
                        act.wait_ge(sw_ready.sem, u)
                    act.activation(wgt[:, :, :], logw[:, :, :], ACT.Exp).then_inc(w_ready.sem, 1)

            @block.vector
            def _(dve):
                dve.memset(state[:, :, :, :], 0.0).then_inc(zeroed.sem, 1)
                dve.wait_ge(zeroed.sem, 1)

                def finish(u):
                    way, i, j = UNITS[u]
                    intra, inter, fresh = (
                        ps[:, bank + 2 * (u % 2), a * (DH + 1):b * (DH + 1)].rearrange("p (h d) -> p h d", h=b - a)
                        for bank, a, b in ((4, 0, HEADS), (5, 0, HEADS), (5, HEADS, HEADS + 2)))
                    dve.wait_ge(u_mm.sem, u + 1)
                    dv2.mark(dve.tensor_tensor(tmp[:, :, :], inter, col(j, 1, way).unsqueeze(2).broadcast_to([P, HEADS, DH + 1]),
                                               ALU.mult))
                    for hp in range(2):
                        dv2.mark(dve.scalar_tensor_tensor(out=state[:, way, hp, :], in0=state[:, way, hp, :],
                                                          scalar=decay[:, way * 2 + hp, j:j + 1], in1=fresh[:, hp, :],
                                                          op0=ALU.mult, op1=ALU.add))
                    dve.wait_ge(dv2.sem, dv2.n)
                    dve.wait_ge(intra_mm.sem, u + 1)
                    dv2.link(dve, dve.tensor_tensor(num[:, :, :], intra, tmp[:, :, :], ALU.add))
                    nq = num[:, :, DH:DH + 1]
                    d3 = den[:, :].unsqueeze(2)
                    dv2.link(dve, dve.scalar_tensor_tensor(out=d3, in0=nq, scalar=-1.0, in1=nq, op0=ALU.mult, op1=ALU.max))
                    dv2.link(dve, dve.tensor_tensor(den[:, :], den[:, :], col(j, 2, way), ALU.max))
                    dv2.link(dve, dve.reciprocal(den[:, :], den[:, :]))
                    rec = den[:, :].unsqueeze(2).broadcast_to([P, HEADS, DH])
                    if second_visit(u):
                        dv2.link(dve, dve.tensor_tensor(num[:, :, 0:DH], num[:, :, 0:DH], rec, ALU.mult))
                        dv2.link(dve, dve.tensor_tensor(hB[:, j, :, :], hB[:, j, :, :], num[:, :, 0:DH], ALU.add))
                    else:
                        dv2.link(dve, dve.tensor_tensor(hB[:, j, :, :], num[:, :, 0:DH], rec, ALU.mult))
                    dve.wait_ge(dv2.sem, dv2.n)
                    dve.sem_inc(finished.sem, 1)

                def log_weights(u):
                    way, i, j = UNITS[u]
                    dve.wait_ge(d_mm.sem, u + 1)
                    if u >= 1:
                        dve.wait_ge(w_ready.sem, u)
                    for h in range(HEADS):
                        dve.scalar_tensor_tensor(out=logw[:, h, :], in0=ps[:, u % 2, h * P:(h + 1) * P],
                                                 scalar=col(j, 0, way)[:, h:h + 1], in1=neg[:, way, :],
                                                 op0=ALU.add, op1=ALU.min).then_inc(dm_ready.sem, 1)

                log_weights(0)
                for u in range(NU):
                    if u + 1 < NU:
                        log_weights(u + 1)
                    dve.wait_ge(w_ready.sem, u + 1)
                    dve.wait_ge(s_mm.sem, u + 1)
                    if u >= 1:
                        dve.wait_ge(intra_mm.sem, u)
                    dve.tensor_tensor(sw[:, :, :], ps[:, 2 + u % 2, :].rearrange("p (h t) -> p h t", h=HEADS), wgt[:, :, :],
                                      ALU.mult).then_inc(sw_ready.sem, 1)
                    if u >= 1:
                        finish(u - 1)
                finish(NU - 1)

        turn_out(nc, env, hB, 2, "b", norm=True)


def turn_out(nc, env, src, tile0, name, norm, slabs=None):
    ps, signal, yT = env["ps"], env["signal"], env["yT"]
    sq_ready, ms_ready, root, dv, normed, turned, kept = (
        signal(f"{name}_{n}") for n in ("out_square", "out_mean", "out_root", "out_dve", "out_normed", "out_turned", "out_kept"))
    gain = W(env, "out_gain")
    with ExitStack() as own, nc.Block() as block:
        sq = own.enter_context(nc.sbuf_tensor(f"{name}_outsq", [P, 2, HEADS, DH], F32))
        stat = own.enter_context(nc.sbuf_tensor(f"{name}_outstat", [P, 2, NT, HEADS], F32))

        if slabs:
            @block.sync
            def _(sp):
                load_slabs(sp, env, *slabs)

        if norm:
            @block.vector
            def _(dve):
                for t in range(NT):
                    dve.wait_ge(sq_ready.sem, t + 1)
                    dv.mark(dve.tensor_reduce(stat[:, 0, t, :], sq[:, t % 2, :, :], AX.X, ALU.add))
                dve.wait_ge(dv.sem, NT)
                dv.link(dve, dve.tensor_scalar(stat[:, 0, :, :], stat[:, 0, :, :], 1.0 / DH, EPS, ALU.mult, ALU.add))
                dve.sem_inc(ms_ready.sem, 1)
                dve.wait_ge(root.sem, 2)
                for t in range(NT):
                    dve.tensor_tensor(src[:, t, :, :], src[:, t, :, :],
                                      stat[:, 1, t, :].unsqueeze(2).broadcast_to([P, HEADS, DH]), ALU.mult)\
                       .then_inc(normed.sem, 1)

        @block.tensor
        def _(pe):
            for t in range(NT):
                if norm:
                    pe.wait_ge(normed.sem, t + 1)
                if t >= 4:
                    pe.wait_ge(kept.sem, 2 * (t - 3))
                flat = src[:, t, :, :].rearrange("p h d -> p (h d)")
                for c in range(2):
                    last = pe.transpose(ps[:, t % 4, c * P:(c + 1) * P], flat[:, c * P:(c + 1) * P], C(env, "ident"))
                last.then_inc(turned.sem, 1)

        @block.scalar
        def _(act):
            if norm:
                for t in range(NT):
                    if t >= 2:
                        act.wait_ge(dv.sem, t - 1)
                    act.activation(sq[:, t % 2, :, :], src[:, t, :, :], ACT.Square).then_inc(sq_ready.sem, 1)
                act.wait_ge(ms_ready.sem, 1)
                root.link(act, act.activation(stat[:, 1, :, :], stat[:, 0, :, :], ACT.Ln))
                root.mark(act.activation(stat[:, 1, :, :], stat[:, 1, :, :], ACT.Exp, scale=-0.5))
            for t in range(NT):
                act.wait_ge(turned.sem, t + 1)
                for c in range(2):
                    act.activation(yT[:, tile0 + c, t * P:(t + 1) * P], ps[:, t % 4, c * P:(c + 1) * P], ACT.Copy,
                                   scale=gain[:, tile0 + c:tile0 + c + 1]).then_inc(kept.sem, 1)
            act.wait_ge(kept.sem, 2 * NT)


def stage_gla(nc, env):
    ps, signal, hT, yT = (env[n] for n in ("ps", "signal", "hT", "yT"))
    loaded, slab_used = env["loaded"], env["slab_used"]
    outer = ExitStack()
    with outer:
        vC = yT[:, 4:6, :].rearrange("p a t -> p (a t)").rearrange("p (t c) -> p t c", t=NT)
        qT = outer.enter_context(nc.sbuf_tensor("c_qT", [P, T], F32))
        kT = outer.enter_context(nc.sbuf_tensor("c_kT", [P, T], F32))
        hC = yT[:, 0:2, :].rearrange("p a t -> p (a t)").rearrange("p (t h d) -> p t h d", t=NT, h=HEADS)
        sums = yT[:, 6:8, :]
        mm, ev, logs, dv = (signal(n) for n in ("c_product", "c_kept", "c_logs", "c_dve"))
        jobs = [(kind, 0, b) for kind in ("q", "k", "lr") for b in BLOCKS] + [("v", t, None) for t in range(NT)] + \
            [("la", z, b) for z in range(2) for b in BLOCKS]
        with ExitStack() as own, nc.Block() as block:
            lrT = own.enter_context(nc.sbuf_tensor("c_lrT", [2 * RANK, T], F32))
            la = own.enter_context(nc.sbuf_tensor("c_la", [P, 2, T], F32))

            @block.sync
            def _(sp):
                load_slabs(sp, env, 10, 12)

            @block.tensor
            def _(pe):
                for n, (kind, c, b) in enumerate(jobs):
                    if n == 0:
                        pe.wait_ge(loaded[S_CQK].sem, 16)
                    if n == 9:
                        pe.wait_ge(loaded[S_CV].sem, 16)
                    if n >= 4:
                        pe.wait_ge(ev.sem, n - 3)
                    bank = ps[:, n % 4, :]
                    if kind in ("q", "k"):
                        c0 = 0 if kind == "q" else P
                        last = proj_channels(pe, env, bank[:, 0:b[1]], S_CQK, c0, c0 + P, *b)
                    elif kind == "lr":
                        last = proj_channels(pe, env, bank[0:2 * RANK, 0:b[1]], S_CQK, GW, GW + 2 * RANK, *b)
                    elif kind == "v":
                        last = proj_tokens(pe, env, bank[:, 0:GW], S_CV, 0, GW, c)
                    else:
                        wg = W(env, "c_wg", 2 * RANK)[:, c * P:(c + 1) * P]
                        last = pe.matmul(bank[:, 0:b[1]], wg, lrT[:, b[0]:b[0] + b[1]], start=True, stop=True)
                    last.then_inc(mm.sem, 1)
                    if n in (8, 18):
                        pe.wait_ge(mm.sem, n + 1)
                        pe.sem_inc(slab_used.sem, 1)

            @block.scalar
            def _(act):
                for n, (kind, c, b) in enumerate(jobs):
                    act.wait_ge(mm.sem, n + 1)
                    bank = ps[:, n % 4, :]
                    if kind == "v":
                        ins = act.activation(vC[:, c, :], bank[:, 0:GW], ACT.Copy)
                    elif kind == "la":
                        ins = act.activation(la[:, c, b[0]:b[0] + b[1]], bank[:, 0:b[1]], ACT.Identity,
                                             bias=W(env, "c_bg")[:, c:c + 1])
                    else:
                        rows = 2 * RANK if kind == "lr" else P
                        out = {"q": qT, "k": kT, "lr": lrT}[kind]
                        ins = act.activation(out[:, b[0]:b[0] + b[1]], bank[0:rows, 0:b[1]], ACT.Copy,
                                             scale=(DH // 2) ** -0.5 if kind == "q" else 1.0)
                    ins.then_inc(ev.sem, 1)
                act.wait_ge(ev.sem, len(jobs))
                logs.link(act, act.activation(sums[:, :, :], la[:, :, :], ACT.Abs))
                logs.link(act, act.activation(sums[:, :, :], sums[:, :, :], ACT.Exp, scale=-1.0))
                logs.mark(act.activation(sums[:, :, :], sums[:, :, :], ACT.Ln, bias=1.0))

            @block.vector
            def _(dve):
                dve.wait_ge(logs.sem, 3)
                dv.link(dve, dve.scalar_tensor_tensor(out=la[:, :, :], in0=la[:, :, :], scalar=0.0, in1=sums[:, :, :],
                                                      op0=ALU.min, op1=ALU.subtract))
                dv.link(dve, dve.tensor_scalar(la[:, :, :], la[:, :, :], 1.0 / TAU, LA_MIN, ALU.mult, ALU.max))
                for t in range(NT):
                    a, b = t * P, (t + 1) * P
                    dv.mark(dve.tensor_tensor_scan(sums[:, 0, a:b], C(env, "ones"), la[:, 0, a:b], 0.0, ALU.mult, ALU.add))
                    dv.mark(dve.tensor_tensor_scan(sums[:, 1, a:b][:, ::-1], C(env, "ones"), la[:, 1, a:b][:, ::-1], 0.0,
                                                   ALU.mult, ALU.add))
                dve.wait_ge(dv.sem, dv.n)

        (diff_ready, decay_ready, k_scaled, q_multiplied, q_scaled, q_placed_v, q_placed_s, far_mm, map_mm, src_turned, src_kept, far_kept,
         picked, o_mm, u_mm, finished, zeroed, cleared, dv2, act2) = (
            signal(n) for n in ("c_diff", "c_decay", "c_k_scaled", "c_q_multiplied", "c_q_scaled", "c_q_placed_v", "c_q_placed_s", "c_far_mm",
                                "c_map_mm", "c_src_turned", "c_src_kept", "c_far_kept", "c_picked", "c_out_mm", "c_new_mm",
                                "c_finished", "c_zeroed", "c_cleared", "c_dve2", "c_act2"))
        LEVELS = (64, 32, 16, 8)
        NU = len(UNITS)
        with ExitStack() as own, nc.Block() as block:
            def tile(name, shape):
                return own.enter_context(nc.sbuf_tensor(name, shape, F32))

            diff = tile("c_diffs", [P, 2, 5, P])
            decays = tile("c_decays", [P, 2, 8, P])
            kx = tile("c_kx", [P, 2, 6, P])
            from_start = tile("c_from_start", [P, 4, P])
            qx = tile("c_qx", [P, 2, 5, P])
            qh = tile("c_qh", [P, 2, 5, HEADS, P])
            spare = env["ring"][:, S_AV % RING, KT * SLAB_W[S_AV]:]
            acc = spare[:, 0:2 * HEADS * P].rearrange("p (w h t) -> p w h t", w=2, h=HEADS)
            state = spare[:, 2 * HEADS * P:2 * HEADS * P + 2 * GW].rearrange("p (w c) -> p w c", w=2)
            new = spare[:, 2 * HEADS * P + 2 * GW:2 * HEADS * P + 3 * GW]
            src = spare[:, 2 * HEADS * P + 3 * GW:2 * HEADS * P + 3 * GW + 2 * P].rearrange("p (u c) -> p u c", u=2)
            start = tile("c_start", [P, 4])

            def span(u):
                return slice(UNITS[u][2] * P, (UNITS[u][2] + 1) * P)

            def place(u, h):
                r = slice(32 * h, 32 * h + 32)
                return qh[r, u % 2, :, h, :], qx[r, u % 2, :, :]

            @block.gpsimd
            def _(pool):
                def differences(u):
                    way, i, j = UNITS[u]
                    if u >= 2:
                        pool.wait_ge(decay_ready.sem, u - 1)
                    for lev, half in enumerate(LEVELS + (4,)):
                        mid = half - 1 + way
                        view = sums[:, way, span(u)].rearrange("p (b t) -> p b t", t=2 * half)
                        out = diff[:, u % 2, lev, :].rearrange("p (b t) -> p b t", t=2 * half)
                        pool.tensor_tensor(out, view, view[:, :, mid:mid + 1].broadcast_to([P, P // (2 * half), 2 * half]),
                                           ALU.subtract).then_inc(diff_ready.sem, 1)

                def scale_k(u):
                    pool.wait_ge(decay_ready.sem, u + 1)
                    if u >= 2:
                        pool.wait_ge(map_mm.sem, 3 * (u - 1))
                    pool.tensor_tensor(kx[:, u % 2, :, :], decays[:, u % 2, 0:6, :],
                                       kT[:, span(u)].unsqueeze(1).broadcast_to([P, 6, P]), ALU.mult).then_inc(k_scaled.sem, 1)

                differences(0)
                pool.memset(acc[:, :, :, :], 0.0).then_inc(zeroed.sem, 1)
                pool.memset(state[:, :, :], 0.0).then_inc(zeroed.sem, 1)
                differences(1)
                for u in range(NU):
                    scale_k(u)
                    if u + 2 < NU:
                        differences(u + 2)

            @block.scalar
            def _(act):
                def decay(u):
                    way, i, j = UNITS[u]
                    s = sums[:, way, span(u)]
                    end = P - 1 if way == 0 else 0
                    d = decays[:, u % 2, :, :]
                    act.wait_ge(diff_ready.sem, 5 * (u + 1))
                    if u >= 2:
                        act.wait_ge(k_scaled.sem, u - 1)
                        act.wait_ge(q_scaled.sem, u - 1)
                    act2.link(act, act.activation(d[:, 2:6, :], diff[:, u % 2, 0:4, :], ACT.Abs))
                    act.activation(d[:, 2:6, :], d[:, 2:6, :], ACT.Exp, scale=-1.0)
                    act.activation(d[:, 0, :], diff[:, u % 2, 4, :], ACT.Exp, scale=-1.0)
                    act.activation(d[:, 6, :], diff[:, u % 2, 4, :], ACT.Exp)
                    act.activation(d[:, 7, :], s, ACT.Exp)
                    act.activation(d[:, 1, :], s, ACT.Exp, scale=-1.0, bias=s[:, end:end + 1]).then_inc(decay_ready.sem, 1)

                def place_q(u):
                    act.wait_ge(q_multiplied.sem, u + 1)
                    if u == 0:
                        act.wait_ge(cleared.sem, 1)
                    if u >= 2:
                        act.wait_ge(map_mm.sem, 3 * (u - 1))
                    for h in (1, 2, 3):
                        act.activation(*place(u, h), ACT.Copy).then_inc(q_placed_s.sem, 1)

                decay(0)
                decay(1)
                place_q(0)
                for u, (way, i, j) in enumerate(UNITS):
                    act.wait_ge(src_turned.sem, u + 1)
                    if u >= 2:
                        act.wait_ge(u_mm.sem, u - 1)
                    act.activation(src[:, u % 2, :], ps[:, 7, 0:P], ACT.Copy).then_inc(src_kept.sem, 1)
                    act.wait_ge(far_mm.sem, u + 1)
                    if u >= 2:
                        act.wait_ge(o_mm.sem, u - 1)
                    if u == 0:
                        act.wait_ge(zeroed.sem, 1)
                    s0, t0 = (0, 64) if way == 0 else (64, 0)
                    act.activation(acc[s0:s0 + 64, way, :, t0:t0 + 64],
                                   ps[s0:s0 + 64, 3, 0:256].rearrange("p (h t) -> p h t", h=HEADS), ACT.Copy)\
                       .then_inc(far_kept.sem, 1)
                    for blk in (0, 64):
                        s0, t0 = (blk, blk + 32) if way == 0 else (blk + 32, blk)
                        act.activation(acc[s0:s0 + 32, way, :, t0:t0 + 32],
                                       ps[s0:s0 + 32, 3, 256:384].rearrange("p (h t) -> p h t", h=HEADS), ACT.Copy)\
                           .then_inc(far_kept.sem, 1)
                    if u + 1 < NU:
                        place_q(u + 1)
                    if u + 2 < NU:
                        decay(u + 2)

            @block.tensor
            def _(pe):
                def levels(u):
                    way, i, j = UNITS[u]
                    q, k = qh[:, u % 2, :, :, :], kx[:, u % 2, :, :]
                    pe.wait_ge(k_scaled.sem, u + 1)
                    if u >= 1:
                        pe.wait_ge(src_kept.sem, u)
                    pe.transpose(ps[:, 7, 0:P], k[:, 1, :], C(env, "ident")).then_inc(src_turned.sem, 1)
                    pe.wait_ge(q_placed_v.sem, u + 1)
                    pe.wait_ge(q_placed_s.sem, 3 * (u + 1))
                    if u >= 1:
                        pe.wait_ge(far_kept.sem, 3 * u)
                    s0, t0 = (0, 64) if way == 0 else (64, 0)
                    pe.matmul(ps[s0:s0 + 64, 3, 0:256], k[:, 2, s0:s0 + 64], q[:, 0, :, t0:t0 + 64], start=True, stop=True,
                              tile_position=(0, s0))
                    for blk in (0, 64):
                        s0, t0 = (blk, blk + 32) if way == 0 else (blk + 32, blk)
                        last = pe.matmul(ps[s0:s0 + 32, 3, 256:384], k[:, 3, s0:s0 + 32], q[:, 1, :, t0:t0 + 32],
                                         start=True, stop=True, tile_position=(0, s0))
                    last.then_inc(far_mm.sem, 1)
                    for n, (a, b) in enumerate(((4, 2), (5, 3), (0, 4))):
                        if u >= 1:
                            pe.wait_ge(picked.sem, 3 * (u - 1) + n + 1)
                        pe.matmul(ps[:, n, :], k[:, a, :], q[:, b, :, :], start=True, stop=True).then_inc(map_mm.sem, 1)

                def out(u):
                    way, i, j = UNITS[u]
                    pe.wait_ge(src_kept.sem, u + 1)
                    pe.wait_ge(zeroed.sem, 2)
                    if u >= 1:
                        pe.wait_ge(finished.sem, u)
                    pe.matmul(ps[:, 6, 0:GW], src[:, u % 2, :], vC[:, j, :], start=True, stop=True).then_inc(u_mm.sem, 1)
                    pe.wait_ge(q_scaled.sem, u + 1)
                    pe.matmul(ps[:, 5, 0:GW], from_start[:, u % 4, :], state[:, way, :], start=True, stop=False,
                              skip_group_check=True)
                    pe.wait_ge(picked.sem, 3 * (u + 1))
                    for h in range(HEADS):
                        last = pe.matmul(ps[:, 5, h * DH:(h + 1) * DH], acc[:, way, h, :], vC[:, j, h * DH:(h + 1) * DH],
                                         start=False, stop=h == HEADS - 1, skip_group_check=True)
                    last.then_inc(o_mm.sem, 1)

                for u in range(NU):
                    levels(u)
                    if u >= 1:
                        out(u - 1)
                out(NU - 1)

            @block.vector
            def _(dve):
                def scale_q(u):
                    way, i, j = UNITS[u]
                    dve.wait_ge(decay_ready.sem, u + 1)
                    if u >= 2:
                        dve.wait_ge(q_placed_s.sem, 3 * (u - 1))
                        dve.wait_ge(map_mm.sem, 3 * (u - 1))
                    if u >= 4:
                        dve.wait_ge(o_mm.sem, u - 3)
                    if u == 0:
                        dve.wait_ge(cleared.sem, 1)
                    end = P - 1 if way == 0 else 0
                    d = decays[:, u % 2, :, :]
                    q = qT[:, span(u)].unsqueeze(1)
                    dve.tensor_copy(start[:, u % 4:u % 4 + 1], d[:, 7, end:end + 1])
                    dve.tensor_tensor(qx[:, u % 2, :, :], d[:, 2:7, :], q.broadcast_to([P, 5, P]), ALU.mult)\
                       .then_inc(q_multiplied.sem, 1)
                    dve.tensor_tensor(place(u, 0)[0], d[0:32, 2:7, :], q[0:32].broadcast_to([32, 5, P]), ALU.mult)\
                       .then_inc(q_placed_v.sem, 1)
                    dve.tensor_tensor(from_start[:, u % 4, :], d[:, 7, :], qT[:, span(u)], ALU.mult).then_inc(q_scaled.sem, 1)

                def finish(u):
                    way, i, j = UNITS[u]
                    dve.wait_ge(u_mm.sem, u + 1)
                    dv2.link(dve, dve.tensor_tensor(new[:, :], ps[:, 6, 0:GW], C(env, "diag"), ALU.mult))
                    dve.wait_ge(o_mm.sem, u + 1)
                    dv2.mark(dve.scalar_tensor_tensor(out=state[:, way, :], in0=state[:, way, :], scalar=start[:, u % 4:u % 4 + 1],
                                                      in1=new[:, :], op0=ALU.mult, op1=ALU.add))
                    o = ps[:, 5, 0:GW].rearrange("p (h d) -> p h d", h=HEADS)
                    if second_visit(u):
                        dv2.mark(dve.tensor_tensor(hC[:, j, :, :], o, hC[:, j, :, :], ALU.add))
                    else:
                        dv2.mark(dve.tensor_copy(hC[:, j, :, :], o))
                    dve.wait_ge(dv2.sem, dv2.n)
                    dve.sem_inc(finished.sem, 1)

                pick = C(env, "pick").bitcast(mybir.dt.uint32).rearrange("p (a b c) -> p a b c", a=2, b=3)
                dve.memset(qh[:, :, :, :, :], 0.0).then_inc(cleared.sem, 1)
                scale_q(0)
                for u, (way, i, j) in enumerate(UNITS):
                    if u + 1 < NU:
                        scale_q(u + 1)
                    if u >= 2:
                        finish(u - 2)
                    dve.wait_ge(far_kept.sem, 3 * (u + 1))
                    for n in range(3):
                        dve.wait_ge(map_mm.sem, 3 * u + n + 1)
                        if n:
                            dve.wait_ge(picked.sem, 3 * u + n)
                        mask = pick[:, way, n, :].unsqueeze(1).broadcast_to([P, HEADS, P])
                        dve.copy_predicated(acc[:, way, :, :], mask, ps[:, n, :].rearrange("p (h t) -> p h t", h=HEADS))\
                           .then_inc(picked.sem, 1)
                finish(NU - 2)
                finish(NU - 1)

        turn_out(nc, env, hC, 4, "c", norm=True)


def project_qk(nc, env, name, s_qk, groups, width, qkT, v_of, last_slab_next, halves=None):
    ps, signal = env["ps"], env["signal"]
    n_qk = groups * width
    nch = n_qk // P
    mm, ev, sq_ready, ms_ready, root, normed, gained, cos_ready, rotated, dv, turned, kept, v_mm, v_ev = (
        signal(f"{name}_{n}") for n in ("product", "kept", "square", "mean", "root", "normed", "gained", "cos", "rotated",
                                        "dve", "turned", "turned_kept", "v_product", "v_kept"))
    loaded, slab_used = env["loaded"], env["slab_used"]
    s_v, v0, nv, v_dst = v_of
    with ExitStack() as own, nc.Block() as block:
        def tile(n, shape):
            return own.enter_context(nc.sbuf_tensor(f"{name}_{n}", shape, F32))

        raw = tile("raw", [P, 2, n_qk])
        sq = tile("sq", [P, n_qk])
        turn = tile("turn", [P, n_qk])
        rot = tile("rot", [P, 2, n_qk])
        stat = tile("stat", [P, 3, groups])
        ms, rstd, tmp = (stat[:, i, :] for i in range(3))
        cos = C(env, f"cos_{name}").rearrange("p (t w) -> p t w", t=NT)
        sin = C(env, f"sin_{name}").rearrange("p (t w) -> p t w", t=NT)
        q4 = width // 4

        def grouped(x):
            return x.rearrange("p (g w) -> p g w", g=groups)

        def quarters(x):
            return x.rearrange("p (g f s w) -> p g f s w", g=groups, f=2, s=2)

        @block.sync
        def _(sp):
            load_slabs(sp, env, *last_slab_next)

        @block.tensor
        def _(pe):
            def turns(t):
                if halves:
                    return
                pe.wait_ge(rotated.sem, t + 1)
                if t >= 2:
                    pe.wait_ge(kept.sem, t - 1)
                for c in range(nch):
                    last = pe.transpose(ps[:, 2 + t % 2, c * P:(c + 1) * P], rot[:, t % 2, c * P:(c + 1) * P], C(env, "ident"))
                last.then_inc(turned.sem, 1)

            pe.wait_ge(loaded[s_qk].sem, 16)
            for t in range(NT):
                if t >= 2:
                    pe.wait_ge(sq_ready.sem, t - 1)
                    pe.wait_ge(ev.sem, t - 1)
                proj_tokens(pe, env, ps[:, t % 2, 0:n_qk], s_qk, 0, n_qk, t).then_inc(mm.sem, 1)
                if t >= 2:
                    turns(t - 2)
                if s_v != s_qk and t == NT - 1:
                    pe.wait_ge(mm.sem, NT)
                    pe.sem_inc(slab_used.sem, 1)
            if s_v != s_qk:
                pe.wait_ge(loaded[s_v].sem, 16)
            for t in range(NT):
                if t >= 2:
                    pe.wait_ge(v_ev.sem, t - 1)
                proj_tokens(pe, env, ps[:, 4 + t % 2, 0:nv], s_v, v0, v0 + nv, t).then_inc(v_mm.sem, 1)
                if t < 2:
                    turns(NT - 2 + t)
            pe.wait_ge(v_mm.sem, NT)
            pe.sem_inc(slab_used.sem, 1)

        @block.scalar
        def _(act):
            def keep_turned(t):
                if halves:
                    return
                act.wait_ge(turned.sem, t + 1)
                act.activation(qkT[:, 0:nch, t * P:(t + 1) * P], ps[:, 2 + t % 2, 0:n_qk].rearrange("p (c t) -> p c t", c=nch),
                               ACT.Copy).then_inc(kept.sem, 1)

            for t in range(NT):
                act.wait_ge(mm.sem, t + 1)
                if t >= 1:
                    act.wait_ge(ms_ready.sem, t)
                act.activation(sq[:, :], ps[:, t % 2, 0:n_qk], ACT.Square).then_inc(sq_ready.sem, 1)
                if t >= 2:
                    act.wait_ge(rotated.sem, t - 1)
                act.activation(raw[:, t % 2, :], ps[:, t % 2, 0:n_qk], ACT.Copy).then_inc(ev.sem, 1)
                act.wait_ge(ms_ready.sem, t + 1)
                if t >= 1:
                    act.wait_ge(normed.sem, t)
                root.link(act, act.activation(rstd, ms, ACT.Ln))
                root.link(act, act.activation(rstd, rstd, ACT.Exp, scale=-0.5))
                if t >= 2:
                    keep_turned(t - 2)
            for t in range(NT):
                if t < 2:
                    act.wait_ge(v_mm.sem, t + 1)
                    act.activation(v_dst(t), ps[:, 4 + t % 2, 0:nv], ACT.Copy).then_inc(v_ev.sem, 1)
                    keep_turned(NT - 2 + t)
                else:
                    act.wait_ge(v_mm.sem, t + 1)
                    act.activation(v_dst(t), ps[:, 4 + t % 2, 0:nv], ACT.Copy).then_inc(v_ev.sem, 1)
            act.wait_ge(v_ev.sem, NT)
            if not halves:
                act.wait_ge(kept.sem, NT)

        @block.gpsimd
        def _(pool):
            for t in range(NT):
                pool.wait_ge(normed.sem, t + 1)
                pool.tensor_tensor(raw[:, t % 2, :], raw[:, t % 2, :], W(env, f"{name}_gain"), ALU.mult)\
                    .then_inc(gained.sem, 1)
                pool.wait_ge(gained.sem, t + 1)
                if t >= 2:
                    pool.wait_ge(rotated.sem if halves else turned.sem, t - 1)
                pool.tensor_tensor(grouped(rot[:, t % 2, :]), grouped(raw[:, t % 2, :]),
                                   cos[:, t, :].unsqueeze(1).broadcast_to([P, groups, width]), ALU.mult)\
                    .then_inc(cos_ready.sem, 1)

        @block.vector
        def _(dve):
            for t in range(NT):
                dve.wait_ge(sq_ready.sem, t + 1)
                if halves and t == 0:
                    gain = W(env, f"{name}_gain")[:, 0:n_qk // 2]
                    dv.link(dve, dve.tensor_scalar(gain, gain, width ** -0.5, None, ALU.mult))
                if t >= 1:
                    dve.wait_ge(root.sem, 2 * t)
                dv.link(dve, dve.tensor_reduce(ms, grouped(sq[:, :]), AX.X, ALU.add))
                dv.link(dve, dve.tensor_scalar(ms, ms, 1.0 / width, EPS, ALU.mult, ALU.add))
                dve.sem_inc(ms_ready.sem, 1)
                dve.wait_ge(root.sem, 2 * (t + 1))
                rsqrt_newton(dve, dv, rstd, ms, tmp)
                dve.wait_ge(ev.sem, t + 1)
                dve.tensor_tensor(grouped(raw[:, t % 2, :]), grouped(raw[:, t % 2, :]),
                                  rstd.unsqueeze(2).broadcast_to([P, groups, width]), ALU.mult).then_inc(normed.sem, 1)
                dve.wait_ge(gained.sem, t + 1)
                x, y = quarters(raw[:, t % 2, :]), quarters(turn[:, :])
                s = sin[:, t, :].rearrange("p (f s w) -> p f s w", f=2, s=2)
                for i in range(2):
                    for f in range(2):
                        ins = dve.tensor_tensor(y[:, :, f, i, :], x[:, :, f, 1 - i, :],
                                                s[:, f, i, :].unsqueeze(1).broadcast_to([P, groups, q4]), ALU.mult)
                        dv.mark(ins)
                dve.wait_ge(dv.sem, dv.n)
                dve.wait_ge(cos_ready.sem, t + 1)
                if halves:
                    for i, half in enumerate(halves):
                        a, b = (x.rearrange("p (s i c) -> p s i c", s=2, i=2)[:, :, i, :] for x in (rot[:, t % 2, :], turn[:, :]))
                        ins = dve.tensor_tensor(half[:, t, :].rearrange("p (s c) -> p s c", s=2), a, b, ALU.add)
                        if i == 0:
                            dv.mark(ins)
                    dve.wait_ge(dv.sem, dv.n)
                    ins.then_inc(rotated.sem, 1)
                else:
                    dve.tensor_tensor(rot[:, t % 2, :], rot[:, t % 2, :], turn[:, :], ALU.add).then_inc(rotated.sem, 1)
                dve.wait_ge(rotated.sem, t + 1)


def stack_pair(nc, env, src, q4, k4, name):
    ps, signal = env["ps"], env["signal"]
    split, low, high, turned, kept_q, kept_k = (
        signal(f"{name}_{n}") for n in ("stack_split", "stack_low", "stack_high", "stack_turned", "stack_q", "stack_k"))
    with ExitStack() as own, nc.Block() as block:
        hi = own.enter_context(nc.sbuf_tensor(f"{name}_hi", [P, 2, 2 * P], F32R))
        stack = env["ring"].rearrange("p a n -> p (a n)")[:, 0:2048].rearrange("p (u s m b c) -> p u s m b c", u=2, s=2, m=4, b=4)

        def maps(x, s):
            return x.rearrange("p (s m c) -> p s m c", s=2, m=4)[:, s, :, :].unsqueeze(2).broadcast_to([P, 4, 2, 32])

        def places(t, s, low):
            x = stack[:, t % 2, s, :, :, :]
            return x[:, :, 2 * low:2 * low + 2, :] if s == 0 else x[:, :, low::2, :]

        @block.vector
        def _(dve):
            for t in range(NT):
                if t >= 2:
                    dve.wait_ge(high.sem, 2 * (t - 1))
                    dve.wait_ge(turned.sem, t - 1)
                dve.tensor_copy(hi[:, t % 2, :], src[:, t, :]).then_inc(split.sem, 1)
                dve.wait_ge(split.sem, t + 1)
                for s in range(2):
                    dve.tensor_tensor(places(t, s, 1), maps(src[:, t, :], s), maps(hi[:, t % 2, :].bitcast(F32), s), ALU.subtract)\
                       .then_inc(low.sem, 1)
                if t >= 1:
                    dve.wait_ge(turned.sem, t)
                    dve.tensor_copy(k4[:, :, (t - 1) * P:t * P],
                                    ps[:, 2 * ((t - 1) % 2) + 1, :].rearrange("p (m t) -> p m t", m=4)).then_inc(kept_k.sem, 1)
            dve.wait_ge(turned.sem, NT)
            dve.tensor_copy(k4[:, :, (NT - 1) * P:NT * P], ps[:, 2 * ((NT - 1) % 2) + 1, :].rearrange("p (m t) -> p m t", m=4))\
               .then_inc(kept_k.sem, 1)

        @block.gpsimd
        def _(pool):
            for t in range(NT):
                pool.wait_ge(split.sem, t + 1)
                for s in range(2):
                    pool.tensor_copy(places(t, s, 0), maps(hi[:, t % 2, :].bitcast(F32), s)).then_inc(high.sem, 1)

        @block.tensor
        def _(pe):
            for t in range(NT):
                pe.wait_ge(low.sem, 2 * (t + 1))
                pe.wait_ge(high.sem, 2 * (t + 1))
                if t >= 2:
                    pe.wait_ge(kept_q.sem, t - 1)
                    pe.wait_ge(kept_k.sem, t - 1)
                for s in range(2):
                    for m in range(4):
                        last = pe.transpose(ps[:, 2 * (t % 2) + s, m * P:(m + 1) * P],
                                            stack[:, t % 2, s, m, :, :].rearrange("p b c -> p (b c)"), C(env, "ident"))
                last.then_inc(turned.sem, 1)

        @block.scalar
        def _(act):
            for t in range(NT):
                act.wait_ge(turned.sem, t + 1)
                act.activation(q4[:, :, t * P:(t + 1) * P], ps[:, 2 * (t % 2), :].rearrange("p (m t) -> p m t", m=4), ACT.Copy)\
                   .then_inc(kept_q.sem, 1)


def stage_diff_attention(nc, env):
    ps, signal = env["ps"], env["signal"]
    yT = env["yT"]
    with ExitStack() as outer:
        by_token = lambda k: yT[:, k:k + 2, :].rearrange("p a t -> p (a t)").rearrange("p (t c) -> p t c", t=NT)
        vA = by_token(0)
        yA = by_token(6).rearrange("p t (h d) -> p t h d", h=HEADS)
        second = outer.enter_context(nc.sbuf_tensor("a_qk1", [P, NT, 2 * P], F32))
        pairs = [by_token(6), second]
        project_qk(nc, env, "a", S_AQK, 16, 32, None, (S_AV, 0, GW, lambda t: vA[:, t, :]), (12, 12), halves=pairs)
        q4 = outer.enter_context(nc.sbuf_tensor("a_q4", [P, 4, T], F32R))
        k4 = outer.enter_context(nc.sbuf_tensor("a_k4", [P, 4, T], F32R))
        nlam = outer.enter_context(nc.sbuf_tensor("a_nlam", [P, 1], F32))
        for pair in range(2):
            stack_pair(nc, env, pairs[pair], q4, k4, f"a{pair}")
            attend_pair(nc, env, pair, q4, k4, vA, yA, nlam)
        turn_out(nc, env, yA, 0, "a", norm=True, slabs=(12, 14))


def attend_pair(nc, env, pair, q4, k4, vA, yA, nlam):
    ps, signal = env["ps"], env["signal"]
    name = f"a{pair}"
    (s_mm, mx, exped, comb, t_mm, t_kept, o_mm, o_kept, dv, lam_a) = (
        signal(f"{name}_{n}") for n in ("scores", "max", "exp", "combined", "turns", "turn_kept", "out_mm", "out_read",
                                        "dve", "lam"))
    SLOTS = 6
    units = [(t, h) for t in range(NT) for h in range(2)]
    NU = len(units)
    scratch = env["ring"][:, :, :].rearrange("p a n -> p (a n)")
    probs = [[scratch[:, i * T:(i + 1) * T] for i in places] for places in ((0, 1, 2), (3, 4))]

    def p(u, c, n):
        return probs[c][u % len(probs[c])][:, 0:n]

    def keys(t):
        return NC if t < NC else NT

    def chunks(t):
        n = keys(t)
        return [(a, min(a + 4, n)) for a in range(0, n, 4)]

    def before(u):
        return sum(len(chunks(units[i][0])) for i in range(u))

    with ExitStack() as own, nc.Block() as block:
        def tile(n, shape):
            return own.enter_context(nc.sbuf_tensor(f"{name}_{n}", shape, F32))

        turned = [scratch[:, 5 * T:6 * T], tile("aT", [P, T])[:, :]]
        aT = [x.rearrange("p (k t) -> p k t", t=P) for x in turned]
        stat = tile("st", [P, SLOTS, 2, 4])
        lam = tile("lm", [P, 2, 32])
        lam2 = tile("lm2", [P, 2])

        @block.tensor
        def _(pe):
            def scores(u, c):
                t, h = units[u]
                if u >= 1:
                    pe.wait_ge(exped.sem, 2 * (u - 1) + c + 1)
                n = keys(t) * P
                for b, k0 in enumerate(range(0, n, BANK)):
                    w = min(BANK, n - k0)
                    last = pe.matmul(ps[:, 3 * c + b, 0:w], q4[:, 2 * h + c, t * P:(t + 1) * P], k4[:, 2 * h + c, k0:k0 + w],
                                     start=True, stop=True)
                last.then_inc(s_mm.sem, 1)

            def turns(u):
                t, h = units[u]
                pe.wait_ge(comb.sem, u + 1)
                for n, (a, b) in enumerate(chunks(t)):
                    if n == 0:
                        pe.wait_ge(t_kept.sem, before(u))
                    if n == 1 and u >= 2:
                        pe.wait_ge(o_kept.sem, u - 1)
                    if n == 2:
                        pe.wait_ge(t_kept.sem, before(u) + 1)
                    for k in range(a, b):
                        last = pe.transpose(ps[:, 6 + n % 2, (k - a) * P:(k - a + 1) * P], p(u, 0, T)[:, k * P:(k + 1) * P],
                                            C(env, "ident"))
                    last.then_inc(t_mm.sem, 1)

            def value(u):
                t, h = units[u]
                pe.wait_ge(t_kept.sem, before(u + 1))
                if u + 1 < NU:
                    pe.wait_ge(t_kept.sem, before(u + 1) + min(2, len(chunks(units[u + 1][0]))))
                if u >= 1:
                    pe.wait_ge(o_kept.sem, u)
                n = keys(t)
                h = 2 * pair + h
                for k in range(n):
                    last = pe.matmul(ps[:, 7, 0:DH], aT[u % 2][:, k, :], vA[:, k, h * DH:(h + 1) * DH], start=k == 0, stop=k == n - 1)
                last.then_inc(o_mm.sem, 1)

            scores(0, 0)
            for u in range(NU):
                scores(u, 1)
                if u >= 2:
                    turns(u - 2)
                if u + 1 < NU:
                    scores(u + 1, 0)
                if u >= 3:
                    value(u - 3)
            turns(NU - 2)
            value(NU - 3)
            turns(NU - 1)
            value(NU - 2)
            value(NU - 1)

        @block.scalar
        def _(act):
            def exp(u, c):
                t, h = units[u]
                act.wait_ge(mx.sem, 2 * u + c + 1)
                if c == 0 and u >= 3:
                    act.wait_ge(t_mm.sem, before(u - 2))
                if c == 1 and u >= 2:
                    act.wait_ge(comb.sem, u - 1)
                n = keys(t) * P
                st = stat[:, u % SLOTS, c, :]
                act.activation(p(u, c, n), ps[:, 3 * c:3 * c + 3, :].rearrange("p b n -> p (b n)")[:, 0:n], ACT.Exp,
                               bias=st[:, 0:1], accum_out=st[:, 1:2]).then_inc(exped.sem, 1)

            def keep(u):
                t, h = units[u]
                for n, (a, b) in enumerate(chunks(t)):
                    act.wait_ge(t_mm.sem, before(u) + n + 1)
                    if n == 0 and u >= 2:
                        act.wait_ge(o_mm.sem, u - 1)
                    act.activation(aT[u % 2][:, a:b, :], ps[:, 6 + n % 2, 0:(b - a) * P].rearrange("p (k t) -> p k t", t=P),
                                   ACT.Copy).then_inc(t_kept.sem, 1)

            if pair == 0:
                act.wait_ge(lam_a.sem, 2)
                act.activation(lam2[:, :], lam2[:, :], ACT.Exp).then_inc(lam_a.sem, 1)
            for u in range(NU):
                exp(u, 0)
                if u >= 2:
                    keep(u - 2)
                exp(u, 1)
            keep(NU - 2)
            keep(NU - 1)

        @block.vector
        def _(dve):
            def maximum(u, c):
                t, h = units[u]
                dve.wait_ge(s_mm.sem, 2 * u + c + 1)
                n = keys(t) * P
                dve.tensor_reduce(stat[:, u % SLOTS, c, 0:1], ps[:, 3 * c:3 * c + 3, :].rearrange("p b n -> p (b n)")[:, 0:n],
                                  AX.X, ALU.max, negate=True).then_inc(mx.sem, 1)

            def combine(u):
                t, h = units[u]
                st = stat[:, u % SLOTS, :, :]
                dve.wait_ge(exped.sem, 2 * u + 2)
                dv.link(dve, dve.reciprocal(st[:, :, 2:3], st[:, :, 1:2]))
                dv.link(dve, dve.scalar_tensor_tensor(out=st[:, 0, 3:4], in0=st[:, 0, 1:2], scalar=st[:, 1, 2:3], in1=nlam[:, :],
                                                      op0=ALU.mult, op1=ALU.mult))
                n = keys(t) * P
                dve.scalar_tensor_tensor(out=p(u, 0, n), in0=p(u, 1, n), scalar=st[:, 0, 3:4],
                                         in1=p(u, 0, n), op0=ALU.mult, op1=ALU.add).then_inc(comb.sem, 1)

            def keep(u):
                t, h = units[u]
                dve.wait_ge(o_mm.sem, u + 1)
                dve.tensor_scalar(yA[:, t, 2 * pair + h, :], ps[:, 7, 0:DH], stat[:, u % SLOTS, 0, 2:3], None, ALU.mult)\
                   .then_inc(o_kept.sem, 1)

            if pair == 0:
                lp = W(env, "a_lam").rearrange("p (a b w) -> p a b w", a=2, b=2)
                lam_a.link(dve, dve.tensor_tensor(lam[:, :, :], lp[:, :, 0, :], lp[:, :, 1, :], ALU.mult))
                lam_a.mark(dve.tensor_reduce(lam2[:, :], lam[:, :, :], AX.X, ALU.add))
                dve.wait_ge(lam_a.sem, 3)
                dv.link(dve, dve.tensor_tensor(nlam[:, :], lam2[:, 1:2], lam2[:, 0:1], ALU.subtract))
                dv.link(dve, dve.tensor_tensor(nlam[:, :], nlam[:, :], W(env, "lam_init")[:, 0:1], ALU.subtract))
            for u in range(NU):
                maximum(u, 0)
                if u >= 4:
                    keep(u - 4)
                maximum(u, 1)
                if u >= 1:
                    combine(u - 1)
            combine(NU - 1)
            for u in range(NU - 4, NU):
                keep(u)
            dve.wait_ge(o_kept.sem, NU)


def stage_window_attention(nc, env):
    ps, signal = env["ps"], env["signal"]
    SCALE = DH ** -0.5
    with ExitStack() as outer:
        qkT = outer.enter_context(nc.sbuf_tensor("d_qkT", [P, 3, T], F32))
        vD = outer.enter_context(nc.sbuf_tensor("d_v", [P, NT, P], F32))
        yD = outer.enter_context(nc.sbuf_tensor("d_y", [P, NT, HEADS, DH], F32))
        project_qk(nc, env, "d", S_D, 6, 64, qkT, (S_D, 384, P, lambda t: vD[:, t, :]), (14, 15))
        (s_mm, mx, exped, summed, t_mm, t_kept, o_mm, o_kept, dv, sunk) = (
            signal(n) for n in ("d_scores", "d_max", "d_exp", "d_sum", "d_turns", "d_turn_kept", "d_out_mm", "d_out_read",
                                "d_dve2", "d_sink"))
        units = [(t, h) for t in range(NT) for h in range(HEADS)]
        NU = len(units)

        def key_tiles(t):
            ctx = [(k, None) for k in range(NC)]
            return ctx if t < NC else ctx + [(k, {-1: 0, 0: None, 1: 1}[k - t]) for k in (t - 1, t, t + 1) if NC <= k < NT]

        def nch(t):
            return 1 if len(key_tiles(t)) <= 4 else 2

        def before(u):
            return sum(nch(units[i][0]) for i in range(u))

        with ExitStack() as own, nc.Block() as block:
            def tile(n, shape):
                return own.enter_context(nc.sbuf_tensor(f"d_{n}", shape, F32))

            p = tile("p", [P, 2, 5 * P])
            aT = tile("aT", [P, 2, 5, P])
            stat = tile("st", [P, 4, 4])
            band = C(env, "band").rearrange("p (a b) -> p a b", a=2)

            @block.tensor
            def _(pe):
                def scores(u):
                    t, h = units[u]
                    kv, g = h // 2, h % 2
                    r = slice(64 * kv, 64 * kv + 64)
                    if u >= 2:
                        pe.wait_ge(exped.sem, u - 1)
                    for n, (k, mask) in enumerate(key_tiles(t)):
                        out = ps[:, 2 * (u % 2) + n // 4, (n % 4) * P:(n % 4 + 1) * P]
                        last = pe.matmul(out, qkT[r, g, t * P:(t + 1) * P], qkT[r, 2, k * P:(k + 1) * P],
                                         start=True, stop=mask is None)
                        if mask is not None:
                            last = pe.matmul(out, C(env, "ident"), band[:, mask, :], start=False, stop=True)
                    last.then_inc(s_mm.sem, 1)

                def turns(u):
                    t, h = units[u]
                    kt = key_tiles(t)
                    pe.wait_ge(exped.sem, u + 1)
                    if u >= 1:
                        pe.wait_ge(t_kept.sem, before(u))
                    for c in range(nch(t)):
                        for n in range(4 * c, min(4 * c + 4, len(kt))):
                            last = pe.transpose(ps[:, 4 + c, (n % 4) * P:(n % 4 + 1) * P], p[:, u % 2, n * P:(n + 1) * P],
                                                C(env, "ident"))
                        last.then_inc(t_mm.sem, 1)

                def value(u):
                    t, h = units[u]
                    kv = h // 2
                    kt = key_tiles(t)
                    pe.wait_ge(t_kept.sem, before(u + 1))
                    if u >= 2:
                        pe.wait_ge(o_kept.sem, u - 1)
                    for n, (k, _) in enumerate(kt):
                        last = pe.matmul(ps[:, 6 + u % 2, 0:DH], aT[:, u % 2, n, :], vD[:, k, kv * DH:(kv + 1) * DH],
                                         start=n == 0, stop=n == len(kt) - 1)
                    last.then_inc(o_mm.sem, 1)

                for u in range(NU):
                    scores(u)
                    if u >= 1:
                        turns(u - 1)
                    if u >= 2:
                        value(u - 2)
                turns(NU - 1)
                value(NU - 2)
                value(NU - 1)

            @block.scalar
            def _(act):
                def keep(u):
                    t, h = units[u]
                    if u >= 2:
                        act.wait_ge(o_mm.sem, u - 1)
                    for c in range(nch(t)):
                        n = min(4, len(key_tiles(t)) - 4 * c)
                        act.wait_ge(t_mm.sem, before(u) + c + 1)
                        act.activation(aT[:, u % 2, 4 * c:4 * c + n, :], ps[:, 4 + c, 0:n * P].rearrange("p (k t) -> p k t", t=P),
                                       ACT.Copy).then_inc(t_kept.sem, 1)

                for u in range(NU):
                    t, h = units[u]
                    n = len(key_tiles(t)) * P
                    st = stat[:, u % 4, :]
                    act.wait_ge(mx.sem, u + 1)
                    if u >= 2:
                        act.wait_ge(t_mm.sem, before(u - 1))
                    act.activation(p[:, u % 2, 0:n], ps[:, 2 * (u % 2):2 * (u % 2) + 2, :].rearrange("p b n -> p (b n)")[:, 0:n],
                                   ACT.Exp, bias=st[:, 0:1], scale=SCALE, accum_out=st[:, 1:2]).then_inc(exped.sem, 1)
                    act.activation(st[:, 2:3], W(env, "d_sink")[:, h:h + 1], ACT.Exp, bias=st[:, 0:1]).then_inc(sunk.sem, 1)
                    if u >= 1:
                        keep(u - 1)
                keep(NU - 1)

            @block.vector
            def _(dve):
                def maximum(u):
                    t, h = units[u]
                    n = len(key_tiles(t)) * P
                    st = stat[:, u % 4, :]
                    dve.wait_ge(s_mm.sem, u + 1)
                    dv.link(dve, dve.tensor_reduce(st[:, 0:1], ps[:, 2 * (u % 2):2 * (u % 2) + 2, :]
                                                   .rearrange("p b n -> p (b n)")[:, 0:n], AX.X, ALU.max))
                    dv.link(dve, dve.tensor_scalar(st[:, 0:1], st[:, 0:1], SCALE, W(env, "d_sink")[:, h:h + 1], ALU.mult, ALU.max))
                    dve.tensor_scalar(st[:, 0:1], st[:, 0:1], -1.0, None, ALU.mult).then_inc(mx.sem, 1)

                def finish(u):
                    t, h = units[u]
                    st = stat[:, u % 4, :]
                    dve.wait_ge(exped.sem, u + 1)
                    dve.wait_ge(sunk.sem, u + 1)
                    dv.link(dve, dve.tensor_tensor(st[:, 3:4], st[:, 1:2], st[:, 2:3], ALU.add))
                    dv.link(dve, dve.reciprocal(st[:, 3:4], st[:, 3:4]))
                    dve.wait_ge(o_mm.sem, u + 1)
                    dve.tensor_scalar(yD[:, t, h, :], ps[:, 6 + u % 2, 0:DH], st[:, 3:4], None, ALU.mult)\
                       .then_inc(o_kept.sem, 1)

                for u in range(NU):
                    maximum(u)
                    if u >= 3:
                        finish(u - 3)
                for u in range(NU - 3, NU):
                    finish(u)
                dve.wait_ge(o_kept.sem, NU)

        turn_out(nc, env, yD, 6, "d", norm=False)


def stage_gates(nc, env):
    ps, signal, yT = env["ps"], env["signal"], env["yT"]
    mm, sg, made, done, last_bo = (signal(n) for n in ("g_product", "g_sigmoid", "g_made", "g_done", "g_bo"))
    jobs = [(S_BO, c, 2 + c, b) for c in range(2) for b in BLOCKS] + \
        [(S_G0 + c // 4, c % 4, c, b) for c in range(KT) for b in BLOCKS]
    NJ = len(jobs)
    with ExitStack() as own, nc.Block() as block:
        sig = own.enter_context(nc.sbuf_tensor("g_sig", [P, 2, BANK], F32))
        gate = own.enter_context(nc.sbuf_tensor("g_gate", [P, 2, BANK], F32))

        @block.sync
        def _(sp):
            load_slabs(sp, env, 15, 18)

        @block.tensor
        def _(pe):
            for n, (s, c, k, b) in enumerate(jobs):
                if n == 0 or jobs[n - 1][0] != s:
                    pe.wait_ge(env["loaded"][s].sem, 16)
                if n >= 4:
                    pe.wait_ge(made.sem, n - 3)
                proj_channels(pe, env, ps[:, n % 4, 0:b[1]], s, c * P, (c + 1) * P, *b).then_inc(mm.sem, 1)
                if n == NJ - 1 or jobs[n + 1][0] != s:
                    pe.wait_ge(mm.sem, n + 1)
                    pe.sem_inc(env["slab_used"].sem, 1)

        @block.scalar
        def _(act):
            for n, (s, c, k, b) in enumerate(jobs):
                act.wait_ge(mm.sem, n + 1)
                if n >= 2:
                    act.wait_ge(made.sem, n - 1)
                act.activation(sig[:, n % 2, 0:b[1]], ps[:, n % 4, 0:b[1]], ACT.Sigmoid).then_inc(sg.sem, 1)

        @block.vector
        def _(dve):
            for n, (s, c, k, b) in enumerate(jobs):
                dve.wait_ge(sg.sem, n + 1)
                if n >= 2:
                    dve.wait_ge(done.sem, n - 1)
                if s == S_BO:
                    ins = dve.tensor_copy(gate[:, n % 2, 0:b[1]], sig[:, n % 2, 0:b[1]])
                else:
                    ins = dve.tensor_tensor(gate[:, n % 2, 0:b[1]], ps[:, n % 4, 0:b[1]], sig[:, n % 2, 0:b[1]], ALU.mult)
                ins.then_inc(made.sem, 1)

        @block.gpsimd
        def _(pool):
            for n, (s, c, k, b) in enumerate(jobs):
                pool.wait_ge(made.sem, n + 1)
                y = yT[:, k, b[0]:b[0] + b[1]]
                pool.tensor_tensor(y, y, gate[:, n % 2, 0:b[1]], ALU.mult).then_inc(done.sem, 1)
                if s == S_BO:
                    pool.wait_ge(done.sem, n + 1)
            pool.wait_ge(done.sem, NJ)


def stage_output(nc, env):
    ps, signal, yT, dram = (env[n] for n in ("ps", "signal", "yT", "dram"))
    NB = 4
    x_in = [signal(f"res{i}_loaded") for i in range(NB)]
    x_out = [signal(f"res{i}_stored") for i in range(NB)]
    mm, gated, added = (signal(n) for n in ("o_product", "o_gated", "o_added"))
    jobs = [(n, t) for n in range(2) for t in range(NT)]
    NJ = len(jobs)

    def rows(n, t):
        cols = slice(n * 512, (n + 1) * 512)
        return dram["ctx_now"][t * P:(t + 1) * P, cols] if t < NC else dram["out"][(t - NC) * P:(t - NC + 1) * P, cols]

    with ExitStack() as own, nc.Block() as block:
        res = own.enter_context(nc.sbuf_tensor("o_res", [P, NB, 512], F32))
        prod = own.enter_context(nc.sbuf_tensor("o_prod", [P, 2, 512], F32))

        @block.sync
        def _(sp):
            for i, (n, t) in enumerate(jobs):
                if i >= NB:
                    sp.wait_ge(x_out[i % NB].sem, 16 * (i // NB))
                sp.dma_start(res[:, i % NB, :], rows(n, t)).then_inc(x_in[i % NB].sem, 16)

        @block.tensor
        def _(pe):
            for i, (n, t) in enumerate(jobs):
                if t == 0:
                    pe.wait_ge(env["loaded"][S_OUT + n].sem, 16)
                if i >= 4:
                    pe.wait_ge(gated.sem, i - 3)
                for k in range(KT):
                    last = pe.matmul(ps[:, i % 4, :], yT[:, k, t * P:(t + 1) * P], slab(env, S_OUT + n)[:, k, :],
                                     start=k == 0, stop=k == KT - 1)
                last.then_inc(mm.sem, 1)

        @block.vector
        def _(dve):
            for i, (n, t) in enumerate(jobs):
                dve.wait_ge(mm.sem, i + 1)
                if i >= 2:
                    dve.wait_ge(added.sem, i - 1)
                v = 0 if t < NC else 1
                dve.tensor_tensor(prod[:, i % 2, :], ps[:, i % 4, :], env["gate_rows"][:, v, n * 512:(n + 1) * 512], ALU.mult)\
                   .then_inc(gated.sem, 1)

        @block.gpsimd
        def _(pool):
            for i, (n, t) in enumerate(jobs):
                pool.wait_ge(gated.sem, i + 1)
                pool.wait_ge(x_in[i % NB].sem, 16 * (i // NB + 1))
                pool.tensor_tensor(res[:, i % NB, :], res[:, i % NB, :], prod[:, i % 2, :], ALU.add).then_inc(added.sem, 1)

        @block.scalar
        def _(act):
            for i, (n, t) in enumerate(jobs):
                act.wait_ge(added.sem, i + 1)
                act.dma_start(rows(n, t), res[:, i % NB, :]).then_inc(x_out[i % NB].sem, 16)
            for b in range(NB):
                act.wait_ge(x_out[b].sem, 16 * (NJ // NB))


def constants():
    c = np.zeros((P, NCST), np.float32)

    def put(name, rows=P):
        a, b = CST[name]
        return c[0:rows, a:b]

    i, j = np.arange(P)[:, None], np.arange(P)[None, :]
    put("ident")[:] = i == j
    put("neg")[:, 0:P] = np.where(j >= i, 0.0, NEG)
    put("neg")[:, P:] = np.where(j <= i, 0.0, NEG)
    put("band")[:, 0:P] = np.where(j >= i, 0.0, NEG)
    put("band")[:, P:] = np.where(j <= i, 0.0, NEG)
    pos = np.arange(SEQ)
    for name, width in (("a", 32), ("d", 64)):
        nq = width // 4
        inv = np.float32(10000.0) ** (-np.arange(nq, dtype=np.float32) / np.float32(nq))
        r = (pos // GRID_W).astype(np.float32)[:, None] * inv
        q = (pos % GRID_W).astype(np.float32)[:, None] * inv
        cos = np.ones((T, width), np.float32)
        sin = np.zeros((T, width), np.float32)
        cos[CTX:] = np.concatenate([np.cos(r), np.cos(r), np.cos(q), np.cos(q)], 1)
        sin[CTX:] = np.concatenate([-np.sin(r), np.sin(r), -np.sin(q), np.sin(q)], 1)
        put(f"cos_{name}")[:] = cos.reshape(NT, P, width).transpose(1, 0, 2).reshape(P, -1)
        put(f"sin_{name}")[:] = sin.reshape(NT, P, width).transpose(1, 0, 2).reshape(P, -1)
    sel = put("sel_row").reshape(P, 8, P)
    pair = put("sel_pair").reshape(P, 4, P)
    for way in range(2):
        for h in range(HEADS):
            sel[32 * way + h, way * HEADS + h, :] = 1.0
            pair[32 * way + h, way * 2 + h // 2, 64 * (h % 2):64 * (h % 2) + 64] = 1.0
    put("sel_row")[:] = sel.reshape(P, -1)
    put("sel_pair")[:] = pair.reshape(P, -1)
    mod = put("sel_mod")
    mod[0, 0:P] = 1.0
    mod[1, P:] = 1.0
    put("ones")[:] = 1.0
    put("diag")[:] = (np.arange(P)[:, None] // 32) == (np.arange(GW)[None, :] // DH)
    pick = np.zeros((P, 2, 3, P), np.float32)
    for n, half in enumerate((16, 8)):
        same = (i // (2 * half)) == (j // (2 * half))
        pick[:, 0, n] = same & (i % (2 * half) < half) & (j % (2 * half) >= half)
        pick[:, 1, n] = same & (i % (2 * half) >= half) & (j % (2 * half) < half)
    pick[:, 0, 2] = ((i // 8) == (j // 8)) & (i <= j)
    pick[:, 1, 2] = ((i // 8) == (j // 8)) & (i >= j)
    put("pick")[:] = pick.reshape(P, -1)
    return c


def layout(w):
    return w.reshape(KT, P, w.shape[1]).transpose(1, 0, 2).reshape(P, -1)


def column(v):
    return v.reshape(-1, P).T


def pack(inputs):
    x = {k: np.asarray(v) for k, v in inputs.items()}
    w_all, par_all = [], []
    for l in range(DEPTH):
        wi = x["w_in"][l]
        gates = wi[:, B_G:B_G + 16].reshape(D, 4, HEADS)
        gap = np.zeros((D, 32 - HEADS), np.float32)
        li = np.concatenate([gates[:, 0], gap, gates[:, 2]], 1)
        lf = np.concatenate([gates[:, 1], gap, gates[:, 3]], 1)
        take = lambda a, n: wi[:, a:a + n]
        dq = take(D0, 256).reshape(D, 2, 2, DH).transpose(0, 2, 1, 3).reshape(D, 256)
        slabs = [x["w_mod"][l][:, i * 512:(i + 1) * 512] for i in range(6)]
        slabs += [take(*B_QK), np.concatenate([take(*B_V), li, lf], 1), np.concatenate([take(*C_QK), take(*C_LR)], 1),
                  take(*C_V), take(*A_QK), take(*A_V), np.concatenate([dq, take(D0 + 256, 256)], 1), take(*B_O),
                  take(G0, 512), take(G0 + 512, 512)]
        slabs += [x["w_out"][l][:, i * 512:(i + 1) * 512] for i in range(2)]
        w_all.append(np.concatenate([layout(s) for s in slabs], 1))
        p = np.zeros((P, NPAR), np.float32)

        def put(name):
            a, b = PAR[name]
            return p[:, a:b]

        put("norm_g")[:] = column(x["norm_g"][l])
        put("b_sh")[:] = column(x["b_mod"][l][0:D])
        put("b_sc")[:] = column(x["b_mod"][l][D:2 * D])
        put("b_gt")[:] = x["b_mod"][l][None, 2 * D:]
        put("a_gain")[:] = np.concatenate([np.tile(x["a_qn"][l], 8), np.tile(x["a_kn"][l], 8)])[None]
        put("d_gain")[:] = np.concatenate([np.tile(x["d_qn"][l], 4), np.tile(x["d_kn"][l], 2)])[None]
        put("conv_w")[:] = x["b_conv_w"][l].reshape(3, 4, P).transpose(2, 1, 0).reshape(P, 12)
        put("conv_b")[:] = column(x["b_conv_b"][l])
        for way in range(2):
            put("gate_li")[32 * way:32 * way + HEADS, 0] = x["b_gate_b"][l][2 * way]
            put("gate_lf")[32 * way:32 * way + HEADS, 0] = x["b_gate_b"][l][2 * way + 1]
        put("c_bg")[:] = x["c_bg"][l].T
        for z in range(2):
            put("c_wg")[z * RANK:(z + 1) * RANK, z * P:(z + 1) * P] = x["c_wg"][l][z]
        put("out_gain")[:] = 1.0
        for k, name in ((0, "a_subln"), (2, "b_outn"), (4, "c_outn")):
            put("out_gain")[:, k:k + 2] = np.tile(x[name][l], 2)[:, None]
        put("a_lam")[:] = x["a_lam"][l].reshape(1, -1)
        put("d_sink")[:] = x["d_sink"][l][None]
        lam_init = 0.8 - 0.6 * float(np.exp(-0.3 * l))
        put("lam_init")[:] = np.array([[lam_init, 1.0 - lam_init]], np.float32)
        par_all.append(p)
    return {
        "w": np.concatenate(w_all, 0), "par": np.concatenate(par_all, 0), "cst": constants(),
        "tok": np.concatenate([x["ctx"][0], x["x"][0]], 0),
        "c": np.stack([column(x["c_ctx"]), column(x["c"][0])], 2).reshape(P, 2 * KT),
    }


def kernel(**inputs):
    import concourse.bacc as bacc
    from concourse.bass_utils import run_bass_kernel_spmd

    nc = bacc.Bacc("TRN2", target_bir_lowering=False, num_devices=1)
    arrays = {f"in_{k}": np.ascontiguousarray(v) for k, v in pack(inputs).items()}
    dram = {k[3:]: nc.dram_tensor(k, v.shape, mybir.dt.from_np(v.dtype), kind="ExternalInput").ap()
            for k, v in arrays.items()}
    dram["ctx_now"] = nc.dram_tensor("ctx_now", (CTX, D), F32, kind="Internal").ap()
    dram["out"] = nc.dram_tensor("latents", (SEQ, D), F32, kind="ExternalOutput").ap()
    layer_program(nc, dram)
    r = run_bass_kernel_spmd(nc, [arrays], core_ids=[0])
    return r.results[0]["latents"].reshape(1, SEQ, D)
```

```python
from contextlib import ExitStack

import numpy as np

import concourse.bass as bass
from concourse import mybir

F32 = mybir.dt.float32
F32R = mybir.dt.float32r
ALU = mybir.AluOpType
ACT = mybir.ActivationFunctionType
AX = mybir.AxisListType

P = 128
DEPTH = 2
D = 1024
KT = D // P
CTX = 256
SEQ = 1024
T = CTX + SEQ
NT = T // P
NC = CTX // P
GRID_W = 64
HEADS = 4
DH = 64
GW = HEADS * DH
RANK = 16
TAU = 16.0
EPS = 1e-6
NEG = -1e30
LA_MIN = -19.0
BANK = 512
ROWS = 36
BLOCKS = [(0, 512), (512, 512), (1024, 256)]

A0, B0, C0, D0, G0 = 0, 768, 1808, 2352, 2864
A_QK, A_V = (A0, 512), (A0 + 512, 256)
B_QK, B_V, B_G, B_O = (B0, 512), (B0 + 512, 256), B0 + 768, (B0 + 784, 256)
C_QK, C_V, C_LR = (C0, 256), (C0 + 256, 256), (C0 + 512, 32)

SLAB_W = [512] * 6 + [328, 512, 256, 288, 512, 256, 512, 256, 512, 512] + [512] * 2
SLAB_AT = [sum(SLAB_W[:i]) * KT for i in range(len(SLAB_W) + 1)]
(S_BV, S_BQK, S_CQK, S_CV, S_AQK, S_AV, S_D, S_BO, S_G0, S_G1) = range(6, 16)
S_OUT = 16
NSLAB = len(SLAB_W)
RING = 2

PAR = {}
_at = 0
for _n, _w in [("norm_g", KT), ("b_sh", KT), ("b_sc", KT), ("b_gt", D), ("a_gain", 512), ("d_gain", 384),
               ("conv_w", 12), ("conv_b", 4), ("gate_li", 1), ("gate_lf", 1), ("c_bg", 2), ("c_wg", 256),
               ("out_gain", KT), ("a_lam", 128), ("d_sink", 4), ("lam_init", 2)]:
    PAR[_n] = (_at, _at + _w)
    _at += _w
NPAR = _at

CST = {}
_at = 0
for _n, _w in [("ident", P), ("neg", 2 * P), ("band", 2 * P), ("cos_a", NT * 32), ("sin_a", NT * 32),
               ("cos_d", NT * 64), ("sin_d", NT * 64), ("sel_row", 8 * P), ("sel_pair", 4 * P),
               ("sel_mod", 2 * P), ("ones", P), ("diag", GW), ("pick", 6 * P)]:
    CST[_n] = (_at, _at + _w)
    _at += _w
NCST = _at


class Signal:

    def __init__(self, sem):
        self.sem, self.n = sem, 0

    def mark(self, ins, by=1):
        ins.then_inc(self.sem, by)
        self.n += by
        return self.n

    def link(self, eng, ins):
        self.mark(ins)
        eng.wait_ge(self.sem, self.n)


def layer_program(nc, dram):
    ctx = ExitStack()
    with ctx:
        def keep(name, shape, dt=F32):
            return ctx.enter_context(nc.sbuf_tensor(name, shape, dt))

        def signal(name):
            s = stage_ctx[-1].enter_context(nc.semaphore(name, num=first_free + len(stage_sems)))
            stage_sems.append(s)
            return Signal(s)

        stage_ctx, stage_sems = [], []
        ps = ctx.enter_context(nc.psum_tensor("ps", [P, 8, BANK], F32))
        hT = keep("hT", [P, KT, T])
        yT = keep("yT", [P, KT, T])
        ring = keep("ring", [P, RING, KT * 512])
        gate_rows = keep("gate_rows", [P, 2, D])
        par = keep("par", [P, NPAR])
        cst = keep("cst", [P, NCST])
        csil = keep("csil", [P, KT, 2])
        setup_sem = [Signal(ctx.enter_context(nc.semaphore(n))) for n in ("const_loaded", "setup_act", "setup_dve")]

        loaded = [Signal(ctx.enter_context(nc.semaphore(f"slab{i}_loaded"))) for i in range(NSLAB)]
        slab_used = Signal(ctx.enter_context(nc.semaphore("slab_used")))
        first_free = slab_used.sem.num + 1
        env = dict(nc=nc, ps=ps, hT=hT, yT=yT, ring=ring, gate_rows=gate_rows, par=par, cst=cst,
                   csil=csil, mod_cols=keep("mod_cols", [P, 2, KT, 2]), loaded=loaded, slab_used=slab_used,
                   signal=signal, dram=dram)
        setup(nc, env, setup_sem)
        with nc.Fori(0, DEPTH) as layer:
            env["layer"] = layer
            for stage in (stage_modulation, stage_norm, stage_mlstm, stage_gla, stage_diff_attention,
                          stage_window_attention, stage_gates, stage_output):
                with ExitStack() as own:
                    stage_ctx.append(own)
                    stage(nc, env)
                    first = loaded[0].sem.num if stage is stage_output else first_free
                    nc.all_engine_barrier(sems_to_clear=range(first, first_free + len(stage_sems)))
                stage_sems.clear()


def C(env, name, rows=P):
    a, b = CST[name]
    return env["cst"][0:rows, a:b]


def W(env, name, rows=P):
    a, b = PAR[name]
    return env["par"][0:rows, a:b]


def slab(env, i):
    w = SLAB_W[i]
    return env["ring"][:, i % RING, 0:KT * w].rearrange("p (k n) -> p k n", k=KT)


def load_slabs(sp, env, first, last):
    for i in range(first, last):
        if i >= RING:
            sp.wait_ge(env["slab_used"].sem, i - RING + 1)
        src = env["dram"]["w"][bass.ds(env["layer"] * P, P), SLAB_AT[i]:SLAB_AT[i + 1]]
        sp.dma_start(env["ring"][:, i % RING, 0:KT * SLAB_W[i]], src).then_inc(env["loaded"][i].sem, 16)


def rsqrt_newton(dve, sig, y, x, t):
    sig.link(dve, dve.tensor_tensor(t, y, y, ALU.mult))
    sig.link(dve, dve.tensor_tensor(t, t, x, ALU.mult))
    sig.link(dve, dve.tensor_scalar(t, t, -0.5, 1.5, ALU.mult, ALU.add))
    sig.link(dve, dve.tensor_tensor(y, y, t, ALU.mult))


def setup(nc, env, sems):
    dram = env["dram"]
    const_loaded, act_done, dve_done = sems
    with ExitStack() as own, nc.Block() as block:
        craw = own.enter_context(nc.sbuf_tensor("craw", [P, KT, 2], F32))
        csig = own.enter_context(nc.sbuf_tensor("csig", [P, KT, 2], F32))

        @block.sync
        def _(sp):
            sp.dma_start(env["cst"][:, :], dram["cst"][:, :]).then_inc(const_loaded.sem, 16)
            sp.dma_start(craw[:, :, :], dram["c"].rearrange("p (k c) -> p k c", k=KT)).then_inc(const_loaded.sem, 16)
            sp.dma_start(dram["ctx_now"][:, :], dram["tok"][0:CTX, :]).then_inc(const_loaded.sem, 16)
            sp.dma_start(dram["out"][:, :], dram["tok"][CTX:T, :]).then_inc(const_loaded.sem, 16)
            sp.wait_ge(const_loaded.sem, 64)

        @block.scalar
        def _(act):
            act.wait_ge(const_loaded.sem, 64)
            act.activation(csig[:, :, :], craw[:, :, :], ACT.Sigmoid).then_inc(act_done.sem, 1)

        @block.vector
        def _(dve):
            dve.wait_ge(act_done.sem, 1)
            dve.tensor_tensor(env["csil"][:, :, :], craw[:, :, :], csig[:, :, :], ALU.mult)\
               .then_inc(dve_done.sem, 1)
            dve.wait_ge(dve_done.sem, 1)


def stage_modulation(nc, env):
    ps, signal = env["ps"], env["signal"]
    par_loaded, mm, ev, tr, dv, gate_mm, gate_ev = (
        signal(n) for n in ("par_loaded", "mod_product", "mod_rows", "mod_turned", "mod_dve", "gate_spread", "gate_kept"))
    own = ExitStack()
    mod_cols = env["mod_cols"]
    rowsx = env["yT"][:, :, :].rearrange("p k t -> p (k t)").rearrange("p (t d) -> p t d", t=NT)
    junk = env["hT"][:, :, :].rearrange("p k t -> p (k t)").rearrange("p (t d) -> p t d", t=NT)
    x_loaded = [signal(f"x{t}_loaded") for t in range(NT)]
    squares, ms_ready, root, rstd_ready, scaled_a, scaled_d, norm_dv = (
        signal(n) for n in ("x_squares", "x_mean", "x_root", "x_rstd", "x_scaled_act", "x_scaled_dve", "norm_dve"))
    with own, nc.Block() as block:
        small = own.enter_context(nc.sbuf_tensor("x_stats", [P, 4, NT], F32))
        ss, ms, rstd, tmp = (small[:, i, :] for i in range(4))
        rows = own.enter_context(nc.sbuf_tensor("mod_row", [2, 3 * D], F32))

        @block.sync
        def _(sp):
            sp.dma_start(env["par"][:, :], env["dram"]["par"][bass.ds(env["layer"] * P, P), :])\
              .then_inc(par_loaded.sem, 16)
            load_slabs(sp, env, 0, 2)
            for t in range(NT):
                src = env["dram"]["ctx_now"][t * P:(t + 1) * P, :] if t < NC else \
                    env["dram"]["out"][(t - NC) * P:(t - NC + 1) * P, :]
                sp.dma_start(rowsx[:, t, :], src).then_inc(x_loaded[t].sem, 16)
            load_slabs(sp, env, 2, 8)
            sp.wait_ge(par_loaded.sem, 16)

        @block.tensor
        def _(pe):
            for s in range(6):
                pe.wait_ge(env["loaded"][s].sem, 16)
                if s >= 2:
                    pe.wait_ge(ev.sem, s - 1)
                for k in range(KT):
                    last = pe.matmul(ps[0:2, s % 2, :], env["csil"][:, k, :], slab(env, s)[:, k, :],
                                     start=k == 0, stop=k == KT - 1)
                last.then_inc(mm.sem, 1)
                pe.wait_ge(mm.sem, s + 1)
                pe.sem_inc(env["slab_used"].sem, 1)
            pe.wait_ge(ev.sem, 4)
            for i in range(2 * KT):
                last = pe.transpose(ps[:, 2, 2 * i:2 * i + 2], rows[:, i * P:(i + 1) * P], C(env, "ident")[0:2, 0:2])
            last.then_inc(tr.sem, 1)
            pe.wait_ge(dv.sem, 1)
            sel = C(env, "sel_mod", 2).rearrange("p (a b) -> p a b", a=2)
            for v in range(2):
                for n in range(2):
                    last = pe.matmul(ps[:, 3 + 2 * v + n, :], sel[:, v, :], rows[:, 2 * D + n * 512:2 * D + (n + 1) * 512],
                                     start=True, stop=True)
                    last.then_inc(gate_mm.sem, 1)

        @block.scalar
        def _(act):
            def keep_rows(s):
                act.wait_ge(mm.sem, s + 1)
                act.activation(rows[:, s * 512:(s + 1) * 512], ps[0:2, s % 2, :], ACT.Copy).then_inc(ev.sem, 1)

            keep_rows(0)
            for t in range(NT):
                act.wait_ge(x_loaded[t].sem, 16)
                act.activation(junk[:, t, :], rowsx[:, t, :], ACT.Square, accum_out=ss[:, t:t + 1]).then_inc(squares.sem, 1)
                if t == 4:
                    keep_rows(1)
            keep_rows(2)
            act.wait_ge(ms_ready.sem, 1)
            root.link(act, act.activation(rstd, ms, ACT.Ln))
            root.mark(act.activation(rstd, rstd, ACT.Exp, scale=-0.5))
            keep_rows(3)
            act.wait_ge(rstd_ready.sem, 1)
            for t in range(0, NT, 2):
                act.activation(rowsx[:, t, :], rowsx[:, t, :], ACT.Copy, scale=rstd[:, t:t + 1]).then_inc(scaled_a.sem, 1)
            keep_rows(4)
            keep_rows(5)
            act.wait_ge(scaled_a.sem, NT // 2)
            for i in range(4):
                act.wait_ge(gate_mm.sem, i + 1)
                act.activation(env["gate_rows"][:, i // 2, (i % 2) * 512:(i % 2 + 1) * 512], ps[:, 3 + i, :], ACT.Copy)\
                   .then_inc(gate_ev.sem, 1)
            act.wait_ge(gate_ev.sem, 4)

        @block.vector
        def _(dve):
            dve.wait_ge(squares.sem, NT)
            dve.tensor_scalar(ms, ss, 1.0 / D, EPS, ALU.mult, ALU.add).then_inc(ms_ready.sem, 1)
            dve.wait_ge(root.sem, 2)
            rsqrt_newton(dve, norm_dv, rstd, ms, tmp)
            dve.sem_inc(rstd_ready.sem, 1)
            for t in range(1, NT, 2):
                dve.tensor_scalar(rowsx[:, t, :], rowsx[:, t, :], rstd[:, t:t + 1], None, ALU.mult)\
                   .then_inc(scaled_d.sem, 1)
            dve.wait_ge(scaled_d.sem, NT // 2)
            dve.wait_ge(par_loaded.sem, 16)
            dve.wait_ge(ev.sem, 6)
            dv.mark(dve.tensor_tensor(rows[:, 2 * D:], rows[:, 2 * D:], W(env, "b_gt", 2), ALU.add))
            dve.wait_ge(tr.sem, 1)
            turned = ps[:, 2, 0:4 * KT].rearrange("p (s k v) -> p s k v", s=2, k=KT)
            for s, b in ((0, "b_sh"), (1, "b_sc")):
                dv.link(dve, dve.tensor_tensor(mod_cols[:, s, :, :], turned[:, s, :, :],
                                               W(env, b).unsqueeze(2).broadcast_to([P, KT, 2]), ALU.add))
            dv.link(dve, dve.tensor_scalar(mod_cols[:, 1, :, :], mod_cols[:, 1, :, :], 1.0, None, ALU.add))
            dv.link(dve, dve.tensor_tensor(mod_cols[:, 1, :, :], mod_cols[:, 1, :, :],
                                           W(env, "norm_g").unsqueeze(2).broadcast_to([P, KT, 2]), ALU.mult))
            dv.link(dve, dve.tensor_scalar(W(env, "out_gain")[:, 0:2], W(env, "out_gain")[:, 0:2],
                                           W(env, "lam_init")[:, 1:2], None, ALU.mult))


def stage_norm(nc, env):
    ps, signal, hT = env["ps"], env["signal"], env["hT"]
    rowsx = env["yT"][:, :, :].rearrange("p k t -> p (k t)").rearrange("p (t d) -> p t d", t=NT)
    turned, kept_a, kept_d = (signal(n) for n in ("x_turned", "h_kept_act", "h_kept_dve"))
    mod_cols = env["mod_cols"]
    groups = [(0, 0, 2), (1, 2, 4), (1, 6, 4)]
    jobs = [(k, g) for g in groups for k in range(KT)]
    with nc.Block() as block:
        @block.scalar
        def _(act):
            for n, (k, (v, t0, m)) in enumerate(jobs):
                if n % 2 == 0:
                    act.wait_ge(turned.sem, n + 1)
                    act.activation(hT[:, k, t0 * P:(t0 + m) * P], ps[:, n % 4, 0:m * P], ACT.Identity,
                                   bias=mod_cols[:, 0, k, v:v + 1], scale=mod_cols[:, 1, k, v:v + 1]).then_inc(kept_a.sem, 1)

        @block.vector
        def _(dve):
            for n, (k, (v, t0, m)) in enumerate(jobs):
                if n % 2 == 1:
                    dve.wait_ge(turned.sem, n + 1)
                    dve.tensor_scalar(hT[:, k, t0 * P:(t0 + m) * P], ps[:, n % 4, 0:m * P],
                                      mod_cols[:, 1, k, v:v + 1], mod_cols[:, 0, k, v:v + 1], ALU.mult, ALU.add)\
                       .then_inc(kept_d.sem, 1)

        @block.tensor
        def _(pe):
            for n, (k, (v, t0, m)) in enumerate(jobs):
                if n >= 4:
                    pe.wait_ge((kept_a if n % 2 == 0 else kept_d).sem, (n - 4) // 2 + 1)
                for t in range(t0, t0 + m):
                    last = pe.transpose(ps[:, n % 4, (t - t0) * P:(t - t0 + 1) * P],
                                        rowsx[:, t, k * P:(k + 1) * P], C(env, "ident"))
                last.then_inc(turned.sem, 1)


def split_weights(dve, w, hi, lo, sig):
    sig.link(dve, dve.tensor_copy(hi, w))
    return dve.tensor_tensor(lo, w, hi.bitcast(F32), ALU.subtract)


class SplitProduct:

    def __init__(self, nc, env, own, name, groups, bufs=2):
        self.env, self.groups, self.BUFS = env, groups, bufs
        self.steps = [(g, k) for g in range(len(groups)) for k in range(KT)]
        self.first = [sum(len(q[5]) for q in groups[:g]) for g in range(len(groups) + 1)]
        self.hi, self.lo, self.weights, self.dv, self.used, self.ready, self.read = (
            env["signal"](f"{name}_{n}") for n in ("x_hi", "x_lo", "w_parts", "split", "parts_used", "sum_ready", "sum_read"))
        toks, cols = max(q[4] for q in groups), max(q[2] for q in groups)
        part = lambda n, width: own.enter_context(nc.sbuf_tensor(f"{name}_{n}", [P, self.BUFS, width], F32R))
        self.x_hi, self.x_lo = part("xh", toks), part("xl", toks)
        self.w_hi, self.w_lo = part("wh", cols), part("wl", cols)

    def wait_used(self, engine, i):
        g, k = self.steps[i]
        if k == KT - 1:
            engine.wait_ge(self.ready.sem, self.first[g + 1])
        else:
            engine.wait_ge(self.used.sem, (KT - 1) * g + k + 1)

    def high(self, act, i):
        g, k = self.steps[i]
        _, _, _, t0, m, _ = self.groups[g]
        if i >= self.BUFS:
            self.wait_used(act, i - self.BUFS)
        act.activation(self.x_hi[:, i % self.BUFS, 0:m], self.env["hT"][:, k, t0:t0 + m], ACT.Copy).then_inc(self.hi.sem, 1)

    def low(self, dve, i):
        g, k = self.steps[i]
        s, c0, w, t0, m, _ = self.groups[g]
        at = i % self.BUFS
        if k == 0 and (g == 0 or self.groups[g - 1][0] != s):
            dve.wait_ge(self.env["loaded"][s].sem, 16)
        if i >= self.BUFS:
            self.wait_used(dve, i - self.BUFS)
        split_weights(dve, slab(self.env, s)[:, k, c0:c0 + w], self.w_hi[:, at, 0:w], self.w_lo[:, at, 0:w], self.dv)\
            .then_inc(self.weights.sem, 1)
        if k == KT - 1 and (g + 1 == len(self.groups) or self.groups[g + 1][0] != s):
            dve.wait_ge(self.weights.sem, i + 1)
            dve.sem_inc(self.env["slab_used"].sem, 1)
        dve.wait_ge(self.hi.sem, i + 1)
        dve.tensor_tensor(self.x_lo[:, at, 0:m], self.env["hT"][:, k, t0:t0 + m], self.x_hi[:, at, 0:m].bitcast(F32),
                          ALU.subtract).then_inc(self.lo.sem, 1)

    def multiply(self, pe, i, banks=8):
        g, k = self.steps[i]
        sums, at = self.groups[g][5], i % self.BUFS
        pe.wait_ge(self.hi.sem, i + 1)
        pe.wait_ge(self.weights.sem, i + 1)
        pe.wait_ge(self.lo.sem, i + 1)
        for a, (channels, cols, toks, rows, width) in enumerate(sums):
            n = self.first[g] + a
            if k == 0 and n >= banks:
                pe.wait_ge(self.read.sem, n - banks + 1)
            out = self.env["ps"][0:rows, n % banks, 0:width]
            w = [self.w_hi[:, at, cols], self.w_lo[:, at, cols]]
            x = [self.x_hi[:, at, toks], self.x_lo[:, at, toks]]
            for j, (p, q) in enumerate(((0, 0), (0, 1), (1, 0))):
                left, right = (w[p], x[q]) if channels else (x[p], w[q])
                last = pe.matmul(out, left, right, start=k == 0 and j == 0, stop=k == KT - 1 and j == 2)
            if k == KT - 1:
                last.then_inc(self.ready.sem, 1)
        if k < KT - 1:
            last.then_inc(self.used.sem, 1)


def channel_sums(chunks, blocks):
    t0 = blocks[0][0]
    return [(True, slice(c * P, (c + 1) * P), slice(b[0] - t0, b[0] - t0 + b[1]), P, b[1]) for c in range(chunks) for b in blocks]


def token_sums(cols, tiles):
    return [(False, slice(0, cols), slice(a * P, (a + 1) * P), P, cols) for a in range(tiles)]


def scan_order(way):
    return list(range(NT)) if way == 0 else list(range(NC - 1, -1, -1)) + list(range(NT - 1, NC - 1, -1))


UNITS = [(way, i, scan_order(way)[i]) for i in range(NT) for way in range(2)]


def second_visit(u):
    return any(UNITS[n][2] == UNITS[u][2] for n in range(u))


def stage_mlstm(nc, env):
    ps, signal, yT, ring = (env[n] for n in ("ps", "signal", "yT", "ring"))
    outer = ExitStack()
    with outer:
        v1 = outer.enter_context(nc.sbuf_tensor("b_v", [P, NT, HEADS, DH + 1], F32))
        qkT = outer.enter_context(nc.sbuf_tensor("b_qkT", [P, 4, T], F32))
        after = lambda s_, n: ring[:, s_ % RING, KT * SLAB_W[s_]:KT * SLAB_W[s_] + n]
        cols = after(S_CV, NT * 4 * ROWS).rearrange("p (t q r) -> p t q r", t=NT, q=4)
        row_d = after(S_CQK, T)[0:ROWS, :]
        row_a, row_c, row_e, row_b = (yT[0:ROWS, i, :] for i in range(4))
        ends = outer.enter_context(nc.sbuf_tensor("b_ends", [ROWS, 4, NT], F32))
        decay = outer.enter_context(nc.sbuf_tensor("b_decay", [P, 4, NT], F32))
        conv_in = yT[:, 4:8, :]
        ktm = yT[:, 4:6, :].rearrange("p a t -> p (a t)").rearrange("p (t c) -> p t c", t=NT)
        hB = yT[:, 0:2, :].rearrange("p a t -> p (a t)").rearrange("p (t h d) -> p t h d", t=NT, h=HEADS)
        gt = yT[:, 4, 0:NT * 2 * ROWS].rearrange("p (t r) -> p t r", t=NT)
        q_of = [yT[:, 6 + h // 2, :] if h % 2 else qkT[:, h // 2, :] for h in range(HEADS)]

        act_s, act_l, dv, conv_ready, silu_ready, gates_turned, gates_kept, rows_ready, turned, turned_kept, dec_ready, v_ones, q_moved, q_cleared = (
            signal(n) for n in ("b_sigmoid", "b_logs", "b_dve", "b_conv", "b_silu", "b_gates_turned", "b_gates_kept",
                                "b_rows", "b_turned", "b_turned_kept", "b_dec", "b_ones", "b_q_moved", "b_q_cleared"))
        HT = T // 2
        WV = GW + 2 * ROWS
        groups = [(S_BV, 0, WV, h * HT, HT, token_sums(WV, NT // 2)) for h in range(2)] + \
            [(S_BQK, c0, GW, 0, T, channel_sums(2, BLOCKS)) for c0 in (GW, 0)]
        BANKS = 6

        with ExitStack() as own, nc.Block() as block:
            proj = SplitProduct(nc, env, own, "b_proj", groups)
            chunked = [r.rearrange("p (c t) -> p c t", c=NT) for r in (row_a, row_b, row_c, row_d, row_e)]

            @block.sync
            def _(sp):
                load_slabs(sp, env, 8, 10)

            @block.gpsimd
            def _(pool):
                pool.memset(v1[:, :, :, DH:DH + 1], 1.0).then_inc(v_ones.sem, 1)
                pool.wait_ge(v_ones.sem, 1)
                pool.memset(yT[:, 3, :], 0.0).then_inc(v_ones.sem, 1)
                pool.wait_ge(v_ones.sem, 2)
                pool.wait_ge(silu_ready.sem, 2)
                pool.memset(yT[0:64, 6:8, :], 0.0).then_inc(q_cleared.sem, 1)
                pool.wait_ge(q_cleared.sem, 1)
                for c in range(2):
                    pool.wait_ge(act_s.sem, 3 + c)
                    pool.tensor_tensor(yT[64:P, 6 + c, :], qkT[64:P, c, :], conv_in[64:P, c, :], ALU.mult).then_inc(q_moved.sem, 1)
                    pool.wait_ge(q_moved.sem, c + 1)
                    pool.memset(qkT[64:P, c, :], 0.0).then_inc(q_cleared.sem, 1)
                    pool.wait_ge(q_cleared.sem, c + 2)

            @block.tensor
            def _(pe):
                def turn_gates(n):
                    b = BLOCKS[n]
                    if n == 0:
                        pe.wait_ge(proj.read.sem, NT)
                    else:
                        pe.wait_ge(gates_kept.sem, 2 * n)
                    for i in range(2):
                        for t in range(b[0] // P, (b[0] + b[1]) // P):
                            last = pe.transpose(ps[0:ROWS, 6 + i, t * P - b[0]:(t + 1) * P - b[0]],
                                                gt[:, t, i * ROWS:(i + 1) * ROWS], C(env, "ident"))
                    last.then_inc(gates_turned.sem, 1)

                for i, (g, k) in enumerate(proj.steps):
                    proj.multiply(pe, i, BANKS)
                    if g == 2 and k in (1, 2, 3):
                        turn_gates(k - 1)
                pe.wait_ge(proj.read.sem, proj.first[-1])
                pe.wait_ge(rows_ready.sem, 1)
                for t in range(NT):
                    for q, r in enumerate((row_a, row_c, row_d, row_e)):
                        at = (t % 3) * 4 * ROWS + q * ROWS
                        last = pe.transpose(ps[:, 4 + t // 3, at:at + ROWS], r[:, t * P:(t + 1) * P],
                                            C(env, "ident")[0:ROWS, 0:ROWS])
                last.then_inc(turned.sem, 1)
                pe.wait_ge(dec_ready.sem, 1)
                sel = C(env, "sel_pair", ROWS).rearrange("p (a b) -> p a b", a=4)
                for i in range(4):
                    last = pe.matmul(ps[:, 0, i * NT:(i + 1) * NT], sel[:, i, :], ends[:, 3, :], start=True, stop=True)
                last.then_inc(turned.sem, 1)
                pe.wait_ge(silu_ready.sem, 4)
                pe.wait_ge(q_moved.sem, 2)
                for t in range(NT):
                    if t == 0:
                        pe.wait_ge(turned_kept.sem, 17)
                    if t >= 4:
                        pe.wait_ge(turned_kept.sem, 17 + t - 3)
                    for c in range(2):
                        last = pe.transpose(ps[:, t % 4, c * P:(c + 1) * P], qkT[:, 2 + c, t * P:(t + 1) * P], C(env, "ident"))
                    last.then_inc(turned.sem, 1)

            @block.scalar
            def _(act):
                def keep(n):
                    act.wait_ge(proj.ready.sem, n + 1)
                    bank = ps[:, n % BANKS, :]
                    if n < NT:
                        act.activation(v1[:, n, :, 0:DH], bank[:, 0:GW].rearrange("p (h d) -> p h d", h=HEADS), ACT.Copy)
                        ins = act.activation(gt[:, n, :], bank[:, GW:WV], ACT.Copy)
                    else:
                        c, b = (2, 3, 0, 1)[(n - NT) // 3], BLOCKS[(n - NT) % 3]
                        if n == NT:
                            act.wait_ge(gates_turned.sem, 3)
                        ins = act.activation(conv_in[:, c, b[0]:b[0] + b[1]], bank[:, 0:b[1]], ACT.Copy)
                    ins.then_inc(proj.read.sem, 1)

                def keep_gates(n):
                    b = BLOCKS[n]
                    if n == 0:
                        act.wait_ge(v_ones.sem, 2)
                    act.wait_ge(gates_turned.sem, n + 1)
                    for i, (row, gate) in enumerate(((row_a, "li"), (row_b, "lf"))):
                        act.activation(row[:, b[0]:b[0] + b[1]], ps[0:ROWS, 6 + i, 0:b[1]], ACT.Identity,
                                       bias=W(env, "gate_" + gate, ROWS)).then_inc(gates_kept.sem, 1)

                def sigmoid(c):
                    act.wait_ge(conv_ready.sem, (2, 3, 0, 1).index(c) + 1)
                    act.activation(conv_in[:, c, :], qkT[:, c, :], ACT.Sigmoid).then_inc(act_s.sem, 1)

                for i, (g, k) in enumerate(proj.steps):
                    proj.high(act, i)
                    if g >= 1 and k == 1:
                        for n in range(proj.first[g - 1], proj.first[g]):
                            keep(n)
                    if g == 2 and k in (2, 3, 4):
                        keep_gates(k - 2)
                    if g == 2 and k == 5:
                        act.wait_ge(gates_kept.sem, 6)
                        act_l.link(act, act.activation(row_c, row_b, ACT.Abs))
                        act_l.link(act, act.activation(row_c, row_c, ACT.Exp, scale=-1.0))
                        act_l.mark(act.activation(row_c, row_c, ACT.Ln, bias=1.0))
                    if g == 3 and k in (4, 6):
                        sigmoid(2 if k == 4 else 3)
                for n in range(proj.first[-2], proj.first[-1]):
                    keep(n)
                for c in range(2):
                    sigmoid(c)
                act.wait_ge(rows_ready.sem, 1)
                act.activation(ends[:, 3, :], ends[:, 3, :], ACT.Exp).then_inc(dec_ready.sem, 1)
                act.wait_ge(turned.sem, 1)
                for b in range(4):
                    m = min(3, NT - 3 * b)
                    src = ps[:, 4 + b, 0:m * 4 * ROWS].rearrange("p (t q r) -> p t q r", t=m, q=4)
                    for q, (f, scale) in enumerate(((ACT.Copy, 1.0), (ACT.Exp, 1.0), (ACT.Exp, -1.0), (ACT.Exp, 1.0))):
                        act.activation(cols[:, 3 * b:3 * b + m, q, :], src[:, :, q, :], f, scale=scale)\
                           .then_inc(turned_kept.sem, 1)
                act.wait_ge(turned.sem, 2)
                act.activation(decay[:, :, :], ps[:, 0, 0:4 * NT].rearrange("p (a b) -> p a b", a=4), ACT.Copy)\
                   .then_inc(turned_kept.sem, 1)
                for t in range(NT):
                    act.wait_ge(turned.sem, 2 + t + 1)
                    act.activation(ktm[:, t, :], ps[:, t % 4, 0:GW], ACT.Copy).then_inc(turned_kept.sem, 1)
                act.wait_ge(turned_kept.sem, NT + 17)

            @block.vector
            def _(dve):
                cw = W(env, "conv_w").rearrange("p (c j) -> p c j", c=4)

                def convolve(c):
                    dve.wait_ge(proj.read.sem, NT + 3 * ((2, 3, 0, 1).index(c) + 1))
                    y, x = qkT[:, c, :], conv_in[:, c, :]
                    dv.link(dve, dve.tensor_scalar(y, x, cw[:, c, 1:2], W(env, "conv_b")[:, c:c + 1], ALU.mult, ALU.add))
                    for a, b in ((0, CTX), (CTX, T)):
                        dv.link(dve, dve.scalar_tensor_tensor(out=y[:, a + 1:b], in0=x[:, a:b - 1], scalar=cw[:, c, 0:1],
                                                              in1=y[:, a + 1:b], op0=ALU.mult, op1=ALU.add))
                        ins = dve.scalar_tensor_tensor(out=y[:, a:b - 1], in0=x[:, a + 1:b], scalar=cw[:, c, 2:3],
                                                       in1=y[:, a:b - 1], op0=ALU.mult, op1=ALU.add)
                        dv.link(dve, ins)
                    dve.sem_inc(conv_ready.sem, 1)

                def gate_sums():
                    dve.wait_ge(act_l.sem, 3)
                    dv.link(dve, dve.scalar_tensor_tensor(out=row_b, in0=row_b, scalar=0.0, in1=row_c,
                                                          op0=ALU.min, op1=ALU.subtract))
                    ones = C(env, "ones")
                    dv.mark(dve.memset(row_d, 0.0))
                    dv.link(dve, dve.memset(ends[:, :, :], 0.0))
                    for t in range(NT):
                        a, b = t * P, (t + 1) * P
                        dv.mark(dve.tensor_tensor_scan(row_c[0:HEADS, a:b], ones[0:HEADS, :], row_b[0:HEADS, a:b],
                                                       0.0, ALU.mult, ALU.add))
                        dv.mark(dve.tensor_tensor_scan(row_c[32:ROWS, a:b][:, ::-1], ones[32:ROWS, :],
                                                       row_b[32:ROWS, a:b][:, ::-1], 0.0, ALU.mult, ALU.add))

                def gate_rows():
                    dv.mark(dve.tensor_tensor_scan(row_d[0:HEADS, :], row_b[0:HEADS, :], row_a[0:HEADS, :], 0.0,
                                                   ALU.add, ALU.max))
                    dv.link(dve, dve.tensor_tensor_scan(row_d[32:ROWS, 0:CTX][:, ::-1], row_b[32:ROWS, 0:CTX][:, ::-1],
                                                        row_a[32:ROWS, 0:CTX][:, ::-1], 0.0, ALU.add, ALU.max))
                    dv.link(dve, dve.tensor_tensor_scan(row_d[32:ROWS, CTX:T][:, ::-1], row_b[32:ROWS, CTX:T][:, ::-1],
                                                        row_a[32:ROWS, CTX:T][:, ::-1], row_d[32:ROWS, 0:1], ALU.add, ALU.max))
                    cc, cd = chunked[2], chunked[3]
                    for r, at in ((slice(0, HEADS), P - 1), (slice(32, ROWS), 0)):
                        dv.mark(dve.tensor_copy(ends[r, 0, :].unsqueeze(2), cc[r, :, at:at + 1]))
                        dv.link(dve, dve.tensor_copy(ends[r, 1, :].unsqueeze(2), cd[r, :, at:at + 1]))
                    dv.mark(dve.tensor_copy(ends[0:HEADS, 2, 1:NT], ends[0:HEADS, 1, 0:NT - 1]))
                    dv.mark(dve.tensor_copy(ends[32:ROWS, 2, 0:1], ends[32:ROWS, 1, 1:2]))
                    dv.mark(dve.tensor_copy(ends[32:ROWS, 2, NT - 1:NT], ends[32:ROWS, 1, 0:1]))
                    dv.link(dve, dve.tensor_copy(ends[32:ROWS, 2, NC:NT - 1], ends[32:ROWS, 1, NC + 1:NT]))
                    dv.link(dve, dve.tensor_tensor(ends[:, 0, :], ends[:, 0, :], ends[:, 1, :], ALU.subtract))
                    dv.link(dve, dve.tensor_tensor(ends[:, 3, :], ends[:, 0, :], ends[:, 2, :], ALU.add))
                    wide = lambda i: ends[:, i, :].unsqueeze(2).broadcast_to([ROWS, NT, P])
                    dv.link(dve, dve.tensor_tensor(row_a, row_a, row_c, ALU.subtract))
                    dv.link(dve, dve.tensor_tensor(row_b, row_c, row_d, ALU.subtract))
                    dv.mark(dve.tensor_tensor(chunked[2], chunked[1], wide(2), ALU.add))
                    dv.link(dve, dve.tensor_tensor(chunked[4], chunked[0], wide(0), ALU.add))
                    dve.sem_inc(rows_ready.sem, 1)

                def silu_k(c):
                    dve.wait_ge(act_s.sem, c - 1)
                    dve.scalar_tensor_tensor(out=qkT[:, c, :], in0=qkT[:, c, :], scalar=DH ** -0.5,
                                             in1=conv_in[:, c, :], op0=ALU.mult, op1=ALU.mult).then_inc(silu_ready.sem, 1)

                for i, (g, k) in enumerate(proj.steps):
                    proj.low(dve, i)
                    if (g, k) == (2, 6):
                        gate_sums()
                    if (g, k) == (3, 0):
                        gate_rows()
                    if g == 3 and k in (2, 4):
                        convolve(2 if k == 2 else 3)
                    if g == 3 and k in (5, 7):
                        silu_k(2 if k == 5 else 3)
                for c in range(2):
                    convolve(c)
                for c in range(2):
                    dve.wait_ge(act_s.sem, 3 + c)
                    dve.tensor_tensor(qkT[0:64, c, :], qkT[0:64, c, :], conv_in[0:64, c, :], ALU.mult).then_inc(silu_ready.sem, 1)
                dve.wait_ge(silu_ready.sem, 4)

        (d_mm, s_mm, dm_ready, w_ready, sw_ready, u_mm, intra_mm, vw_ready, dv2, finished, zeroed) = (
            signal(n) for n in ("b_logs_mm", "b_scores_mm", "b_logw", "b_weight", "b_weighted", "b_new_mm",
                                "b_intra_mm", "b_vw", "b_dve2", "b_state", "b_zeroed"))
        with ExitStack() as own, nc.Block() as block:
            def tile(name, shape):
                return own.enter_context(nc.sbuf_tensor(name, shape, F32))

            logw = tile("b_logw", [P, HEADS, P])
            wgt = tile("b_wgt", [P, HEADS, P])
            sw = tile("b_sw", [P, HEADS, P])
            vw = tile("b_vw", [P, 2, HEADS, DH + 1])
            state = tile("b_state", [P, 2, 2, DH + 1])
            tmp = tile("b_tmp", [P, HEADS, DH + 1])
            num = tile("b_num", [P, HEADS, DH + 1])
            den = tile("b_den", [P, HEADS])
            neg = C(env, "neg").rearrange("p (a b) -> p a b", a=2)
            sel = C(env, "sel_row").rearrange("p (a b) -> p a b", a=8)
            NU = len(UNITS)

            def col(j, q, way):
                return cols[:, j, q, 32 * way:32 * way + HEADS]

            @block.gpsimd
            def _(pool):
                for u, (way, i, j) in enumerate(UNITS):
                    if u >= 2:
                        pool.wait_ge(u_mm.sem, u - 1)
                    pool.tensor_tensor(vw[:, u % 2, :, :], v1[:, j, :, :],
                                       col(j, 3, way).unsqueeze(2).broadcast_to([P, HEADS, DH + 1]), ALU.mult)\
                        .then_inc(vw_ready.sem, 1)

            @block.tensor
            def _(pe):
                def logs(u):
                    way, i, j = UNITS[u]
                    if u >= 2:
                        pe.wait_ge(dm_ready.sem, HEADS * (u - 1))
                    for h in range(HEADS):
                        last = pe.matmul(ps[:, u % 2, h * P:(h + 1) * P], sel[:, way * HEADS + h, :],
                                         yT[:, 3, j * P:(j + 1) * P], start=True, stop=True)
                    last.then_inc(d_mm.sem, 1)

                def scores(u):
                    j = UNITS[u][2]
                    t0, t1 = j * P, (j + 1) * P
                    if u >= 2:
                        pe.wait_ge(sw_ready.sem, u - 1)
                    for h in range(HEADS):
                        last = pe.matmul(ps[:, 2 + u % 2, h * P:(h + 1) * P], qkT[:, 2 + h // 2, t0:t1], q_of[h][:, t0:t1],
                                         start=True, stop=True)
                    last.then_inc(s_mm.sem, 1)

                logs(0)
                scores(0)
                for u, (way, i, j) in enumerate(UNITS):
                    t0, t1 = j * P, (j + 1) * P
                    if u + 1 < NU:
                        logs(u + 1)
                        scores(u + 1)
                    if u == 0:
                        pe.wait_ge(zeroed.sem, 1)
                    if u >= 2:
                        pe.wait_ge(finished.sem, u - 1)
                    for h in range(HEADS):
                        pe.matmul(ps[:, 5 + 2 * (u % 2), h * (DH + 1):(h + 1) * (DH + 1)], q_of[h][:, t0:t1],
                                  state[:, way, h // 2, :], start=True, stop=True)
                    pe.wait_ge(vw_ready.sem, u + 1)
                    for h in range(HEADS):
                        r = slice(64 * (h % 2), 64 * (h % 2) + 64)
                        a = (HEADS + h // 2) * (DH + 1)
                        last = pe.matmul(ps[r, 5 + 2 * (u % 2), a:a + DH + 1], ktm[:, j, h * DH:(h + 1) * DH],
                                         vw[:, u % 2, h, :], start=True, stop=True)
                    last.then_inc(u_mm.sem, 1)
                    pe.wait_ge(sw_ready.sem, u + 1)
                    for h in range(HEADS):
                        last = pe.matmul(ps[:, 4 + 2 * (u % 2), h * (DH + 1):(h + 1) * (DH + 1)], sw[:, h, :], v1[:, j, h, :],
                                         start=True, stop=True)
                    last.then_inc(intra_mm.sem, 1)

            @block.scalar
            def _(act):
                for u in range(NU):
                    act.wait_ge(dm_ready.sem, HEADS * (u + 1))
                    if u >= 1:
                        act.wait_ge(sw_ready.sem, u)
                    act.activation(wgt[:, :, :], logw[:, :, :], ACT.Exp).then_inc(w_ready.sem, 1)

            @block.vector
            def _(dve):
                dve.memset(state[:, :, :, :], 0.0).then_inc(zeroed.sem, 1)
                dve.wait_ge(zeroed.sem, 1)

                def finish(u):
                    way, i, j = UNITS[u]
                    intra, inter, fresh = (
                        ps[:, bank + 2 * (u % 2), a * (DH + 1):b * (DH + 1)].rearrange("p (h d) -> p h d", h=b - a)
                        for bank, a, b in ((4, 0, HEADS), (5, 0, HEADS), (5, HEADS, HEADS + 2)))
                    dve.wait_ge(u_mm.sem, u + 1)
                    dv2.mark(dve.tensor_tensor(tmp[:, :, :], inter, col(j, 1, way).unsqueeze(2).broadcast_to([P, HEADS, DH + 1]),
                                               ALU.mult))
                    for hp in range(2):
                        dv2.mark(dve.scalar_tensor_tensor(out=state[:, way, hp, :], in0=state[:, way, hp, :],
                                                          scalar=decay[:, way * 2 + hp, j:j + 1], in1=fresh[:, hp, :],
                                                          op0=ALU.mult, op1=ALU.add))
                    dve.wait_ge(dv2.sem, dv2.n)
                    dve.wait_ge(intra_mm.sem, u + 1)
                    dv2.link(dve, dve.tensor_tensor(num[:, :, :], intra, tmp[:, :, :], ALU.add))
                    nq = num[:, :, DH:DH + 1]
                    d3 = den[:, :].unsqueeze(2)
                    dv2.link(dve, dve.scalar_tensor_tensor(out=d3, in0=nq, scalar=-1.0, in1=nq, op0=ALU.mult, op1=ALU.max))
                    dv2.link(dve, dve.tensor_tensor(den[:, :], den[:, :], col(j, 2, way), ALU.max))
                    dv2.link(dve, dve.reciprocal(den[:, :], den[:, :]))
                    rec = den[:, :].unsqueeze(2).broadcast_to([P, HEADS, DH])
                    if second_visit(u):
                        dv2.link(dve, dve.tensor_tensor(num[:, :, 0:DH], num[:, :, 0:DH], rec, ALU.mult))
                        dv2.link(dve, dve.tensor_tensor(hB[:, j, :, :], hB[:, j, :, :], num[:, :, 0:DH], ALU.add))
                    else:
                        dv2.link(dve, dve.tensor_tensor(hB[:, j, :, :], num[:, :, 0:DH], rec, ALU.mult))
                    dve.wait_ge(dv2.sem, dv2.n)
                    dve.sem_inc(finished.sem, 1)

                def log_weights(u):
                    way, i, j = UNITS[u]
                    dve.wait_ge(d_mm.sem, u + 1)
                    if u >= 1:
                        dve.wait_ge(w_ready.sem, u)
                    for h in range(HEADS):
                        dve.scalar_tensor_tensor(out=logw[:, h, :], in0=ps[:, u % 2, h * P:(h + 1) * P],
                                                 scalar=col(j, 0, way)[:, h:h + 1], in1=neg[:, way, :],
                                                 op0=ALU.add, op1=ALU.min).then_inc(dm_ready.sem, 1)

                log_weights(0)
                for u in range(NU):
                    if u + 1 < NU:
                        log_weights(u + 1)
                    dve.wait_ge(w_ready.sem, u + 1)
                    dve.wait_ge(s_mm.sem, u + 1)
                    if u >= 1:
                        dve.wait_ge(intra_mm.sem, u)
                    dve.tensor_tensor(sw[:, :, :], ps[:, 2 + u % 2, :].rearrange("p (h t) -> p h t", h=HEADS), wgt[:, :, :],
                                      ALU.mult).then_inc(sw_ready.sem, 1)
                    if u >= 1:
                        finish(u - 1)
                finish(NU - 1)

        turn_out(nc, env, hB, 2, "b", norm=True)


def turn_out(nc, env, src, tile0, name, norm, slabs=None):
    ps, signal, yT = env["ps"], env["signal"], env["yT"]
    sq_ready, ms_ready, root, dv, normed, turned, kept = (
        signal(f"{name}_{n}") for n in ("out_square", "out_mean", "out_root", "out_dve", "out_normed", "out_turned", "out_kept"))
    gain = W(env, "out_gain")
    with ExitStack() as own, nc.Block() as block:
        sq = own.enter_context(nc.sbuf_tensor(f"{name}_outsq", [P, 2, HEADS, DH], F32))
        stat = own.enter_context(nc.sbuf_tensor(f"{name}_outstat", [P, 2, NT, HEADS], F32))

        if slabs:
            @block.sync
            def _(sp):
                load_slabs(sp, env, *slabs)

        if norm:
            @block.vector
            def _(dve):
                for t in range(NT):
                    dve.wait_ge(sq_ready.sem, t + 1)
                    dv.mark(dve.tensor_reduce(stat[:, 0, t, :], sq[:, t % 2, :, :], AX.X, ALU.add))
                dve.wait_ge(dv.sem, NT)
                dv.link(dve, dve.tensor_scalar(stat[:, 0, :, :], stat[:, 0, :, :], 1.0 / DH, EPS, ALU.mult, ALU.add))
                dve.sem_inc(ms_ready.sem, 1)
                dve.wait_ge(root.sem, 2)
                for t in range(NT):
                    dve.tensor_tensor(src[:, t, :, :], src[:, t, :, :],
                                      stat[:, 1, t, :].unsqueeze(2).broadcast_to([P, HEADS, DH]), ALU.mult)\
                       .then_inc(normed.sem, 1)

        @block.tensor
        def _(pe):
            for t in range(NT):
                if norm:
                    pe.wait_ge(normed.sem, t + 1)
                if t >= 4:
                    pe.wait_ge(kept.sem, 2 * (t - 3))
                flat = src[:, t, :, :].rearrange("p h d -> p (h d)")
                for c in range(2):
                    last = pe.transpose(ps[:, t % 4, c * P:(c + 1) * P], flat[:, c * P:(c + 1) * P], C(env, "ident"))
                last.then_inc(turned.sem, 1)

        @block.scalar
        def _(act):
            if norm:
                for t in range(NT):
                    if t >= 2:
                        act.wait_ge(dv.sem, t - 1)
                    act.activation(sq[:, t % 2, :, :], src[:, t, :, :], ACT.Square).then_inc(sq_ready.sem, 1)
                act.wait_ge(ms_ready.sem, 1)
                root.link(act, act.activation(stat[:, 1, :, :], stat[:, 0, :, :], ACT.Ln))
                root.mark(act.activation(stat[:, 1, :, :], stat[:, 1, :, :], ACT.Exp, scale=-0.5))
            for t in range(NT):
                act.wait_ge(turned.sem, t + 1)
                for c in range(2):
                    act.activation(yT[:, tile0 + c, t * P:(t + 1) * P], ps[:, t % 4, c * P:(c + 1) * P], ACT.Copy,
                                   scale=gain[:, tile0 + c:tile0 + c + 1]).then_inc(kept.sem, 1)
            act.wait_ge(kept.sem, 2 * NT)


def stage_gla(nc, env):
    ps, signal, yT = (env[n] for n in ("ps", "signal", "yT"))
    outer = ExitStack()
    with outer:
        vC = yT[:, 4:6, :].rearrange("p a t -> p (a t)").rearrange("p (t c) -> p t c", t=NT)
        qT = outer.enter_context(nc.sbuf_tensor("c_qT", [P, T], F32))
        kT = outer.enter_context(nc.sbuf_tensor("c_kT", [P, T], F32))
        hC = yT[:, 0:2, :].rearrange("p a t -> p (a t)").rearrange("p (t h d) -> p t h d", t=NT, h=HEADS)
        sums = yT[:, 6:8, :]
        ev, turned, mm, logs, dv = (signal(n) for n in ("c_kept", "c_rank_turned", "c_product", "c_logs", "c_dve"))
        HT = T // 2
        groups = [(S_CQK, 0, GW, 0, T, channel_sums(2, BLOCKS))] + \
            [(S_CV, 0, GW + 2 * RANK, h * HT, HT, token_sums(GW + 2 * RANK, NT // 2)) for h in range(2)]
        with ExitStack() as own, nc.Block() as block:
            lr = own.enter_context(nc.sbuf_tensor("c_lr", [P, NT, 2 * RANK], F32))
            lrT = own.enter_context(nc.sbuf_tensor("c_lrT", [2 * RANK, T], F32))
            la = own.enter_context(nc.sbuf_tensor("c_la", [P, 2, T], F32))
            proj = SplitProduct(nc, env, own, "c_proj", groups)
            qk_sums = 2 * len(BLOCKS)
            las = [(z, b) for z in range(2) for b in BLOCKS]

            @block.sync
            def _(sp):
                load_slabs(sp, env, 10, 12)

            @block.tensor
            def _(pe):
                for i in range(len(proj.steps)):
                    proj.multiply(pe, i)
                pe.wait_ge(proj.read.sem, qk_sums + NT)
                for n, b in enumerate(BLOCKS):
                    for t in range(b[0] // P, (b[0] + b[1]) // P):
                        last = pe.transpose(ps[0:2 * RANK, n, t * P - b[0]:(t + 1) * P - b[0]], lr[:, t, :], C(env, "ident"))
                    last.then_inc(turned.sem, 1)
                for n, (z, b) in enumerate(las):
                    pe.wait_ge(ev.sem, n % 3 + 1)
                    if n >= 5:
                        pe.wait_ge(ev.sem, 4)
                    wg = W(env, "c_wg", 2 * RANK)[:, z * P:(z + 1) * P]
                    pe.matmul(ps[:, 3 + n % 5, 0:b[1]], wg, lrT[:, b[0]:b[0] + b[1]], start=True, stop=True).then_inc(mm.sem, 1)

            @block.scalar
            def _(act):
                def keep(n):
                    act.wait_ge(proj.ready.sem, n + 1)
                    bank = ps[:, n % 8, :]
                    if n < qk_sums:
                        b = BLOCKS[n % 3]
                        ins = act.activation((qT, kT)[n // 3][:, b[0]:b[0] + b[1]], bank[:, 0:b[1]], ACT.Copy,
                                             scale=(DH // 2) ** -0.5 if n < 3 else 1.0)
                    else:
                        t = n - qk_sums
                        act.activation(vC[:, t, :], bank[:, 0:GW], ACT.Copy)
                        ins = act.activation(lr[:, t, :], bank[:, GW:GW + 2 * RANK], ACT.Copy)
                    ins.then_inc(proj.read.sem, 1)

                for i, (g, k) in enumerate(proj.steps):
                    proj.high(act, i)
                    if g >= 1 and k == 1:
                        for n in range(proj.first[g - 1], proj.first[g]):
                            keep(n)
                for n in range(proj.first[-2], proj.first[-1]):
                    keep(n)
                act.wait_ge(proj.read.sem, proj.first[-1])
                for n, b in enumerate(BLOCKS):
                    act.wait_ge(turned.sem, n + 1)
                    act.activation(lrT[:, b[0]:b[0] + b[1]], ps[0:2 * RANK, n, 0:b[1]], ACT.Copy).then_inc(ev.sem, 1)
                for n, (z, b) in enumerate(las):
                    act.wait_ge(mm.sem, n + 1)
                    act.activation(la[:, z, b[0]:b[0] + b[1]], ps[:, 3 + n % 5, 0:b[1]], ACT.Identity,
                                   bias=W(env, "c_bg")[:, z:z + 1]).then_inc(ev.sem, 1)
                act.wait_ge(ev.sem, 3 + len(las))
                logs.link(act, act.activation(sums[:, :, :], la[:, :, :], ACT.Abs))
                logs.link(act, act.activation(sums[:, :, :], sums[:, :, :], ACT.Exp, scale=-1.0))
                logs.mark(act.activation(sums[:, :, :], sums[:, :, :], ACT.Ln, bias=1.0))

            @block.vector
            def _(dve):
                for i in range(len(proj.steps)):
                    proj.low(dve, i)
                dve.wait_ge(logs.sem, 3)
                dv.link(dve, dve.scalar_tensor_tensor(out=la[:, :, :], in0=la[:, :, :], scalar=0.0, in1=sums[:, :, :],
                                                      op0=ALU.min, op1=ALU.subtract))
                dv.link(dve, dve.tensor_scalar(la[:, :, :], la[:, :, :], 1.0 / TAU, LA_MIN, ALU.mult, ALU.max))
                for t in range(NT):
                    a, b = t * P, (t + 1) * P
                    dv.mark(dve.tensor_tensor_scan(sums[:, 0, a:b], C(env, "ones"), la[:, 0, a:b], 0.0, ALU.mult, ALU.add))
                    dv.mark(dve.tensor_tensor_scan(sums[:, 1, a:b][:, ::-1], C(env, "ones"), la[:, 1, a:b][:, ::-1], 0.0,
                                                   ALU.mult, ALU.add))
                dve.wait_ge(dv.sem, dv.n)

        (diff_ready, decay_ready, k_scaled, q_multiplied, q_scaled, q_placed_v, q_placed_s, far_mm, map_mm, src_turned, src_kept, far_kept,
         picked, o_mm, u_mm, finished, zeroed, cleared, dv2, act2) = (
            signal(n) for n in ("c_diff", "c_decay", "c_k_scaled", "c_q_multiplied", "c_q_scaled", "c_q_placed_v", "c_q_placed_s", "c_far_mm",
                                "c_map_mm", "c_src_turned", "c_src_kept", "c_far_kept", "c_picked", "c_out_mm", "c_new_mm",
                                "c_finished", "c_zeroed", "c_cleared", "c_dve2", "c_act2"))
        LEVELS = (64, 32, 16, 8)
        NU = len(UNITS)
        with ExitStack() as own, nc.Block() as block:
            def tile(name, shape):
                return own.enter_context(nc.sbuf_tensor(name, shape, F32))

            diff = tile("c_diffs", [P, 2, 5, P])
            decays = tile("c_decays", [P, 2, 8, P])
            kx = tile("c_kx", [P, 2, 6, P])
            from_start = tile("c_from_start", [P, 4, P])
            qx = tile("c_qx", [P, 2, 5, P])
            qh = tile("c_qh", [P, 2, 5, HEADS, P])
            spare = env["ring"][:, S_AV % RING, KT * SLAB_W[S_AV]:]
            acc = spare[:, 0:2 * HEADS * P].rearrange("p (w h t) -> p w h t", w=2, h=HEADS)
            state = spare[:, 2 * HEADS * P:2 * HEADS * P + 2 * GW].rearrange("p (w c) -> p w c", w=2)
            new = spare[:, 2 * HEADS * P + 2 * GW:2 * HEADS * P + 3 * GW]
            src = spare[:, 2 * HEADS * P + 3 * GW:2 * HEADS * P + 3 * GW + 2 * P].rearrange("p (u c) -> p u c", u=2)
            start = tile("c_start", [P, 4])

            def span(u):
                return slice(UNITS[u][2] * P, (UNITS[u][2] + 1) * P)

            def place(u, h):
                r = slice(32 * h, 32 * h + 32)
                return qh[r, u % 2, :, h, :], qx[r, u % 2, :, :]

            @block.gpsimd
            def _(pool):
                def differences(u):
                    way, i, j = UNITS[u]
                    if u >= 2:
                        pool.wait_ge(decay_ready.sem, u - 1)
                    for lev, half in enumerate(LEVELS + (4,)):
                        mid = half - 1 + way
                        view = sums[:, way, span(u)].rearrange("p (b t) -> p b t", t=2 * half)
                        out = diff[:, u % 2, lev, :].rearrange("p (b t) -> p b t", t=2 * half)
                        pool.tensor_tensor(out, view, view[:, :, mid:mid + 1].broadcast_to([P, P // (2 * half), 2 * half]),
                                           ALU.subtract).then_inc(diff_ready.sem, 1)

                def scale_k(u):
                    pool.wait_ge(decay_ready.sem, u + 1)
                    if u >= 2:
                        pool.wait_ge(map_mm.sem, 3 * (u - 1))
                    pool.tensor_tensor(kx[:, u % 2, :, :], decays[:, u % 2, 0:6, :],
                                       kT[:, span(u)].unsqueeze(1).broadcast_to([P, 6, P]), ALU.mult).then_inc(k_scaled.sem, 1)

                differences(0)
                pool.memset(acc[:, :, :, :], 0.0).then_inc(zeroed.sem, 1)
                pool.memset(state[:, :, :], 0.0).then_inc(zeroed.sem, 1)
                differences(1)
                for u in range(NU):
                    scale_k(u)
                    if u + 2 < NU:
                        differences(u + 2)

            @block.scalar
            def _(act):
                def decay(u):
                    way, i, j = UNITS[u]
                    s = sums[:, way, span(u)]
                    end = P - 1 if way == 0 else 0
                    d = decays[:, u % 2, :, :]
                    act.wait_ge(diff_ready.sem, 5 * (u + 1))
                    if u >= 2:
                        act.wait_ge(k_scaled.sem, u - 1)
                        act.wait_ge(q_scaled.sem, u - 1)
                    act2.link(act, act.activation(d[:, 2:6, :], diff[:, u % 2, 0:4, :], ACT.Abs))
                    act.activation(d[:, 2:6, :], d[:, 2:6, :], ACT.Exp, scale=-1.0)
                    act.activation(d[:, 0, :], diff[:, u % 2, 4, :], ACT.Exp, scale=-1.0)
                    act.activation(d[:, 6, :], diff[:, u % 2, 4, :], ACT.Exp)
                    act.activation(d[:, 7, :], s, ACT.Exp)
                    act.activation(d[:, 1, :], s, ACT.Exp, scale=-1.0, bias=s[:, end:end + 1]).then_inc(decay_ready.sem, 1)

                def place_q(u):
                    act.wait_ge(q_multiplied.sem, u + 1)
                    if u == 0:
                        act.wait_ge(cleared.sem, 1)
                    if u >= 2:
                        act.wait_ge(map_mm.sem, 3 * (u - 1))
                    for h in (1, 2, 3):
                        act.activation(*place(u, h), ACT.Copy).then_inc(q_placed_s.sem, 1)

                decay(0)
                decay(1)
                place_q(0)
                for u, (way, i, j) in enumerate(UNITS):
                    act.wait_ge(src_turned.sem, u + 1)
                    if u >= 2:
                        act.wait_ge(u_mm.sem, u - 1)
                    act.activation(src[:, u % 2, :], ps[:, 7, 0:P], ACT.Copy).then_inc(src_kept.sem, 1)
                    act.wait_ge(far_mm.sem, u + 1)
                    if u >= 2:
                        act.wait_ge(o_mm.sem, u - 1)
                    if u == 0:
                        act.wait_ge(zeroed.sem, 1)
                    s0, t0 = (0, 64) if way == 0 else (64, 0)
                    act.activation(acc[s0:s0 + 64, way, :, t0:t0 + 64],
                                   ps[s0:s0 + 64, 3, 0:256].rearrange("p (h t) -> p h t", h=HEADS), ACT.Copy)\
                       .then_inc(far_kept.sem, 1)
                    for blk in (0, 64):
                        s0, t0 = (blk, blk + 32) if way == 0 else (blk + 32, blk)
                        act.activation(acc[s0:s0 + 32, way, :, t0:t0 + 32],
                                       ps[s0:s0 + 32, 3, 256:384].rearrange("p (h t) -> p h t", h=HEADS), ACT.Copy)\
                           .then_inc(far_kept.sem, 1)
                    if u + 1 < NU:
                        place_q(u + 1)
                    if u + 2 < NU:
                        decay(u + 2)

            @block.tensor
            def _(pe):
                def levels(u):
                    way, i, j = UNITS[u]
                    q, k = qh[:, u % 2, :, :, :], kx[:, u % 2, :, :]
                    pe.wait_ge(k_scaled.sem, u + 1)
                    if u >= 1:
                        pe.wait_ge(src_kept.sem, u)
                    pe.transpose(ps[:, 7, 0:P], k[:, 1, :], C(env, "ident")).then_inc(src_turned.sem, 1)
                    pe.wait_ge(q_placed_v.sem, u + 1)
                    pe.wait_ge(q_placed_s.sem, 3 * (u + 1))
                    if u >= 1:
                        pe.wait_ge(far_kept.sem, 3 * u)
                    s0, t0 = (0, 64) if way == 0 else (64, 0)
                    pe.matmul(ps[s0:s0 + 64, 3, 0:256], k[:, 2, s0:s0 + 64], q[:, 0, :, t0:t0 + 64], start=True, stop=True,
                              tile_position=(0, s0))
                    for blk in (0, 64):
                        s0, t0 = (blk, blk + 32) if way == 0 else (blk + 32, blk)
                        last = pe.matmul(ps[s0:s0 + 32, 3, 256:384], k[:, 3, s0:s0 + 32], q[:, 1, :, t0:t0 + 32],
                                         start=True, stop=True, tile_position=(0, s0))
                    last.then_inc(far_mm.sem, 1)
                    for n, (a, b) in enumerate(((4, 2), (5, 3), (0, 4))):
                        if u >= 1:
                            pe.wait_ge(picked.sem, 3 * (u - 1) + n + 1)
                        pe.matmul(ps[:, n, :], k[:, a, :], q[:, b, :, :], start=True, stop=True).then_inc(map_mm.sem, 1)

                def out(u):
                    way, i, j = UNITS[u]
                    pe.wait_ge(src_kept.sem, u + 1)
                    pe.wait_ge(zeroed.sem, 2)
                    if u >= 1:
                        pe.wait_ge(finished.sem, u)
                    pe.matmul(ps[:, 6, 0:GW], src[:, u % 2, :], vC[:, j, :], start=True, stop=True).then_inc(u_mm.sem, 1)
                    pe.wait_ge(q_scaled.sem, u + 1)
                    pe.matmul(ps[:, 5, 0:GW], from_start[:, u % 4, :], state[:, way, :], start=True, stop=False,
                              skip_group_check=True)
                    pe.wait_ge(picked.sem, 3 * (u + 1))
                    for h in range(HEADS):
                        last = pe.matmul(ps[:, 5, h * DH:(h + 1) * DH], acc[:, way, h, :], vC[:, j, h * DH:(h + 1) * DH],
                                         start=False, stop=h == HEADS - 1, skip_group_check=True)
                    last.then_inc(o_mm.sem, 1)

                for u in range(NU):
                    levels(u)
                    if u >= 1:
                        out(u - 1)
                out(NU - 1)

            @block.vector
            def _(dve):
                def scale_q(u):
                    way, i, j = UNITS[u]
                    dve.wait_ge(decay_ready.sem, u + 1)
                    if u >= 2:
                        dve.wait_ge(q_placed_s.sem, 3 * (u - 1))
                        dve.wait_ge(map_mm.sem, 3 * (u - 1))
                    if u >= 4:
                        dve.wait_ge(o_mm.sem, u - 3)
                    if u == 0:
                        dve.wait_ge(cleared.sem, 1)
                    end = P - 1 if way == 0 else 0
                    d = decays[:, u % 2, :, :]
                    q = qT[:, span(u)].unsqueeze(1)
                    dve.tensor_copy(start[:, u % 4:u % 4 + 1], d[:, 7, end:end + 1])
                    dve.tensor_tensor(qx[:, u % 2, :, :], d[:, 2:7, :], q.broadcast_to([P, 5, P]), ALU.mult)\
                       .then_inc(q_multiplied.sem, 1)
                    dve.tensor_tensor(place(u, 0)[0], d[0:32, 2:7, :], q[0:32].broadcast_to([32, 5, P]), ALU.mult)\
                       .then_inc(q_placed_v.sem, 1)
                    dve.tensor_tensor(from_start[:, u % 4, :], d[:, 7, :], qT[:, span(u)], ALU.mult).then_inc(q_scaled.sem, 1)

                def finish(u):
                    way, i, j = UNITS[u]
                    dve.wait_ge(u_mm.sem, u + 1)
                    dv2.link(dve, dve.tensor_tensor(new[:, :], ps[:, 6, 0:GW], C(env, "diag"), ALU.mult))
                    dve.wait_ge(o_mm.sem, u + 1)
                    dv2.mark(dve.scalar_tensor_tensor(out=state[:, way, :], in0=state[:, way, :], scalar=start[:, u % 4:u % 4 + 1],
                                                      in1=new[:, :], op0=ALU.mult, op1=ALU.add))
                    o = ps[:, 5, 0:GW].rearrange("p (h d) -> p h d", h=HEADS)
                    if second_visit(u):
                        dv2.mark(dve.tensor_tensor(hC[:, j, :, :], o, hC[:, j, :, :], ALU.add))
                    else:
                        dv2.mark(dve.tensor_copy(hC[:, j, :, :], o))
                    dve.wait_ge(dv2.sem, dv2.n)
                    dve.sem_inc(finished.sem, 1)

                pick = C(env, "pick").bitcast(mybir.dt.uint32).rearrange("p (a b c) -> p a b c", a=2, b=3)
                dve.memset(qh[:, :, :, :, :], 0.0).then_inc(cleared.sem, 1)
                scale_q(0)
                for u, (way, i, j) in enumerate(UNITS):
                    if u + 1 < NU:
                        scale_q(u + 1)
                    if u >= 2:
                        finish(u - 2)
                    dve.wait_ge(far_kept.sem, 3 * (u + 1))
                    for n in range(3):
                        dve.wait_ge(map_mm.sem, 3 * u + n + 1)
                        if n:
                            dve.wait_ge(picked.sem, 3 * u + n)
                        mask = pick[:, way, n, :].unsqueeze(1).broadcast_to([P, HEADS, P])
                        dve.copy_predicated(acc[:, way, :, :], mask, ps[:, n, :].rearrange("p (h t) -> p h t", h=HEADS))\
                           .then_inc(picked.sem, 1)
                finish(NU - 2)
                finish(NU - 1)

        turn_out(nc, env, hC, 4, "c", norm=True)


def project_qk(nc, env, name, s_qk, groups, width, qkT, v_of, last_slab_next, halves=None):
    ps, signal = env["ps"], env["signal"]
    n_qk = groups * width
    nch = n_qk // P
    sq_ready, reduced, ms_ready, root, normed, gained, cos_ready, rotated, dv, turned, kept, cleared = (
        signal(f"{name}_{n}") for n in ("square", "reduced", "mean", "root", "normed", "gained", "cos", "rotated",
                                        "dve", "turned", "turned_kept", "k_cleared"))
    s_v, v0, nv, v_dst = v_of
    HN = NT // 2
    HT = HN * P
    plan = [(s_qk, 0, SLAB_W[s_qk], h * HT, HT, token_sums(SLAB_W[s_qk], HN)) for h in range(2)]
    if s_v != s_qk:
        plan += [(s_v, 0, nv, h * HT, HT, token_sums(nv, HN)) for h in range(2)]
    BANKS = 8 if halves else 6
    with ExitStack() as own, nc.Block() as block:
        def tile(n, shape):
            return own.enter_context(nc.sbuf_tensor(f"{name}_{n}", shape, F32))

        raw = tile("raw", [P, HN, n_qk])
        spare = env["ring"][:, S_AV % RING, KT * SLAB_W[S_AV]:]
        sq = spare[:, 0:2 * n_qk].rearrange("p (u c) -> p u c", u=2)
        turn = spare[:, 2 * n_qk:3 * n_qk]
        if halves:
            rot = tile("rot", [P, 2, n_qk])
        else:
            rot = spare[:, 3 * n_qk:5 * n_qk].rearrange("p (u c) -> p u c", u=2)
        stat = tile("stat", [P, 3, HN * groups])
        ms, rstd, tmp = (stat[:, i, :] for i in range(3))
        proj = SplitProduct(nc, env, own, f"{name}_proj", plan, 3)
        cos = C(env, f"cos_{name}").rearrange("p (t w) -> p t w", t=NT)
        sin = C(env, f"sin_{name}").rearrange("p (t w) -> p t w", t=NT)
        q4 = width // 4

        def grouped(x):
            return x.rearrange("p (g w) -> p g w", g=groups)

        def quarters(x):
            return x.rearrange("p (g f s w) -> p g f s w", g=groups, f=2, s=2)

        def of_tile(x, t):
            return x[:, t % HN * groups:(t % HN + 1) * groups]

        @block.sync
        def _(sp):
            load_slabs(sp, env, *last_slab_next)

        @block.tensor
        def _(pe):
            def turns(t):
                pe.wait_ge(rotated.sem, t + 1)
                if t >= 2:
                    pe.wait_ge(kept.sem, t - 1)
                for c in range(nch):
                    last = pe.transpose(ps[:, 6 + t % 2, c * P:(c + 1) * P], rot[:, t % 2, c * P:(c + 1) * P], C(env, "ident"))
                last.then_inc(turned.sem, 1)

            for i, (g, k) in enumerate(proj.steps):
                proj.multiply(pe, i, BANKS)
                if not halves and g == 1 and k == 6:
                    for t in range(2):
                        turns(t)
            if not halves:
                for t in range(2, NT):
                    turns(t)

        @block.scalar
        def _(act):
            def keep_turned(t):
                act.wait_ge(turned.sem, t + 1)
                at = slice(t * P, (t + 1) * P)
                act.activation(qkT[:, 0:nch - 1, at], ps[:, 6 + t % 2, 0:n_qk - P].rearrange("p (c t) -> p c t", c=nch - 1),
                               ACT.Copy)
                if t == 0:
                    act.wait_ge(cleared.sem, 1)
                for i, r in enumerate((slice(0, 64), slice(64, P))):
                    ins = act.activation(qkT[r, nch - 1 + i, at], ps[r, 6 + t % 2, n_qk - P:n_qk], ACT.Copy)
                ins.then_inc(kept.sem, 1)

            def keep(t):
                act.wait_ge(proj.ready.sem, t + 1)
                if t >= 2:
                    act.wait_ge(reduced.sem, t - 1)
                bank = ps[:, t % BANKS, :]
                act.activation(sq[:, t % 2, :], bank[:, 0:n_qk], ACT.Square).then_inc(sq_ready.sem, 1)
                if t >= HN:
                    act.wait_ge(rotated.sem, t - HN + 1)
                if s_v == s_qk:
                    act.activation(v_dst(t), bank[:, v0:v0 + nv], ACT.Copy)
                act.activation(raw[:, t % HN, :], bank[:, 0:n_qk], ACT.Copy).then_inc(proj.read.sem, 1)

            def keep_v(t):
                n = NT + t
                act.wait_ge(proj.ready.sem, n + 1)
                act.activation(v_dst(t), ps[:, n % BANKS, 0:nv], ACT.Copy).then_inc(proj.read.sem, 1)

            def roots(h):
                act.wait_ge(ms_ready.sem, h + 1)
                if h >= 1:
                    act.wait_ge(normed.sem, HN * h)
                root.link(act, act.activation(rstd, ms, ACT.Ln))
                root.link(act, act.activation(rstd, rstd, ACT.Exp, scale=-0.5))

            for i, (g, k) in enumerate(proj.steps):
                proj.high(act, i)
                if g in (1, 2):
                    if k == 1:
                        for a in range(4):
                            keep((g - 1) * HN + a)
                    if k == 2:
                        keep((g - 1) * HN + 4)
                    if k == 3:
                        roots(g - 1)
                if g == 3 and k == 1:
                    for a in range(HN):
                        keep_v(a)
                if not halves and g == 1 and k == 7:
                    for t in range(2):
                        keep_turned(t)
            if s_v == s_qk:
                for a in range(HN):
                    keep(HN + a)
                roots(1)
            else:
                for a in range(HN):
                    keep_v(HN + a)
            if not halves:
                for t in range(2, NT):
                    keep_turned(t)
                act.wait_ge(kept.sem, NT)
            act.wait_ge(proj.read.sem, proj.first[-1])

        @block.gpsimd
        def _(pool):
            if not halves:
                pool.memset(qkT[:, nch - 1:nch + 1, :], 0.0).then_inc(cleared.sem, 1)
                pool.wait_ge(cleared.sem, 1)
            for t in range(NT):
                x = raw[:, t % HN, :]
                pool.wait_ge(normed.sem, t + 1)
                pool.tensor_tensor(x, x, W(env, f"{name}_gain"), ALU.mult).then_inc(gained.sem, 1)
                pool.wait_ge(gained.sem, t + 1)
                if t >= 2:
                    pool.wait_ge(rotated.sem if halves else turned.sem, t - 1)
                pool.tensor_tensor(grouped(rot[:, t % 2, :]), grouped(x),
                                   cos[:, t, :].unsqueeze(1).broadcast_to([P, groups, width]), ALU.mult)\
                    .then_inc(cos_ready.sem, 1)

        @block.vector
        def _(dve):
            def reduce(t):
                dve.wait_ge(sq_ready.sem, t + 1)
                if t == HN:
                    dve.wait_ge(root.sem, 2)
                dve.tensor_reduce(of_tile(ms, t), grouped(sq[:, t % 2, :]), AX.X, ALU.add).then_inc(reduced.sem, 1)

            def means(h):
                dve.wait_ge(reduced.sem, HN * (h + 1))
                dve.tensor_scalar(ms, ms, 1.0 / width, EPS, ALU.mult, ALU.add).then_inc(ms_ready.sem, 1)

            def refine(h):
                dve.wait_ge(ms_ready.sem, h + 1)
                dve.wait_ge(root.sem, 2 * (h + 1))
                rsqrt_newton(dve, dv, rstd, ms, tmp)

            def norm(t):
                dve.wait_ge(proj.read.sem, t + 1)
                x = grouped(raw[:, t % HN, :])
                dve.tensor_tensor(x, x, of_tile(rstd, t).unsqueeze(2).broadcast_to([P, groups, width]), ALU.mult)\
                   .then_inc(normed.sem, 1)

            def rotate(t):
                dve.wait_ge(gained.sem, t + 1)
                x, y = quarters(raw[:, t % HN, :]), quarters(turn)
                s = sin[:, t, :].rearrange("p (f s w) -> p f s w", f=2, s=2)
                if t >= 1:
                    dve.wait_ge(rotated.sem, t)
                for i in range(2):
                    for f in range(2):
                        ins = dve.tensor_tensor(y[:, :, f, i, :], x[:, :, f, 1 - i, :],
                                                s[:, f, i, :].unsqueeze(1).broadcast_to([P, groups, q4]), ALU.mult)
                        dv.mark(ins)
                dve.wait_ge(dv.sem, dv.n)
                dve.wait_ge(cos_ready.sem, t + 1)
                if halves:
                    for i, half in enumerate(halves):
                        a, b = (x.rearrange("p (s i c) -> p s i c", s=2, i=2)[:, :, i, :] for x in (rot[:, t % 2, :], turn[:, :]))
                        ins = dve.tensor_tensor(half[:, t, :].rearrange("p (s c) -> p s c", s=2), a, b, ALU.add)
                        if i == 0:
                            dv.mark(ins)
                    dve.wait_ge(dv.sem, dv.n)
                    ins.then_inc(rotated.sem, 1)
                else:
                    dve.tensor_tensor(rot[:, t % 2, :], rot[:, t % 2, :], turn[:, :], ALU.add).then_inc(rotated.sem, 1)

            def half_step(h, k):
                t0 = HN * h
                if k == 1:
                    for a in range(4):
                        reduce(t0 + a)
                if k == 2:
                    reduce(t0 + 4)
                    means(h)
                if k == 3:
                    refine(h)
                    norm(t0)
                    norm(t0 + 1)
                if k == 4:
                    for a in range(2, HN):
                        norm(t0 + a)
                if k in (5, 6):
                    rotate(t0 + 2 * (k - 5))
                    rotate(t0 + 2 * (k - 5) + 1)
                if k == 7:
                    rotate(t0 + 4)

            if halves:
                gain = W(env, f"{name}_gain")[:, 0:n_qk // 2]
                dv.link(dve, dve.tensor_scalar(gain, gain, width ** -0.5, None, ALU.mult))
            for i, (g, k) in enumerate(proj.steps):
                proj.low(dve, i)
                if g == 1:
                    half_step(0, k)
                elif g == 2 and k < 5:
                    half_step(1, k)
                elif g == 3 and k in (2, 4, 6):
                    half_step(1, 4 + k // 2)
            if s_v == s_qk:
                for k in range(KT):
                    half_step(1, k)
            dve.wait_ge(rotated.sem, NT)


def stack_pair(nc, env, src, q4, k4, name):
    ps, signal = env["ps"], env["signal"]
    split, low, high, high_k, turned, kept_q, kept_k = (
        signal(f"{name}_{n}") for n in ("stack_split", "stack_low", "stack_high", "stack_high_k", "stack_turned", "stack_q", "stack_k"))
    with ExitStack() as own, nc.Block() as block:
        hi = own.enter_context(nc.sbuf_tensor(f"{name}_hi", [P, 2, 2 * P], F32R))
        stack = env["ring"].rearrange("p a n -> p (a n)")[:, 0:2048].rearrange("p (u s m b c) -> p u s m b c", u=2, s=2, m=4, b=4)

        def maps(x, s):
            return x.rearrange("p (s m c) -> p s m c", s=2, m=4)[:, s, :, :].unsqueeze(2).broadcast_to([P, 4, 2, 32])

        def places(t, s, low):
            x = stack[:, t % 2, s, :, :, :]
            return x[:, :, 2 * low:2 * low + 2, :] if s == 0 else x[:, :, low::2, :]

        @block.vector
        def _(dve):
            for t in range(NT):
                if t >= 2:
                    dve.wait_ge(high.sem, t - 1)
                    dve.wait_ge(high_k.sem, t - 1)
                    dve.wait_ge(turned.sem, t - 1)
                dve.tensor_copy(hi[:, t % 2, :], src[:, t, :]).then_inc(split.sem, 1)
                dve.wait_ge(split.sem, t + 1)
                for s in range(2):
                    dve.tensor_tensor(places(t, s, 1), maps(src[:, t, :], s), maps(hi[:, t % 2, :].bitcast(F32), s), ALU.subtract)\
                       .then_inc(low.sem, 1)
                if t >= 1:
                    dve.wait_ge(turned.sem, t)
                    dve.tensor_copy(k4[:, :, (t - 1) * P:t * P],
                                    ps[:, 2 * ((t - 1) % 2) + 1, :].rearrange("p (m t) -> p m t", m=4)).then_inc(kept_k.sem, 1)
            dve.wait_ge(turned.sem, NT)
            dve.tensor_copy(k4[:, :, (NT - 1) * P:NT * P], ps[:, 2 * ((NT - 1) % 2) + 1, :].rearrange("p (m t) -> p m t", m=4))\
               .then_inc(kept_k.sem, 1)

        @block.gpsimd
        def _(pool):
            for t in range(NT):
                pool.wait_ge(split.sem, t + 1)
                pool.tensor_copy(places(t, 0, 0), maps(hi[:, t % 2, :].bitcast(F32), 0)).then_inc(high.sem, 1)

        @block.tensor
        def _(pe):
            for t in range(NT):
                pe.wait_ge(low.sem, 2 * (t + 1))
                pe.wait_ge(high.sem, t + 1)
                pe.wait_ge(high_k.sem, t + 1)
                if t >= 2:
                    pe.wait_ge(kept_q.sem, t - 1)
                    pe.wait_ge(kept_k.sem, t - 1)
                for s in range(2):
                    for m in range(4):
                        last = pe.transpose(ps[:, 2 * (t % 2) + s, m * P:(m + 1) * P],
                                            stack[:, t % 2, s, m, :, :].rearrange("p b c -> p (b c)"), C(env, "ident"))
                last.then_inc(turned.sem, 1)

        @block.scalar
        def _(act):
            def high_part(t):
                act.wait_ge(split.sem, t + 1)
                act.activation(places(t, 1, 0), maps(hi[:, t % 2, :].bitcast(F32), 1), ACT.Copy).then_inc(high_k.sem, 1)

            high_part(0)
            for t in range(NT):
                if t + 1 < NT:
                    high_part(t + 1)
                act.wait_ge(turned.sem, t + 1)
                act.activation(q4[:, :, t * P:(t + 1) * P], ps[:, 2 * (t % 2), :].rearrange("p (m t) -> p m t", m=4), ACT.Copy)\
                   .then_inc(kept_q.sem, 1)


def stage_diff_attention(nc, env):
    yT = env["yT"]
    with ExitStack() as outer:
        by_token = lambda k: yT[:, k:k + 2, :].rearrange("p a t -> p (a t)").rearrange("p (t c) -> p t c", t=NT)
        vA = by_token(0)
        yA = by_token(6).rearrange("p t (h d) -> p t h d", h=HEADS)
        second = outer.enter_context(nc.sbuf_tensor("a_qk1", [P, NT, 2 * P], F32))
        pairs = [by_token(6), second]
        project_qk(nc, env, "a", S_AQK, 16, 32, None, (S_AV, 0, GW, lambda t: vA[:, t, :]), (12, 12), halves=pairs)
        q4 = outer.enter_context(nc.sbuf_tensor("a_q4", [P, 4, T], F32R))
        k4 = outer.enter_context(nc.sbuf_tensor("a_k4", [P, 4, T], F32R))
        nlam = outer.enter_context(nc.sbuf_tensor("a_nlam", [P, 1], F32))
        for pair in range(2):
            stack_pair(nc, env, pairs[pair], q4, k4, f"a{pair}")
            attend_pair(nc, env, pair, q4, k4, vA, yA, nlam)
        turn_out(nc, env, yA, 0, "a", norm=True, slabs=(12, 14))


def attend_pair(nc, env, pair, q4, k4, vA, yA, nlam):
    ps, signal = env["ps"], env["signal"]
    name = f"a{pair}"
    (s_mm, mx, exped, inverse, factored, comb, t_mm, t_kept, o_mm, o_kept, dv, lam_a) = (
        signal(f"{name}_{n}") for n in ("scores", "max", "exp", "inverse", "factor", "combined", "turns", "turn_kept", "out_mm", "out_read",
                                        "dve", "lam"))
    SLOTS = 6
    units = [(t, h) for t in range(NT) for h in range(2)]
    NU = len(units)
    scratch = env["ring"][:, :, :].rearrange("p a n -> p (a n)")
    probs = [[scratch[:, i * T:(i + 1) * T] for i in places] for places in ((0, 1, 2), (3, 4))]

    def p(u, c, n):
        return probs[c][u % len(probs[c])][:, 0:n]

    def keys(t):
        return NC if t < NC else NT

    def chunks(t):
        n = keys(t)
        return [(a, min(a + 4, n)) for a in range(0, n, 4)]

    def before(u):
        return sum(len(chunks(units[i][0])) for i in range(u))

    with ExitStack() as own, nc.Block() as block:
        def tile(n, shape):
            return own.enter_context(nc.sbuf_tensor(f"{name}_{n}", shape, F32))

        turned = [scratch[:, 5 * T:6 * T], tile("aT", [P, T])[:, :]]
        aT = [x.rearrange("p (k t) -> p k t", t=P) for x in turned]
        stat = tile("st", [P, SLOTS, 2, 4])
        lam = tile("lm", [P, 2, 32])
        lam2 = tile("lm2", [P, 2])

        @block.tensor
        def _(pe):
            def scores(u, c):
                t, h = units[u]
                if u >= 1:
                    pe.wait_ge(exped.sem, 2 * (u - 1) + c + 1)
                n = keys(t) * P
                for b, k0 in enumerate(range(0, n, BANK)):
                    w = min(BANK, n - k0)
                    last = pe.matmul(ps[:, 3 * c + b, 0:w], q4[:, 2 * h + c, t * P:(t + 1) * P], k4[:, 2 * h + c, k0:k0 + w],
                                     start=True, stop=True)
                last.then_inc(s_mm.sem, 1)

            def turns(u):
                t, h = units[u]
                pe.wait_ge(comb.sem, u + 1)
                for n, (a, b) in enumerate(chunks(t)):
                    if n == 0:
                        pe.wait_ge(t_kept.sem, before(u))
                    if n == 1 and u >= 2:
                        pe.wait_ge(o_kept.sem, u - 1)
                    if n == 2:
                        pe.wait_ge(t_kept.sem, before(u) + 1)
                    for k in range(a, b):
                        last = pe.transpose(ps[:, 6 + n % 2, (k - a) * P:(k - a + 1) * P], p(u, 0, T)[:, k * P:(k + 1) * P],
                                            C(env, "ident"))
                    last.then_inc(t_mm.sem, 1)

            def value(u):
                t, h = units[u]
                pe.wait_ge(t_kept.sem, before(u + 1))
                if u + 1 < NU:
                    pe.wait_ge(t_kept.sem, before(u + 1) + min(2, len(chunks(units[u + 1][0]))))
                if u >= 1:
                    pe.wait_ge(o_kept.sem, u)
                n = keys(t)
                h = 2 * pair + h
                for k in range(n):
                    last = pe.matmul(ps[:, 7, 0:DH], aT[u % 2][:, k, :], vA[:, k, h * DH:(h + 1) * DH], start=k == 0, stop=k == n - 1)
                last.then_inc(o_mm.sem, 1)

            scores(0, 0)
            for u in range(NU):
                scores(u, 1)
                if u >= 2:
                    turns(u - 2)
                if u + 1 < NU:
                    scores(u + 1, 0)
                if u >= 3:
                    value(u - 3)
            turns(NU - 2)
            value(NU - 3)
            turns(NU - 1)
            value(NU - 2)
            value(NU - 1)

        @block.scalar
        def _(act):
            def exp(u, c):
                t, h = units[u]
                act.wait_ge(mx.sem, 2 * u + c + 1)
                if c == 0 and u >= 3:
                    act.wait_ge(t_mm.sem, before(u - 2))
                if c == 1 and u >= 2:
                    act.wait_ge(comb.sem, u - 1)
                n = keys(t) * P
                st = stat[:, u % SLOTS, c, :]
                act.activation(p(u, c, n), ps[:, 3 * c:3 * c + 3, :].rearrange("p b n -> p (b n)")[:, 0:n], ACT.Exp,
                               bias=st[:, 0:1], accum_out=st[:, 1:2]).then_inc(exped.sem, 1)

            def keep(u):
                t, h = units[u]
                for n, (a, b) in enumerate(chunks(t)):
                    act.wait_ge(t_mm.sem, before(u) + n + 1)
                    if n == 0 and u >= 2:
                        act.wait_ge(o_mm.sem, u - 1)
                    act.activation(aT[u % 2][:, a:b, :], ps[:, 6 + n % 2, 0:(b - a) * P].rearrange("p (k t) -> p k t", t=P),
                                   ACT.Copy).then_inc(t_kept.sem, 1)

            if pair == 0:
                act.wait_ge(lam_a.sem, 2)
                act.activation(lam2[:, :], lam2[:, :], ACT.Exp).then_inc(lam_a.sem, 1)
            for u in range(NU):
                exp(u, 0)
                if u >= 2:
                    keep(u - 2)
                exp(u, 1)
            keep(NU - 2)
            keep(NU - 1)

        @block.vector
        def _(dve):
            def maximum(u, c):
                t, h = units[u]
                dve.wait_ge(s_mm.sem, 2 * u + c + 1)
                n = keys(t) * P
                dve.tensor_reduce(stat[:, u % SLOTS, c, 0:1], ps[:, 3 * c:3 * c + 3, :].rearrange("p b n -> p (b n)")[:, 0:n],
                                  AX.X, ALU.max, negate=True).then_inc(mx.sem, 1)

            def inverses(u):
                st = stat[:, u % SLOTS, :, :]
                dve.wait_ge(exped.sem, 2 * u + 2)
                dve.reciprocal(st[:, :, 2:3], st[:, :, 1:2]).then_inc(inverse.sem, 1)

            def factor(u):
                st = stat[:, u % SLOTS, :, :]
                dve.wait_ge(inverse.sem, u + 1)
                dve.scalar_tensor_tensor(out=st[:, 0, 3:4], in0=st[:, 0, 1:2], scalar=st[:, 1, 2:3], in1=nlam[:, :],
                                         op0=ALU.mult, op1=ALU.mult).then_inc(factored.sem, 1)

            def combine(u):
                t, h = units[u]
                st = stat[:, u % SLOTS, :, :]
                dve.wait_ge(factored.sem, u + 1)
                n = keys(t) * P
                dve.scalar_tensor_tensor(out=p(u, 0, n), in0=p(u, 1, n), scalar=st[:, 0, 3:4],
                                         in1=p(u, 0, n), op0=ALU.mult, op1=ALU.add).then_inc(comb.sem, 1)

            def keep(u):
                t, h = units[u]
                dve.wait_ge(o_mm.sem, u + 1)
                dve.tensor_scalar(yA[:, t, 2 * pair + h, :], ps[:, 7, 0:DH], stat[:, u % SLOTS, 0, 2:3], None, ALU.mult)\
                   .then_inc(o_kept.sem, 1)

            if pair == 0:
                lp = W(env, "a_lam").rearrange("p (a b w) -> p a b w", a=2, b=2)
                lam_a.link(dve, dve.tensor_tensor(lam[:, :, :], lp[:, :, 0, :], lp[:, :, 1, :], ALU.mult))
                lam_a.mark(dve.tensor_reduce(lam2[:, :], lam[:, :, :], AX.X, ALU.add))
                dve.wait_ge(lam_a.sem, 3)
                dv.link(dve, dve.tensor_tensor(nlam[:, :], lam2[:, 1:2], lam2[:, 0:1], ALU.subtract))
                dv.link(dve, dve.tensor_tensor(nlam[:, :], nlam[:, :], W(env, "lam_init")[:, 0:1], ALU.subtract))
            for u in range(NU):
                maximum(u, 0)
                if u >= 1:
                    inverses(u - 1)
                if u >= 4:
                    keep(u - 4)
                if u >= 1:
                    factor(u - 1)
                maximum(u, 1)
                if u >= 1:
                    combine(u - 1)
            inverses(NU - 1)
            factor(NU - 1)
            combine(NU - 1)
            for u in range(NU - 4, NU):
                keep(u)
            dve.wait_ge(o_kept.sem, NU)


def stage_window_attention(nc, env):
    ps, signal = env["ps"], env["signal"]
    SCALE = DH ** -0.5
    with ExitStack() as outer:
        qkT = outer.enter_context(nc.sbuf_tensor("d_qkT", [P, 4, T], F32))
        vD = env["yT"][:, 6, :].rearrange("p (t c) -> p t c", t=NT)
        project_qk(nc, env, "d", S_D, 6, 64, qkT, (S_D, 384, P, lambda t: vD[:, t, :]), (14, 15))
        yD = outer.enter_context(nc.sbuf_tensor("d_y", [P, NT, HEADS, DH], F32))
        (masks, s_mm, mx, exped, summed, t_mm, t_kept, o_mm, o_kept, dv, sunk) = (
            signal(n) for n in ("d_masks", "d_scores", "d_max", "d_exp", "d_sum", "d_turns", "d_turn_kept", "d_out_mm", "d_out_read",
                                "d_dve2", "d_sink"))
        units = [(t, h) for t in range(NT) for h in range(HEADS)]
        NU = len(units)

        def key_tiles(t):
            ctx = [(k, None) for k in range(NC)]
            return ctx if t < NC else ctx + [(k, {-1: 0, 0: None, 1: 1}[k - t]) for k in (t - 1, t, t + 1) if NC <= k < NT]

        def nch(t):
            return 1 if len(key_tiles(t)) <= 4 else 2

        def before(u):
            return sum(nch(units[i][0]) for i in range(u))

        with ExitStack() as own, nc.Block() as block:
            def tile(n, shape):
                return own.enter_context(nc.sbuf_tensor(f"d_{n}", shape, F32))

            p = tile("p", [P, 2, 5 * P])
            aT = tile("aT", [P, 2, 5, P])
            stat = tile("st", [P, 4, 4])
            band = own.enter_context(nc.sbuf_tensor("d_band", [P, 2, P], F32R))
            same = own.enter_context(nc.sbuf_tensor("d_same", [P, P], F32R))

            @block.tensor
            def _(pe):
                def scores(u):
                    if u == 0:
                        pe.wait_ge(masks.sem, 2)
                    t, h = units[u]
                    kv, g = h // 2, h % 2
                    if u >= 2:
                        pe.wait_ge(exped.sem, u - 1)
                    for n, (k, mask) in enumerate(key_tiles(t)):
                        out = ps[:, 2 * (u % 2) + n // 4, (n % 4) * P:(n % 4 + 1) * P]
                        last = pe.matmul(out, qkT[:, g, t * P:(t + 1) * P], qkT[:, 2 + kv, k * P:(k + 1) * P],
                                         start=True, stop=mask is None)
                        if mask is not None:
                            last = pe.matmul(out, same[:, :], band[:, mask, :], start=False, stop=True)
                    last.then_inc(s_mm.sem, 1)

                def turns(u):
                    t, h = units[u]
                    kt = key_tiles(t)
                    pe.wait_ge(exped.sem, u + 1)
                    if u >= 1:
                        pe.wait_ge(t_kept.sem, before(u))
                    for c in range(nch(t)):
                        for n in range(4 * c, min(4 * c + 4, len(kt))):
                            last = pe.transpose(ps[:, 4 + c, (n % 4) * P:(n % 4 + 1) * P], p[:, u % 2, n * P:(n + 1) * P],
                                                C(env, "ident"))
                        last.then_inc(t_mm.sem, 1)

                def value(u):
                    t, h = units[u]
                    kv = h // 2
                    kt = key_tiles(t)
                    pe.wait_ge(t_kept.sem, before(u + 1))
                    if u >= 2:
                        pe.wait_ge(o_kept.sem, u - 1)
                    for n, (k, _) in enumerate(kt):
                        last = pe.matmul(ps[:, 6 + u % 2, 0:DH], aT[:, u % 2, n, :], vD[:, k, kv * DH:(kv + 1) * DH],
                                         start=n == 0, stop=n == len(kt) - 1)
                    last.then_inc(o_mm.sem, 1)

                for u in range(NU):
                    scores(u)
                    if u >= 1:
                        turns(u - 1)
                    if u >= 2:
                        value(u - 2)
                turns(NU - 1)
                value(NU - 2)
                value(NU - 1)

            @block.scalar
            def _(act):
                def keep(u):
                    t, h = units[u]
                    if u >= 2:
                        act.wait_ge(o_mm.sem, u - 1)
                    for c in range(nch(t)):
                        n = min(4, len(key_tiles(t)) - 4 * c)
                        act.wait_ge(t_mm.sem, before(u) + c + 1)
                        act.activation(aT[:, u % 2, 4 * c:4 * c + n, :], ps[:, 4 + c, 0:n * P].rearrange("p (k t) -> p k t", t=P),
                                       ACT.Copy).then_inc(t_kept.sem, 1)

                for u in range(NU):
                    t, h = units[u]
                    n = len(key_tiles(t)) * P
                    st = stat[:, u % 4, :]
                    act.wait_ge(mx.sem, u + 1)
                    if u >= 2:
                        act.wait_ge(t_mm.sem, before(u - 1))
                    act.activation(p[:, u % 2, 0:n], ps[:, 2 * (u % 2):2 * (u % 2) + 2, :].rearrange("p b n -> p (b n)")[:, 0:n],
                                   ACT.Exp, bias=st[:, 0:1], scale=SCALE, accum_out=st[:, 1:2]).then_inc(exped.sem, 1)
                    act.activation(st[:, 2:3], W(env, "d_sink")[:, h:h + 1], ACT.Exp, bias=st[:, 0:1]).then_inc(sunk.sem, 1)
                    if u >= 1:
                        keep(u - 1)
                keep(NU - 1)

            @block.vector
            def _(dve):
                dve.tensor_copy(band[:, :, :], C(env, "band").rearrange("p (a b) -> p a b", a=2)).then_inc(masks.sem, 1)
                dve.tensor_copy(same[:, :], C(env, "ident")).then_inc(masks.sem, 1)
                def maximum(u):
                    t, h = units[u]
                    n = len(key_tiles(t)) * P
                    st = stat[:, u % 4, :]
                    dve.wait_ge(s_mm.sem, u + 1)
                    dv.link(dve, dve.tensor_reduce(st[:, 0:1], ps[:, 2 * (u % 2):2 * (u % 2) + 2, :]
                                                   .rearrange("p b n -> p (b n)")[:, 0:n], AX.X, ALU.max))
                    dv.link(dve, dve.tensor_scalar(st[:, 0:1], st[:, 0:1], SCALE, W(env, "d_sink")[:, h:h + 1], ALU.mult, ALU.max))
                    dve.tensor_scalar(st[:, 0:1], st[:, 0:1], -1.0, None, ALU.mult).then_inc(mx.sem, 1)

                def finish(u):
                    t, h = units[u]
                    st = stat[:, u % 4, :]
                    dve.wait_ge(exped.sem, u + 1)
                    dve.wait_ge(sunk.sem, u + 1)
                    dv.link(dve, dve.tensor_tensor(st[:, 3:4], st[:, 1:2], st[:, 2:3], ALU.add))
                    dv.link(dve, dve.reciprocal(st[:, 3:4], st[:, 3:4]))
                    dve.wait_ge(o_mm.sem, u + 1)
                    dve.tensor_scalar(yD[:, t, h, :], ps[:, 6 + u % 2, 0:DH], st[:, 3:4], None, ALU.mult)\
                       .then_inc(o_kept.sem, 1)

                for u in range(NU):
                    maximum(u)
                    if u >= 3:
                        finish(u - 3)
                for u in range(NU - 3, NU):
                    finish(u)
                dve.wait_ge(o_kept.sem, NU)

        turn_out(nc, env, yD, 6, "d", norm=False)


def stage_gates(nc, env):
    ps, signal, yT, hT = (env[n] for n in ("ps", "signal", "yT", "hT"))
    split_hi, split_lo, weights, dv, step_mm, mm, sg, made, done = (
        signal(f"g_{n}") for n in ("hi", "lo", "weights", "dve", "step", "product", "sigmoid", "made", "done"))
    GROUP = 256
    NA = GROUP // P * len(BLOCKS)
    BUFS = 3
    groups = [(S_BO, 0, 2)] + [(S_G0 + g // 2, g % 2 * GROUP, 2 * g) for g in range(D // GROUP)]
    steps = [(g, k) for g in range(len(groups)) for k in range(KT)]
    sums = [(g, c, b) for g in range(len(groups)) for c in range(GROUP // P) for b in BLOCKS]

    def ends_slab(g):
        return g + 1 == len(groups) or groups[g + 1][0] != groups[g][0]

    with ExitStack() as own, nc.Block() as block:
        x_hi, x_lo = (own.enter_context(nc.sbuf_tensor(f"g_x_{n}", [P, BUFS, T], F32R)) for n in ("hi", "lo"))
        w_hi, w_lo = (own.enter_context(nc.sbuf_tensor(f"g_w_{n}", [P, BUFS, GROUP], F32R)) for n in ("hi", "lo"))
        sig = own.enter_context(nc.sbuf_tensor("g_sig", [P, 2, BANK], F32))
        gate = own.enter_context(nc.sbuf_tensor("g_gate", [P, 2, BANK], F32))

        @block.sync
        def _(sp):
            load_slabs(sp, env, 15, 18)

        @block.tensor
        def _(pe):
            for i, (g, k) in enumerate(steps):
                at = i % BUFS
                pe.wait_ge(split_hi.sem, i + 1)
                pe.wait_ge(weights.sem, i + 1)
                pe.wait_ge(split_lo.sem, i + 1)
                for a in range(NA):
                    n = NA * g + a
                    c, b = sums[n][1:]
                    if k == 0 and n >= 8:
                        pe.wait_ge(made.sem, n - 7)
                    out = ps[:, n % 8, 0:b[1]]
                    cols, toks = slice(c * P, (c + 1) * P), slice(b[0], b[0] + b[1])
                    pe.matmul(out, w_hi[:, at, cols], x_hi[:, at, toks], start=k == 0, stop=False)
                    pe.matmul(out, w_hi[:, at, cols], x_lo[:, at, toks], start=False, stop=False)
                    last = pe.matmul(out, w_lo[:, at, cols], x_hi[:, at, toks], start=False, stop=k == KT - 1)
                    if k == KT - 1 and a < NA - 1:
                        last.then_inc(mm.sem, 1)
                last.then_inc(step_mm.sem, 1)

        @block.scalar
        def _(act):
            def sigmoid(n):
                g, c, b = sums[n]
                if n % NA < NA - 1:
                    act.wait_ge(mm.sem, (NA - 1) * g + n % NA + 1)
                else:
                    act.wait_ge(step_mm.sem, KT * (g + 1))
                if n >= 2:
                    act.wait_ge(made.sem, n - 1)
                act.activation(sig[:, n % 2, 0:b[1]], ps[:, n % 8, 0:b[1]], ACT.Sigmoid).then_inc(sg.sem, 1)

            for i, (g, k) in enumerate(steps):
                if i >= BUFS:
                    act.wait_ge(step_mm.sem, i - BUFS + 1)
                act.activation(x_hi[:, i % BUFS, :], hT[:, k, :], ACT.Copy).then_inc(split_hi.sem, 1)
                if g >= 1 and k in (1, 2):
                    for a in range((k - 1) * NA // 2, k * NA // 2):
                        sigmoid(NA * (g - 1) + a)
            for a in range(NA):
                sigmoid(NA * (len(groups) - 1) + a)

        @block.vector
        def _(dve):
            def make(n):
                g, c, b = sums[n]
                dve.wait_ge(sg.sem, n + 1)
                if n >= 2:
                    dve.wait_ge(done.sem, n - 1)
                if g == 0:
                    ins = dve.tensor_copy(gate[:, n % 2, 0:b[1]], sig[:, n % 2, 0:b[1]])
                else:
                    ins = dve.tensor_tensor(gate[:, n % 2, 0:b[1]], ps[:, n % 8, 0:b[1]], sig[:, n % 2, 0:b[1]], ALU.mult)
                ins.then_inc(made.sem, 1)

            for i, (g, k) in enumerate(steps):
                s, c0, _ = groups[g]
                at = i % BUFS
                if k == 0 and c0 == 0:
                    dve.wait_ge(env["loaded"][s].sem, 16)
                if i >= BUFS:
                    dve.wait_ge(step_mm.sem, i - BUFS + 1)
                split_weights(dve, slab(env, s)[:, k, c0:c0 + GROUP], w_hi[:, at, :], w_lo[:, at, :], dv)\
                    .then_inc(weights.sem, 1)
                if k == KT - 1 and ends_slab(g):
                    dve.wait_ge(weights.sem, i + 1)
                    dve.sem_inc(env["slab_used"].sem, 1)
                dve.wait_ge(split_hi.sem, i + 1)
                dve.tensor_tensor(x_lo[:, at, :], hT[:, k, :], x_hi[:, at, :].bitcast(F32), ALU.subtract).then_inc(split_lo.sem, 1)
                if g >= 1 and k in (1, 2):
                    for a in range((k - 1) * NA // 2, k * NA // 2):
                        make(NA * (g - 1) + a)
            for a in range(NA):
                make(NA * (len(groups) - 1) + a)

        @block.gpsimd
        def _(pool):
            for n, (g, c, b) in enumerate(sums):
                pool.wait_ge(made.sem, n + 1)
                y = yT[:, groups[g][2] + c, b[0]:b[0] + b[1]]
                pool.tensor_tensor(y, y, gate[:, n % 2, 0:b[1]], ALU.mult).then_inc(done.sem, 1)
                if g == 0:
                    pool.wait_ge(done.sem, n + 1)
            pool.wait_ge(done.sem, len(sums))


def stage_output(nc, env):
    ps, signal, yT, dram = (env[n] for n in ("ps", "signal", "yT", "dram"))
    NB = 4
    x_in = [signal(f"res{i}_loaded") for i in range(NB)]
    x_out = [signal(f"res{i}_stored") for i in range(NB)]
    split_hi, split_lo, weights, dv, step_mm, mm, gated, added = (
        signal(f"o_{n}") for n in ("hi", "lo", "weights", "dve", "step", "product", "gated", "added"))
    NA = NT // 2
    HT = NA * P
    BUFS = 3
    groups = [(n, half) for n in range(2) for half in range(2)]
    steps = [(g, k) for g in range(len(groups)) for k in range(KT)]
    jobs = [(n, half * NA + a) for n, half in groups for a in range(NA)]
    NJ = len(jobs)

    def rows(n, t):
        cols = slice(n * 512, (n + 1) * 512)
        return dram["ctx_now"][t * P:(t + 1) * P, cols] if t < NC else dram["out"][(t - NC) * P:(t - NC + 1) * P, cols]

    with ExitStack() as own, nc.Block() as block:
        y_hi, y_lo = (own.enter_context(nc.sbuf_tensor(f"o_y_{n}", [P, BUFS, HT], F32R)) for n in ("hi", "lo"))
        w_hi, w_lo = (own.enter_context(nc.sbuf_tensor(f"o_w_{n}", [P, BUFS, 512], F32R)) for n in ("hi", "lo"))
        res = own.enter_context(nc.sbuf_tensor("o_res", [P, NB, 512], F32))
        prod = own.enter_context(nc.sbuf_tensor("o_prod", [P, 2, 512], F32))

        @block.sync
        def _(sp):
            for i, (n, t) in enumerate(jobs):
                if i >= NB:
                    sp.wait_ge(x_out[i % NB].sem, 16 * (i // NB))
                sp.dma_start(res[:, i % NB, :], rows(n, t)).then_inc(x_in[i % NB].sem, 16)

        @block.tensor
        def _(pe):
            for i, (g, k) in enumerate(steps):
                at = i % BUFS
                pe.wait_ge(split_hi.sem, i + 1)
                pe.wait_ge(weights.sem, i + 1)
                pe.wait_ge(split_lo.sem, i + 1)
                for a in range(NA):
                    n = NA * g + a
                    if k == 0 and n >= 8:
                        pe.wait_ge(gated.sem, n - 7)
                    toks = slice(a * P, (a + 1) * P)
                    pe.matmul(ps[:, n % 8, :], y_hi[:, at, toks], w_hi[:, at, :], start=k == 0, stop=False)
                    pe.matmul(ps[:, n % 8, :], y_hi[:, at, toks], w_lo[:, at, :], start=False, stop=False)
                    last = pe.matmul(ps[:, n % 8, :], y_lo[:, at, toks], w_hi[:, at, :], start=False, stop=k == KT - 1)
                    if k == KT - 1 and a < NA - 1:
                        last.then_inc(mm.sem, 1)
                last.then_inc(step_mm.sem, 1)

        @block.vector
        def _(dve):
            def gated_sum(i):
                n, t = jobs[i]
                g, a = i // NA, i % NA
                if a < NA - 1:
                    dve.wait_ge(mm.sem, (NA - 1) * g + a + 1)
                else:
                    dve.wait_ge(step_mm.sem, KT * (g + 1))
                if i >= 2:
                    dve.wait_ge(added.sem, i - 1)
                v = 0 if t < NC else 1
                dve.tensor_tensor(prod[:, i % 2, :], ps[:, i % 8, :], env["gate_rows"][:, v, n * 512:(n + 1) * 512], ALU.mult)\
                   .then_inc(gated.sem, 1)

            for i, (g, k) in enumerate(steps):
                n, half = groups[g]
                at = i % BUFS
                if k == 0 and half == 0:
                    dve.wait_ge(env["loaded"][S_OUT + n].sem, 16)
                if i >= BUFS:
                    dve.wait_ge(step_mm.sem, i - BUFS + 1)
                split_weights(dve, slab(env, S_OUT + n)[:, k, :], w_hi[:, at, :], w_lo[:, at, :], dv).then_inc(weights.sem, 1)
                dve.wait_ge(split_hi.sem, i + 1)
                dve.tensor_tensor(y_lo[:, at, :], yT[:, k, half * HT:(half + 1) * HT], y_hi[:, at, :].bitcast(F32), ALU.subtract)\
                   .then_inc(split_lo.sem, 1)
                if g >= 1 and k in (1, 2):
                    for a in ((0, 1, 2), (3, 4))[k - 1]:
                        gated_sum(NA * (g - 1) + a)
            for a in range(NA):
                gated_sum(NA * (len(groups) - 1) + a)

        @block.gpsimd
        def _(pool):
            for i, (n, t) in enumerate(jobs):
                pool.wait_ge(gated.sem, i + 1)
                pool.wait_ge(x_in[i % NB].sem, 16 * (i // NB + 1))
                pool.tensor_tensor(res[:, i % NB, :], res[:, i % NB, :], prod[:, i % 2, :], ALU.add).then_inc(added.sem, 1)

        @block.scalar
        def _(act):
            def store(i):
                act.wait_ge(added.sem, i + 1)
                act.dma_start(rows(*jobs[i]), res[:, i % NB, :]).then_inc(x_out[i % NB].sem, 16)

            for i, (g, k) in enumerate(steps):
                half = groups[g][1]
                if i >= BUFS:
                    act.wait_ge(step_mm.sem, i - BUFS + 1)
                act.activation(y_hi[:, i % BUFS, :], yT[:, k, half * HT:(half + 1) * HT], ACT.Copy).then_inc(split_hi.sem, 1)
                if g >= 1 and k in (2, 3, 4, 5, 6):
                    store(NA * (g - 1) + k - 2)
            for a in range(NA):
                store(NA * (len(groups) - 1) + a)
            for b in range(NB):
                act.wait_ge(x_out[b].sem, 16 * (NJ // NB))


def constants():
    c = np.zeros((P, NCST), np.float32)

    def put(name, rows=P):
        a, b = CST[name]
        return c[0:rows, a:b]

    i, j = np.arange(P)[:, None], np.arange(P)[None, :]
    put("ident")[:] = i == j
    put("neg")[:, 0:P] = np.where(j >= i, 0.0, NEG)
    put("neg")[:, P:] = np.where(j <= i, 0.0, NEG)
    put("band")[:, 0:P] = np.where(j >= i, 0.0, NEG)
    put("band")[:, P:] = np.where(j <= i, 0.0, NEG)
    pos = np.arange(SEQ)
    for name, width in (("a", 32), ("d", 64)):
        nq = width // 4
        inv = np.float32(10000.0) ** (-np.arange(nq, dtype=np.float32) / np.float32(nq))
        r = (pos // GRID_W).astype(np.float32)[:, None] * inv
        q = (pos % GRID_W).astype(np.float32)[:, None] * inv
        cos = np.ones((T, width), np.float32)
        sin = np.zeros((T, width), np.float32)
        cos[CTX:] = np.concatenate([np.cos(r), np.cos(r), np.cos(q), np.cos(q)], 1)
        sin[CTX:] = np.concatenate([-np.sin(r), np.sin(r), -np.sin(q), np.sin(q)], 1)
        put(f"cos_{name}")[:] = cos.reshape(NT, P, width).transpose(1, 0, 2).reshape(P, -1)
        put(f"sin_{name}")[:] = sin.reshape(NT, P, width).transpose(1, 0, 2).reshape(P, -1)
    sel = put("sel_row").reshape(P, 8, P)
    pair = put("sel_pair").reshape(P, 4, P)
    for way in range(2):
        for h in range(HEADS):
            sel[32 * way + h, way * HEADS + h, :] = 1.0
            pair[32 * way + h, way * 2 + h // 2, 64 * (h % 2):64 * (h % 2) + 64] = 1.0
    put("sel_row")[:] = sel.reshape(P, -1)
    put("sel_pair")[:] = pair.reshape(P, -1)
    mod = put("sel_mod")
    mod[0, 0:P] = 1.0
    mod[1, P:] = 1.0
    put("ones")[:] = 1.0
    put("diag")[:] = (np.arange(P)[:, None] // 32) == (np.arange(GW)[None, :] // DH)
    pick = np.zeros((P, 2, 3, P), np.float32)
    for n, half in enumerate((16, 8)):
        same = (i // (2 * half)) == (j // (2 * half))
        pick[:, 0, n] = same & (i % (2 * half) < half) & (j % (2 * half) >= half)
        pick[:, 1, n] = same & (i % (2 * half) >= half) & (j % (2 * half) < half)
    pick[:, 0, 2] = ((i // 8) == (j // 8)) & (i <= j)
    pick[:, 1, 2] = ((i // 8) == (j // 8)) & (i >= j)
    put("pick")[:] = pick.reshape(P, -1)
    return c


def layout(w):
    return w.reshape(KT, P, w.shape[1]).transpose(1, 0, 2).reshape(P, -1)


def column(v):
    return v.reshape(-1, P).T


def pack(inputs):
    x = {k: np.asarray(v) for k, v in inputs.items()}
    w_all, par_all = [], []
    for l in range(DEPTH):
        wi = x["w_in"][l]
        gates = wi[:, B_G:B_G + 16].reshape(D, 4, HEADS)
        gap = np.zeros((D, 32 - HEADS), np.float32)
        li = np.concatenate([gates[:, 0], gap, gates[:, 2]], 1)
        lf = np.concatenate([gates[:, 1], gap, gates[:, 3]], 1)
        take = lambda a, n: wi[:, a:a + n]
        dq = take(D0, 256).reshape(D, 2, 2, DH).transpose(0, 2, 1, 3).reshape(D, 256)
        slabs = [x["w_mod"][l][:, i * 512:(i + 1) * 512] for i in range(6)]
        slabs += [np.concatenate([take(*B_V), li, lf], 1), take(*B_QK), take(*C_QK),
                  np.concatenate([take(*C_V), take(*C_LR)], 1), take(*A_QK), take(*A_V), np.concatenate([dq, take(D0 + 256, 256)], 1), take(*B_O),
                  take(G0, 512), take(G0 + 512, 512)]
        slabs += [x["w_out"][l][:, i * 512:(i + 1) * 512] for i in range(2)]
        w_all.append(np.concatenate([layout(s) for s in slabs], 1))
        p = np.zeros((P, NPAR), np.float32)

        def put(name):
            a, b = PAR[name]
            return p[:, a:b]

        put("norm_g")[:] = column(x["norm_g"][l])
        put("b_sh")[:] = column(x["b_mod"][l][0:D])
        put("b_sc")[:] = column(x["b_mod"][l][D:2 * D])
        put("b_gt")[:] = x["b_mod"][l][None, 2 * D:]
        put("a_gain")[:] = np.concatenate([np.tile(x["a_qn"][l], 8), np.tile(x["a_kn"][l], 8)])[None]
        put("d_gain")[:] = np.concatenate([np.tile(x["d_qn"][l], 4), np.tile(x["d_kn"][l], 2)])[None]
        put("conv_w")[:] = x["b_conv_w"][l].reshape(3, 4, P).transpose(2, 1, 0).reshape(P, 12)
        put("conv_b")[:] = column(x["b_conv_b"][l])
        for way in range(2):
            put("gate_li")[32 * way:32 * way + HEADS, 0] = x["b_gate_b"][l][2 * way]
            put("gate_lf")[32 * way:32 * way + HEADS, 0] = x["b_gate_b"][l][2 * way + 1]
        put("c_bg")[:] = x["c_bg"][l].T
        for z in range(2):
            put("c_wg")[z * RANK:(z + 1) * RANK, z * P:(z + 1) * P] = x["c_wg"][l][z]
        put("out_gain")[:] = 1.0
        for k, name in ((0, "a_subln"), (2, "b_outn"), (4, "c_outn")):
            put("out_gain")[:, k:k + 2] = np.tile(x[name][l], 2)[:, None]
        put("a_lam")[:] = x["a_lam"][l].reshape(1, -1)
        put("d_sink")[:] = x["d_sink"][l][None]
        lam_init = 0.8 - 0.6 * float(np.exp(-0.3 * l))
        put("lam_init")[:] = np.array([[lam_init, 1.0 - lam_init]], np.float32)
        par_all.append(p)
    return {
        "w": np.concatenate(w_all, 0), "par": np.concatenate(par_all, 0), "cst": constants(),
        "tok": np.concatenate([x["ctx"][0], x["x"][0]], 0),
        "c": np.stack([column(x["c_ctx"]), column(x["c"][0])], 2).reshape(P, 2 * KT),
    }


def kernel(**inputs):
    import concourse.bacc as bacc
    from concourse.bass_utils import run_bass_kernel_spmd

    nc = bacc.Bacc("TRN2", target_bir_lowering=False, num_devices=1)
    arrays = {f"in_{k}": np.ascontiguousarray(v) for k, v in pack(inputs).items()}
    dram = {k[3:]: nc.dram_tensor(k, v.shape, mybir.dt.from_np(v.dtype), kind="ExternalInput").ap()
            for k, v in arrays.items()}
    dram["ctx_now"] = nc.dram_tensor("ctx_now", (CTX, D), F32, kind="Internal").ap()
    dram["out"] = nc.dram_tensor("latents", (SEQ, D), F32, kind="ExternalOutput").ap()
    layer_program(nc, dram)
    r = run_bass_kernel_spmd(nc, [arrays], core_ids=[0])
    return r.results[0]["latents"].reshape(1, SEQ, D)
```
